# Optimizing a Trainium2 kernel written in Bass

```python
import math
import jax, jax.numpy as jnp
from jax import lax
import numpy as np

D_MODEL = 1024
BATCH = 1
SEQ = 256
DEPTH = 2
DEC_BATCH = 8
DEC_SEQ = 8
PAST_LEN = 1024
PAGE_SIZE = 128

N_EVEN = (DEPTH + 1) // 2
N_ODD = DEPTH // 2
HEAD_DIM = 64
BLK = 128
RMS_EPS = 1e-6
NEG = -1e30

A_Q_HEADS = D_MODEL // 128
A_KV_HEADS = A_Q_HEADS // 4
A_GQA = A_Q_HEADS // A_KV_HEADS
A_WINDOW = 128
A_Q_W = A_Q_HEADS * HEAD_DIM
A_KV_W = A_KV_HEADS * HEAD_DIM

B_WIDTH = D_MODEL // 2
B_GROUP_CH = 16
B_GROUPS = B_WIDTH // B_GROUP_CH
B_STATE = 64

C_WIDTH = D_MODEL // 2
C_BLOCKS = 8
C_BLOCK_W = C_WIDTH // C_BLOCKS
C_CONV = 4
C_POWER = 8.0

D_PAIRS = ((128, 1), (512, 4), (2048, 16))
D_N_GROUPS = 3
D_HEADS_PER = 4
D_QKV_W = D_N_GROUPS * D_HEADS_PER * HEAD_DIM
D_OUT_W = D_HEADS_PER * HEAD_DIM

T5_BUCKETS = 32
T5_MAX_DIST = 2048
T5_HEADS = A_Q_HEADS + D_N_GROUPS * D_HEADS_PER

MOE_GROUPS = 4
MOE_PER_GROUP = 4
MOE_EXPERTS = MOE_GROUPS * MOE_PER_GROUP
MOE_TOPK = 2
MOE_FF = 256

EVEN_IN = A_Q_W + 2 * A_KV_W + B_WIDTH
EVEN_OUT = A_Q_W + B_WIDTH
ODD_IN = 2 * C_WIDTH + 3 * D_QKV_W
ODD_OUT = C_WIDTH + D_OUT_W

kernel_name = 'hybrid_swa_s5_rglru_dilated_hmoe_step'

F32 = jnp.float32

def rmsnorm(x, g):
    xf = x.astype(F32)
    y = xf * lax.rsqrt(jnp.mean(xf * xf, axis=-1, keepdims=True) + RMS_EPS)
    return (y * g.astype(F32)).astype(x.dtype)

def t5_bucket(dist):
    n = jnp.maximum(dist, 0)
    max_exact = T5_BUCKETS // 2
    nf = jnp.maximum(n, 1).astype(F32)
    large = max_exact + (jnp.log(nf / max_exact) / math.log(T5_MAX_DIST / max_exact)
                         * (T5_BUCKETS - max_exact)).astype(jnp.int32)
    return jnp.where(n < max_exact, n, jnp.minimum(large, T5_BUCKETS - 1))

def rel_bias(table, dist):
    return jnp.moveaxis(jnp.take(table.astype(F32), t5_bucket(dist), axis=0), -1, 0)

def seq_blocks(x, blk):
    bt, length = x.shape[:2]
    nb = -(-length // blk)
    x = jnp.pad(x, [(0, 0), (0, nb * blk - length)] + [(0, 0)] * (x.ndim - 2))
    return x.reshape(bt, nb, blk, *x.shape[2:])

def band_keys(xb):
    prev = jnp.pad(xb, [(0, 0), (1, 0)] + [(0, 0)] * (xb.ndim - 2))[:, :-1]
    return jnp.concatenate([prev, xb], axis=2)

def band_geometry(nb, blk, max_dist):
    r = jnp.arange(blk)[:, None]
    s = jnp.arange(2 * blk)[None, :]
    dist = blk + r - s
    k_idx = (jnp.arange(nb)[:, None, None] - 1) * blk + s[None]
    valid = (dist >= 0) & (dist <= max_dist) & (k_idx >= 0)
    return dist, valid

def gqa_sink_attend(q, k, v, bias, valid, sinks):
    s = jnp.einsum('...qhgd,...khd->...hgqk', q, k).astype(F32) * HEAD_DIM ** -0.5 + bias
    s = jnp.where(valid[..., None, None, :, :], s, NEG)
    sink = sinks.astype(F32).reshape(A_KV_HEADS, A_GQA)[:, :, None]
    m = jnp.maximum(jnp.max(s, axis=-1), sink)
    p = jnp.exp(s - m[..., None])
    denom = jnp.sum(p, axis=-1) + jnp.exp(sink - m)
    o = jnp.einsum('...hgqk,...khd->...qhgd', p / denom[..., None], v.astype(F32))
    return o.astype(q.dtype)

def mha_lse_attend(q, k, v, bias, valid):
    s = jnp.einsum('...qhd,...khd->...hqk', q, k).astype(F32) * HEAD_DIM ** -0.5 + bias
    s = jnp.where(valid[..., None, :, :], s, NEG)
    m = jnp.max(s, axis=-1)
    p = jnp.exp(s - m[..., None])
    denom = jnp.sum(p, axis=-1)
    o = jnp.einsum('...hqk,...khd->...qhd', p / denom[..., None], v.astype(F32))
    return o, m + jnp.log(denom)

def linear_scan(a, b, h0):
    b = b.at[:, 0].add(a[:, 0] * h0)

    def combine(left, right):
        return right[0] * left[0], right[0] * left[1] + right[1]

    _, h = lax.associative_scan(combine, (a, b), axis=1)
    return h

def residue_split(x, d):
    bt, t = x.shape[:2]
    x = jnp.moveaxis(x.reshape(bt, t // d, d, *x.shape[2:]), 2, 1)
    return x.reshape(bt * d, t // d, *x.shape[3:])

def residue_merge(x, bt, d):
    length = x.shape[1]
    x = jnp.moveaxis(x.reshape(bt, d, length, *x.shape[2:]), 1, 2)
    return x.reshape(bt, length * d, *x.shape[3:])

def swa_prompt(q, k, v, sinks, table):
    bt, t = q.shape[:2]
    qb = seq_blocks(q.reshape(bt, t, A_KV_HEADS, A_GQA, HEAD_DIM), BLK)
    kb = band_keys(seq_blocks(k, BLK))
    vb = band_keys(seq_blocks(v, BLK))
    nb = qb.shape[1]
    dist, valid = band_geometry(nb, BLK, A_WINDOW - 1)
    bias = rel_bias(table[:, :A_Q_HEADS], dist).reshape(A_KV_HEADS, A_GQA, BLK, 2 * BLK)
    o = gqa_sink_attend(qb, kb, vb, bias, valid, sinks)
    o = o.reshape(bt, nb * BLK, A_Q_W)[:, :t]
    w = min(A_WINDOW, t)
    return o, jnp.stack([k[:, t - w:], v[:, t - w:]], axis=2)

def swa_sample(q, k, v, cache, sinks, table):
    bt, s_len = q.shape[:2]
    w = cache.shape[1]
    k_all = jnp.concatenate([cache[:, :, 0].astype(k.dtype), k], axis=1)
    v_all = jnp.concatenate([cache[:, :, 1].astype(v.dtype), v], axis=1)
    dist = w + jnp.arange(s_len)[:, None] - jnp.arange(w + s_len)[None, :]
    valid = (dist >= 0) & (dist < A_WINDOW)
    bias = rel_bias(table[:, :A_Q_HEADS], dist).reshape(A_KV_HEADS, A_GQA, s_len, w + s_len)
    o = gqa_sink_attend(q.reshape(bt, s_len, A_KV_HEADS, A_GQA, HEAD_DIM), k_all, v_all, bias, valid, sinks)
    new = jnp.concatenate([cache.astype(k.dtype), jnp.stack([k, v], axis=2)], axis=1)[:, -w:]
    return o.reshape(bt, s_len, A_Q_W), new

def s5_mixer(u, h0, p):
    bt, t, _ = u.shape
    uf = u.astype(F32).reshape(bt, t, B_GROUPS, B_GROUP_CH)
    lam = lax.complex(p['s5_a_re'].astype(F32), p['s5_a_im'].astype(F32))
    dt = jnp.exp(p['s5_log_dt'].astype(F32))[:, None]
    lam_bar = jnp.exp(lam * dt)
    b_mat = lax.complex(p['s5_b_re'].astype(F32), p['s5_b_im'].astype(F32))
    b_bar = ((lam_bar - 1.0) / lam)[..., None] * b_mat
    bu = jnp.einsum('gnc,btgc->btgn', b_bar, uf.astype(jnp.complex64))
    h = linear_scan(jnp.broadcast_to(lam_bar, bu.shape), bu, h0)
    c_mat = lax.complex(p['s5_c_re'].astype(F32), p['s5_c_im'].astype(F32))
    y = jnp.einsum('gcn,btgn->btgc', c_mat, h).real \
        + p['s5_d'].astype(F32).reshape(B_GROUPS, B_GROUP_CH) * uf
    y = jax.nn.gelu(y.reshape(bt, t, B_WIDTH))
    out = y * jax.nn.sigmoid(y @ p['s5_glu_w'].astype(F32) + p['s5_glu_b'].astype(F32))
    return out.astype(u.dtype), h[:, -1]

def rglru_mixer(xr, gate, conv_buf, h0, p):
    bt, t, _ = xr.shape
    xp = jnp.concatenate([conv_buf.astype(xr.dtype), xr], axis=1)
    w = p['conv_w']
    xc = xp[:, 0:t] * w[0]
    for tap in range(1, C_CONV):
        xc = xc + xp[:, tap:tap + t] * w[tap]
    xcf = (xc + p['conv_b']).astype(F32)
    xblk = xcf.reshape(bt, t, C_BLOCKS, C_BLOCK_W)
    r = jax.nn.sigmoid(jnp.einsum('btnj,njk->btnk', xblk, p['gate_a_w'].astype(F32)).reshape(bt, t, C_WIDTH)
                       + p['gate_a_b'].astype(F32))
    i = jax.nn.sigmoid(jnp.einsum('btnj,njk->btnk', xblk, p['gate_x_w'].astype(F32)).reshape(bt, t, C_WIDTH)
                       + p['gate_x_b'].astype(F32))
    log_a = -C_POWER * r * jax.nn.softplus(-p['lru_lambda'].astype(F32))
    a = jnp.exp(log_a)
    b = jnp.sqrt(-jnp.expm1(2.0 * log_a)) * (i * xcf)
    h = linear_scan(a, b, h0.astype(F32))
    y = h * jax.nn.gelu(gate.astype(F32))
    return y.astype(xr.dtype), h[:, -1], xp[:, t:]

def combine_dilations(outs, lses):
    o = jnp.stack(outs, axis=2)
    wts = jax.nn.softmax(jnp.stack(lses, axis=2), axis=2)
    y = jnp.sum(o * wts[..., None], axis=2)
    return y.reshape(y.shape[0], y.shape[1], D_OUT_W)

def dilated_prompt(q, k, v, table):
    bt, t = q.shape[:2]
    outs, lses, caches = [], [], []
    for g, (win, dil) in enumerate(D_PAIRS):
        max_d = win // dil
        blk = max(BLK, max_d)
        lo = A_Q_HEADS + g * D_HEADS_PER
        qs = residue_split(q[:, :, g], dil)
        ks = residue_split(k[:, :, g], dil)
        vs = residue_split(v[:, :, g], dil)
        length = qs.shape[1]
        qb = seq_blocks(qs, blk)
        kb = band_keys(seq_blocks(ks, blk))
        vb = band_keys(seq_blocks(vs, blk))
        nb = qb.shape[1]
        dist, valid = band_geometry(nb, blk, max_d)
        bias = rel_bias(table[:, lo:lo + D_HEADS_PER], dist * dil)
        o, lse = mha_lse_attend(qb, kb, vb, bias, valid)
        o = o.reshape(bt * dil, nb * blk, D_HEADS_PER, HEAD_DIM)[:, :length]
        lse = jnp.swapaxes(lse, -1, -2).reshape(bt * dil, nb * blk, D_HEADS_PER)[:, :length]
        outs.append(residue_merge(o, bt, dil))
        lses.append(residue_merge(lse, bt, dil))
        wc = min(win, t)
        caches.append(jnp.stack([k[:, t - wc:, g], v[:, t - wc:, g]], axis=2))
    return combine_dilations(outs, lses), caches

def dilated_sample(q, k, v, caches, table):
    s_len = q.shape[1]
    outs, lses, news = [], [], []
    for g, (win, dil) in enumerate(D_PAIRS):
        cache = caches[g].astype(k.dtype)
        wc = cache.shape[1]
        lo = A_Q_HEADS + g * D_HEADS_PER
        k_all = jnp.concatenate([cache[:, :, 0], k[:, :, g]], axis=1)
        v_all = jnp.concatenate([cache[:, :, 1], v[:, :, g]], axis=1)
        m = jnp.arange(win // dil + 1)
        idx = wc + jnp.arange(s_len)[:, None] - m[None, :] * dil
        valid = idx >= 0
        kg = jnp.take(k_all, jnp.maximum(idx, 0), axis=1)
        vg = jnp.take(v_all, jnp.maximum(idx, 0), axis=1)
        bias = rel_bias(table[:, lo:lo + D_HEADS_PER], m * dil)[:, None, :]
        o, lse = mha_lse_attend(q[:, :, g][:, :, None], kg, vg, bias, valid[:, None, :])
        outs.append(o[:, :, 0])
        lses.append(lse[..., 0])
        new_rows = jnp.stack([k[:, :, g], v[:, :, g]], axis=2)
        news.append(jnp.concatenate([cache, new_rows], axis=1)[:, -wc:])
    return combine_dilations(outs, lses), news

def even_mixer(h, kv_cache, s5_state, p, table):
    bt, t, _ = h.shape
    proj = h @ p['w_in']
    q, k, v, u = jnp.split(proj, [A_Q_W, A_Q_W + A_KV_W, A_Q_W + 2 * A_KV_W], axis=-1)
    q = q.reshape(bt, t, A_Q_HEADS, HEAD_DIM)
    k = k.reshape(bt, t, A_KV_HEADS, HEAD_DIM)
    v = v.reshape(bt, t, A_KV_HEADS, HEAD_DIM)
    if kv_cache is None:
        oa, new_kv = swa_prompt(q, k, v, p['sinks'], table)
        h0 = jnp.zeros((bt, B_GROUPS, B_STATE), jnp.complex64)
    else:
        oa, new_kv = swa_sample(q, k, v, kv_cache, p['sinks'], table)
        h0 = lax.complex(s5_state[..., 0].astype(F32), s5_state[..., 1].astype(F32))
    ob, h_last = s5_mixer(u, h0, p)
    out = jnp.concatenate([oa, ob.astype(oa.dtype)], axis=-1) @ p['w_out']
    return out, new_kv, jnp.stack([h_last.real, h_last.imag], axis=-1)

def odd_mixer(h, conv_buf, lru_h, d_caches, p, table):
    bt, t, _ = h.shape
    proj = h @ p['w_in']
    xr, gate, q, k, v = jnp.split(
        proj, [C_WIDTH, 2 * C_WIDTH, 2 * C_WIDTH + D_QKV_W, 2 * C_WIDTH + 2 * D_QKV_W], axis=-1)
    q = q.reshape(bt, t, D_N_GROUPS, D_HEADS_PER, HEAD_DIM)
    k = k.reshape(bt, t, D_N_GROUPS, D_HEADS_PER, HEAD_DIM)
    v = v.reshape(bt, t, D_N_GROUPS, D_HEADS_PER, HEAD_DIM)
    if d_caches is None:
        conv_buf = jnp.zeros((bt, C_CONV - 1, C_WIDTH), h.dtype)
        lru_h = jnp.zeros((bt, C_WIDTH), F32)
        od, new_d = dilated_prompt(q, k, v, table)
    else:
        od, new_d = dilated_sample(q, k, v, d_caches, table)
    oc, h_last, new_conv = rglru_mixer(xr, gate, conv_buf, lru_h, p)
    out = jnp.concatenate([oc, od.astype(oc.dtype)], axis=-1) @ p['w_out']
    return out, h_last, new_conv, new_d

def hier_moe(x, p):
    bt, t, dm = x.shape
    xf = x.reshape(bt * t, dm)
    n = xf.shape[0]
    g_logits = (xf @ p['router_g']).astype(F32) + p['router_g_b'].astype(F32)
    g_idx = jnp.argmax(g_logits, axis=-1)
    g_w = jnp.take_along_axis(jax.nn.softmax(g_logits, axis=-1), g_idx[:, None], axis=-1)
    e_logits = ((xf @ p['router_e']).astype(F32) + p['router_e_b'].astype(F32)).reshape(
        n, MOE_GROUPS, MOE_PER_GROUP)
    e_in = jnp.take_along_axis(e_logits, g_idx[:, None, None], axis=1)[:, 0]
    top_v, top_i = lax.top_k(e_in, MOE_TOPK)
    top_w = jax.nn.softmax(top_v, axis=-1) * g_w
    eid = g_idx[:, None] * MOE_PER_GROUP + top_i
    gates = jnp.sum(jax.nn.one_hot(eid, MOE_EXPERTS, dtype=F32) * top_w[..., None], axis=1)
    hid = jax.nn.silu(jnp.einsum('nd,edf->nef', xf, p['w_gate'])) * jnp.einsum('nd,edf->nef', xf, p['w_up'])
    y = jnp.einsum('nef,efd->nd', hid * gates[..., None].astype(hid.dtype), p['w_down'])
    return y.reshape(bt, t, dm)

def setup_inputs(seed: int = 0) -> dict:
    key = jax.random.key(seed)
    ks = iter(jax.random.split(key, 64))

    def nrm(shape, scale):
        return jax.random.normal(next(ks), shape, F32) * scale

    w_a = min(A_WINDOW, PAST_LEN)
    w_d = [min(w, PAST_LEN) for (w, _) in D_PAIRS]
    a0 = jax.random.uniform(next(ks), (N_ODD, C_WIDTH), F32, 0.9, 0.999)
    sig = a0 ** (1.0 / C_POWER)
    return {
        'x_prompt': nrm((BATCH, SEQ, D_MODEL), 1.0),
        'x_sample': nrm((DEC_BATCH, DEC_SEQ, D_MODEL), 1.0),
        'cache_a_kv': nrm((N_EVEN, DEC_BATCH, w_a, 2, A_KV_HEADS, HEAD_DIM), 1.0),
        'state_b': nrm((N_EVEN, DEC_BATCH, B_GROUPS, B_STATE, 2), 0.1),
        'state_c_h': nrm((N_ODD, DEC_BATCH, C_WIDTH), 0.5),
        'state_c_conv': nrm((N_ODD, DEC_BATCH, C_CONV - 1, C_WIDTH), 1.0),
        'cache_d_g0': nrm((N_ODD, DEC_BATCH, w_d[0], 2, D_HEADS_PER, HEAD_DIM), 1.0),
        'cache_d_g1': nrm((N_ODD, DEC_BATCH, w_d[1], 2, D_HEADS_PER, HEAD_DIM), 1.0),
        'cache_d_g2': nrm((N_ODD, DEC_BATCH, w_d[2], 2, D_HEADS_PER, HEAD_DIM), 1.0),
        'rel_table': nrm((T5_BUCKETS, T5_HEADS), 0.5),
        'norm_mix': 1.0 + nrm((DEPTH, D_MODEL), 0.05),
        'norm_ffn': 1.0 + nrm((DEPTH, D_MODEL), 0.05),
        'norm_final': 1.0 + nrm((D_MODEL,), 0.05),
        'w_in_even': nrm((N_EVEN, D_MODEL, EVEN_IN), D_MODEL ** -0.5),
        'w_out_even': nrm((N_EVEN, EVEN_OUT, D_MODEL), EVEN_OUT ** -0.5),
        'sinks_a': nrm((N_EVEN, A_Q_HEADS), 0.5),
        's5_a_re': -0.5 + nrm((N_EVEN, B_GROUPS, B_STATE), 0.01),
        's5_a_im': jnp.pi * jnp.arange(B_STATE, dtype=F32) + nrm((N_EVEN, B_GROUPS, B_STATE), 0.01),
        's5_log_dt': jax.random.uniform(next(ks), (N_EVEN, B_GROUPS), F32, math.log(1e-3), math.log(1e-1)),
        's5_b_re': nrm((N_EVEN, B_GROUPS, B_STATE, B_GROUP_CH), (2 * B_GROUP_CH) ** -0.5),
        's5_b_im': nrm((N_EVEN, B_GROUPS, B_STATE, B_GROUP_CH), (2 * B_GROUP_CH) ** -0.5),
        's5_c_re': nrm((N_EVEN, B_GROUPS, B_GROUP_CH, B_STATE), B_STATE ** -0.5),
        's5_c_im': nrm((N_EVEN, B_GROUPS, B_GROUP_CH, B_STATE), B_STATE ** -0.5),
        's5_d': nrm((N_EVEN, B_WIDTH), 1.0),
        's5_glu_w': nrm((N_EVEN, B_WIDTH, B_WIDTH), B_WIDTH ** -0.5),
        's5_glu_b': nrm((N_EVEN, B_WIDTH), 0.01),
        'w_in_odd': nrm((N_ODD, D_MODEL, ODD_IN), D_MODEL ** -0.5),
        'w_out_odd': nrm((N_ODD, ODD_OUT, D_MODEL), ODD_OUT ** -0.5),
        'conv_w': nrm((N_ODD, C_CONV, C_WIDTH), C_CONV ** -0.5),
        'conv_b': nrm((N_ODD, C_WIDTH), 0.01),
        'gate_a_w': nrm((N_ODD, C_BLOCKS, C_BLOCK_W, C_BLOCK_W), C_BLOCK_W ** -0.5),
        'gate_a_b': nrm((N_ODD, C_WIDTH), 0.01),
        'gate_x_w': nrm((N_ODD, C_BLOCKS, C_BLOCK_W, C_BLOCK_W), C_BLOCK_W ** -0.5),
        'gate_x_b': nrm((N_ODD, C_WIDTH), 0.01),
        'lru_lambda': jnp.log(sig) - jnp.log1p(-sig),
        'moe_router_g': nrm((DEPTH, D_MODEL, MOE_GROUPS), D_MODEL ** -0.5),
        'moe_router_g_b': nrm((DEPTH, MOE_GROUPS), 0.01),
        'moe_router_e': nrm((DEPTH, D_MODEL, MOE_EXPERTS), D_MODEL ** -0.5),
        'moe_router_e_b': nrm((DEPTH, MOE_EXPERTS), 0.01),
        'moe_w_gate': nrm((DEPTH, MOE_EXPERTS, D_MODEL, MOE_FF), D_MODEL ** -0.5),
        'moe_w_up': nrm((DEPTH, MOE_EXPERTS, D_MODEL, MOE_FF), D_MODEL ** -0.5),
        'moe_w_down': nrm((DEPTH, MOE_EXPERTS, MOE_FF, D_MODEL), MOE_FF ** -0.5),
    }

def reference(x_prompt, x_sample, cache_a_kv, state_b, state_c_h, state_c_conv,
              cache_d_g0, cache_d_g1, cache_d_g2,
              rel_table, norm_mix, norm_ffn, norm_final,
              w_in_even, w_out_even, sinks_a, s5_a_re, s5_a_im, s5_log_dt,
              s5_b_re, s5_b_im, s5_c_re, s5_c_im, s5_d, s5_glu_w, s5_glu_b,
              w_in_odd, w_out_odd, conv_w, conv_b, gate_a_w, gate_a_b, gate_x_w, gate_x_b, lru_lambda,
              moe_router_g, moe_router_g_b, moe_router_e, moe_router_e_b,
              moe_w_gate, moe_w_up, moe_w_down):
    yp, ys = x_prompt, x_sample
    a_p, a_s, b_p, b_s = [], [], [], []
    ch_p, ch_s, cc_p, cc_s = [], [], [], []
    d0_p, d0_s, d1_p, d1_s, d2_p, d2_s = [], [], [], [], [], []
    for layer in range(DEPTH):
        hp = rmsnorm(yp, norm_mix[layer])
        hs = rmsnorm(ys, norm_mix[layer])
        if layer % 2 == 0:
            e = layer // 2
            ep = {'w_in': w_in_even[e], 'w_out': w_out_even[e], 'sinks': sinks_a[e],
                  's5_a_re': s5_a_re[e], 's5_a_im': s5_a_im[e], 's5_log_dt': s5_log_dt[e],
                  's5_b_re': s5_b_re[e], 's5_b_im': s5_b_im[e], 's5_c_re': s5_c_re[e], 's5_c_im': s5_c_im[e],
                  's5_d': s5_d[e], 's5_glu_w': s5_glu_w[e], 's5_glu_b': s5_glu_b[e]}
            op, kv_np, sb_np = even_mixer(hp, None, None, ep, rel_table)
            os_, kv_ns, sb_ns = even_mixer(hs, cache_a_kv[e], state_b[e], ep, rel_table)
            a_p.append(kv_np)
            a_s.append(kv_ns)
            b_p.append(sb_np)
            b_s.append(sb_ns)
        else:
            o = layer // 2
            od = {'w_in': w_in_odd[o], 'w_out': w_out_odd[o], 'conv_w': conv_w[o], 'conv_b': conv_b[o],
                  'gate_a_w': gate_a_w[o], 'gate_a_b': gate_a_b[o], 'gate_x_w': gate_x_w[o],
                  'gate_x_b': gate_x_b[o], 'lru_lambda': lru_lambda[o]}
            op, h_np, conv_np, d_np = odd_mixer(hp, None, None, None, od, rel_table)
            os_, h_ns, conv_ns, d_ns = odd_mixer(hs, state_c_conv[o], state_c_h[o],
                                                 (cache_d_g0[o], cache_d_g1[o], cache_d_g2[o]), od, rel_table)
            ch_p.append(h_np)
            ch_s.append(h_ns)
            cc_p.append(conv_np)
            cc_s.append(conv_ns)
            d0_p.append(d_np[0])
            d0_s.append(d_ns[0])
            d1_p.append(d_np[1])
            d1_s.append(d_ns[1])
            d2_p.append(d_np[2])
            d2_s.append(d_ns[2])
        yp = yp + op.astype(yp.dtype)
        ys = ys + os_.astype(ys.dtype)
        mp = {'router_g': moe_router_g[layer], 'router_g_b': moe_router_g_b[layer],
              'router_e': moe_router_e[layer], 'router_e_b': moe_router_e_b[layer],
              'w_gate': moe_w_gate[layer], 'w_up': moe_w_up[layer], 'w_down': moe_w_down[layer]}
        yp = yp + hier_moe(rmsnorm(yp, norm_ffn[layer]), mp).astype(yp.dtype)
        ys = ys + hier_moe(rmsnorm(ys, norm_ffn[layer]), mp).astype(ys.dtype)
    y_prompt = rmsnorm(yp, norm_final)
    y_sample = rmsnorm(ys, norm_final)
    return (y_prompt, y_sample,
            jnp.stack(a_p), jnp.stack(a_s), jnp.stack(b_p), jnp.stack(b_s),
            jnp.stack(ch_p), jnp.stack(ch_s), jnp.stack(cc_p), jnp.stack(cc_s),
            jnp.stack(d0_p), jnp.stack(d0_s), jnp.stack(d1_p), jnp.stack(d1_s),
            jnp.stack(d2_p), jnp.stack(d2_s))


_drawn_inputs = setup_inputs


def setup_inputs(seed=0):
    import zlib

    import numpy as np

    out = dict(_drawn_inputs(seed))
    spreads = {}
    factors = {'sinks_a': 4.006,
     's5_a_re': 17.418,
     's5_glu_b': 8.0,
     'gate_a_b': 26.058,
     'gate_x_b': 8.0,
     'moe_router_e_b': 3.965}
    for name, (base, spread) in spreads.items():
        noise = np.random.default_rng([zlib.crc32(name.encode()), seed]).standard_normal(out[name].shape)
        drawn = base * np.exp(spread * noise) if base else spread * noise
        out[name] = __import__('jax').numpy.asarray(drawn.astype(out[name].dtype))
    for name, factor in factors.items():
        out[name] = (out[name] * factor).astype(out[name].dtype)
    return out
```

```python
import math
from contextlib import ExitStack

import numpy as np

import concourse.bass as bass
from concourse import mybir

F32 = mybir.dt.float32
I32 = mybir.dt.int32
U32 = mybir.dt.uint32
ALU = mybir.AluOpType
ACT = mybir.ActivationFunctionType
AX = mybir.AxisListType

P = 128
D = 1024
KC = D // P
SEQ, NB, NS = 256, 8, 8
TOK = SEQ + NB * NS
ROWS = (P, P, NB * NS)
HD = 64
BIG = -1e30
EPS = 1e-6
SCALE = HD ** -0.5

G, GC, NST, CH = 32, 16, 64, 8
NCH = TOK // CH
PCH = SEQ // CH
PAIRS = G // 2

DTOP = 1024 + NS - 1
BROW = DTOP + P + 1
NBUCK = 32
A_H, D_H = 8, 4
WIN = ((128, 1), (512, 4), (2048, 16))
KEYS = (128, 512, 512)
CACHE = (128, 512, 1024)

E_N, FF, CAP = 16, 256, 80
SLOT = 6144
RING = 3


def bucket(dist):
    n = max(dist, 0)
    exact = NBUCK // 2
    if n < exact:
        return n
    v = np.log(np.float32(n) / np.float32(exact)).astype(np.float32) / np.float32(math.log(2048 / exact)) * np.float32(exact)
    return min(exact + int(np.float32(v)), NBUCK - 1)


def bucket_onehots():
    oh = np.zeros((NBUCK + 1, 4, BROW), np.float32)
    kinds = ((A_WINDOW_MAX, 1),) + tuple((w, d) for w, d in WIN)
    for k, (far, dil) in enumerate(kinds):
        for x in range(BROW):
            dist = DTOP - x
            ok = 0 <= dist <= far and dist % dil == 0
            oh[bucket(dist) if ok else NBUCK, k, x] = 1.0
    return oh


def flip_matrices():
    f = np.zeros((P, 6, P), np.float32)
    f[np.arange(P), 0, P - 1 - np.arange(P)] = 1.0
    for b in range(4):
        for h in range(4):
            for s in range(NS):
                f[8 * h + NS - 1 - s, 1, 32 * b + 8 * h + s] = 1.0
                f[8 * h + NS - 1 - s, 2 + b, 32 * b + 8 * h + s] = 1.0
        f[32, 2 + b, :] = 1.0
        f[32, 2 + b, 32 * b:32 * b + 32] = 0.0
    return f.reshape(P, 6 * P)


A_WINDOW_MAX = 127


class Carve:

    def __init__(self, tensor, size, at=0):
        self.tensor, self.size, self.at = tensor, size, at

    def take(self, *shape):
        n = int(np.prod(shape))
        assert self.at + n <= self.size, (self.at, n, self.size)
        ap = self.tensor[:, self.at:self.at + n]
        self.at += n
        names = "abcdef"[:len(shape)]
        if len(shape) > 1:
            ap = ap.rearrange("p (" + " ".join(names) + ") -> p " + " ".join(names),
                              **{c: s for c, s in zip(names[1:], shape[1:])})
        return ap


class Link:

    def __init__(self, eng, sem):
        self.eng, self.sem, self.n = eng, sem, 0

    def __call__(self, ins):
        self.n += 1
        ins.then_inc(self.sem, 1)
        self.eng.wait_ge(self.sem, self.n)


class Core:

    def __init__(self, nc, ctx):
        self.nc, self.ctx = nc, ctx
        sb = lambda name, shape, dt=F32: ctx.enter_context(nc.sbuf_tensor(name, shape, dt))
        self.ring = sb("ring", [P, RING * SLOT])
        self.resid = sb("resid", [P, 3, D])
        self.xnT = sb("xnT", [P, KC, TOK])
        self.ident = sb("ident", [P, P])
        self.cols = sb("cols", [P, 40])
        self.gains = sb("gains", [P, 4, KC])
        self.stat = sb("stat", [P, 16])
        self.AR = 28900
        self.arena = sb("arena", [P, self.AR])
        self.bank = [ctx.enter_context(nc.psum_tensor(f"bank{i}", [P, 512], F32)) for i in range(8)]
        self.ring_in = [nc.alloc_semaphore(f"ring_in{i}") for i in range(RING)]

        self.xg_in = [nc.alloc_semaphore(f"xg_in{i}") for i in range(3)]
        self.y_out = [nc.alloc_semaphore(f"y_out{i}") for i in range(3)]
        self.items, self.need, self.temp, self.cleared = None, None, [], []

    def set_items(self, items):
        self.items, self.need = items, []
        landed = [0] * RING
        for i, parts in enumerate(items):
            landed[i % RING] += len(parts)
            self.need.append(landed[i % RING])

    def load_item(self, sp, i):
        if i < len(self.items):
            slot = self.slot(i)
            for view, src in self.items[i]:
                sp.dma_start(view(slot), src).then_inc(self.ring_in[i % RING], 16)

    def sem(self, name):
        self.temp.append(self.nc.alloc_semaphore(name))
        return self.temp[-1]

    def keep_sem(self, name):
        return self.nc.alloc_semaphore(name)

    def recycle(self):
        for sem in self.cleared:
            self.nc.release_semaphore(sem)
        nums = sorted(sem.num for sem in self.temp)
        while nums:
            n = 1
            while n < len(nums) and nums[n] == nums[0] + n:
                n += 1
            self.nc.gpsimd.sem_clear(range(nums[0], nums[0] + n))
            nums = nums[n:]
        self.cleared, self.temp = self.temp, []

    def slot(self, i, n=SLOT):
        s = (i % RING) * SLOT
        return self.ring[:, s:s + n]

    def arrived(self, eng, i):
        eng.wait_ge(self.ring_in[i % RING], 16 * self.need[i])


def ring_items(w_in_even, glu, w_out_even, w_gate, w_up, w_down, w_in_odd, w_out_odd):
    items = []

    def kmajor(w, c0, n, k0=0, k1=KC, by_p=True):
        src = w.rearrange("(p k) n -> p k n" if by_p else "(k p) n -> p k n", p=P)[:, k0:k1, c0:c0 + n]
        return lambda s: s[:, 0:(k1 - k0) * n].rearrange("p (k n) -> p k n", n=n), src

    def qkv_parts():
        src = w_in_even.rearrange("(p k) n -> p k n", p=P)
        parts = []
        for kv in range(2):
            for i in range(4):
                parts.append((lambda s, kv=kv, i=i: s[:, 0:KC * 768].rearrange("p (k n) -> p k n", n=768)
                              [:, :, i * 128 + kv * 64:i * 128 + kv * 64 + 64],
                              src[:, :, kv * 256 + i * 64:kv * 256 + i * 64 + 64]))
        parts.append((lambda s: s[:, 0:KC * 768].rearrange("p (k n) -> p k n", n=768)[:, :, 512:768],
                      src[:, :, 512:768]))
        return parts

    def experts(layer, e):
        gu = lambda s: s[:, 0:KC * 2 * FF].rearrange("p (k n) -> p k n", n=2 * FF)
        return [(lambda s: gu(s)[:, :, 0:FF], w_gate[layer, e].rearrange("(p k) f -> p k f", k=KC)),
                (lambda s: gu(s)[:, :, FF:2 * FF], w_up[layer, e].rearrange("(p k) f -> p k f", k=KC)),
                (lambda s: s[:, KC * 2 * FF:SLOT].rearrange("p (k n) -> p k n", n=D),
                 w_down[layer, e].rearrange("(k p) n -> p k n", k=2))]

    items.append(qkv_parts())
    items.append([kmajor(w_in_even, 768, 512)])
    items.append([kmajor(glu, 0, 512, 0, 4, False)])
    items.append([kmajor(w_out_even, 0, D, 0, 4, False)])
    items.append([kmajor(w_out_even, 0, D, 4, 8, False)])
    items += [experts(0, e) for e in range(E_N)]
    for c0, n in ((0, 512), (512, 512), (1024, 768), (1792, 768), (2560, 768)):
        items.append([kmajor(w_in_odd, c0, n)])
    items.append([kmajor(w_out_odd, 0, D, 0, 6, False)])
    items += [experts(1, e) for e in range(E_N)]
    return items


IT_QKV, IT_U, IT_GLU, IT_OUT_E, IT_MOE0 = 0, 1, 2, 3, 5
IT_XR, IT_GATE, IT_Q, IT_K, IT_V, IT_OUT_O, IT_MOE1 = (IT_MOE0 + E_N + i for i in range(7))
N_ITEMS = IT_MOE1 + E_N

COL_D, COL_GLU_B, COL_CONV_W, COL_CONV_B, COL_GA_B, COL_GX_B, COL_LAM = 0, 4, 8, 24, 28, 32, 36


def constants_block(c, x):
    nc = c.nc
    ev = even_arena(c)
    win, cp, wuu, state0 = ev["win"], ev["cp"], ev["wuu"], ev["state0"]
    ar = Carve(c.arena, ev["after_s5"])
    rows16 = ar.take(4, P)[0:PAIRS]
    logdt = ar.take(2)[0:PAIRS]
    lam = ar.take(10, P)[0:PAIRS]
    coef = ar.take(4, P)[0:PAIRS]
    prm = ar.take(4, PAIRS)
    pw = ar.take(2, PAIRS, CH + 1)
    pwr = ar.take(2, PAIRS, CH)
    ptmp = ar.take(2, PAIRS, 4)
    btmp = ar.take(PAIRS, GC)
    vrows = ar.take(P)[0:40]
    sraw = ar.take(2 * P)
    table = ar.take(20)[0:NBUCK + 1]
    flat = c.xnT[:, :, :].rearrange("p k t -> p (k t)")
    onehot = [ar.take(BROW)[0:NBUCK + 1], flat[0:NBUCK + 1, 0:BROW], flat[0:NBUCK + 1, BROW:2 * BROW]]
    brow = ar.take(BROW)
    ar = Carve(c.arena, c.AR, ev["end"])
    big = ar.take(PAIRS * (CH + 1) * GC)
    braw = ar.take(2, PAIRS, GC)
    bbar = ar.take(2, PAIRS, GC)
    ct = ar.take(2, PAIRS, GC)
    tau = c.xnT[:, :, :].rearrange("p k t -> p (k t)")[:, 0:G * P // 2]
    craw = win.rearrange("p j r m -> p (j r m)")[:, 0:8 * P].rearrange("p (r i t n) -> p r i t n", r=2, i=4, t=2)
    wt = ev["u40"].rearrange("p (r j s c) -> p r j s c", r=2, j=PAIRS, s=CH)

    ld_x, ld_par = c.sem("b0_x"), c.sem("b0_params")
    ld_oh = [c.sem(f"b0_onehot{k}") for k in range(3)]
    ld_b, ld_c, ld_v, ld_tab = c.sem("b0_b"), c.sem("b0_c"), c.sem("b0_vec"), c.sem("b0_table")
    ident_ok, neg_ok, zero_ok = c.sem("b0_ident"), c.sem("b0_neg_row"), c.sem("b0_zero")
    pe_cols, cols_ok = c.sem("b0_pe_cols"), c.sem("b0_cols")
    pe_bias, bias_sb, bias_out = c.sem("b0_pe_bias"), c.sem("b0_bias_sb"), c.sem("b0_bias_out")
    act_ok, dve_arg = c.sem("b0_act"), c.sem("b0_dve_arg")
    dve_own = c.sem("b0_dve_own")
    coef_ok, pe_prm = c.sem("b0_coef"), c.sem("b0_pe_prm")
    pe_ct, ct_ok = c.sem("b0_pe_ct"), c.sem("b0_ct")
    wt_ok, pe_win, win_ok = c.sem("b0_wt"), c.sem("b0_pe_win"), c.sem("b0_win")
    cp_ok, pe_tau, tau_ok, tau_out = c.sem("b0_cp"), c.sem("b0_pe_tau"), c.sem("b0_tau"), c.sem("b0_tau_out")
    zeroed = c.keep_sem("b0_zeroed")
    tau_part, wuu_zero = c.sem("b0_tau_part"), c.sem("b0_wuu_zero")
    pe_st, st_ok = c.sem("b0_pe_state"), c.sem("b0_state")

    with nc.Block() as block:
        @block.sync
        def _(sp):
            sp.dma_start(rows16[:, 0, :], x["s5_a_re"][0].rearrange("(j g) n -> j (g n)", g=2)).then_inc(ld_par, 16)
            sp.dma_start(rows16[:, 1, :], x["s5_a_im"][0].rearrange("(j g) n -> j (g n)", g=2)).then_inc(ld_par, 16)
            sp.dma_start(logdt, x["s5_log_dt"][0].rearrange("(j g) -> j g", g=2)).then_inc(ld_par, 16)
            for r, name in enumerate(("s5_b_re", "s5_b_im")):
                sp.dma_start(braw[:, r], x[name][0].rearrange("(j g) n c -> (g n) j c", g=2)).then_inc(ld_b, 16)
            for r, name in enumerate(("s5_c_re", "s5_c_im")):
                for twice in range(2):
                    sp.dma_start(craw[:, r, :, twice, :],
                                 x[name][0].rearrange("(i g) c n -> (g c) i n", g=8)).then_inc(ld_c, 16)
            for t, src in enumerate((x["x_prompt"][0, 0:P, :], x["x_prompt"][0, P:SEQ, :],
                                     x["x_sample"].rearrange("b s d -> (b s) d"))):
                sp.dma_start(c.resid[0:ROWS[t], t, :], src).then_inc(ld_x, 16)
            for i in (IT_U, IT_QKV, IT_GLU):
                c.load_item(sp, i)
            for half in range(2):
                sp.wait_ge(tau_ok, half + 1)
                for s in range(CH):
                    if s == 0 and half == 0:
                        sp.wait_ge(wuu_zero, 1)
                    gs = slice(half * G // 2, (half + 1) * G // 2)
                    sp.dma_start(wuu[s * GC:(s + 1) * GC, gs, s * GC:P],
                                 tau[0:GC, :].rearrange("p (g m) -> p g m", g=G // 2)[:, :, 0:P - s * GC])\
                        .then_inc(tau_out, 16)
            sp.wait_ge(tau_out, 2 * 16 * CH)
            sp.wait_ge(bias_out, 4 * 16)
            sp.wait_ge(ld_x, 48)

        @block.gpsimd
        def _(pool):
            nc.gpsimd.memset(c.stat[:, :], 1.0)
            nc.gpsimd.memset(c.ident[:, :], 0.0).then_inc(zero_ok, 1)
            zeros = c.arena[:, c.AR - D:c.AR]
            nc.gpsimd.memset(zeros, 0.0).then_inc(zero_ok, 1)
            pool.wait_ge(zero_ok, 2)
            nc.gpsimd.affine_select(out=c.ident[:, :], in_=c.ident[:, :], compare_op=ALU.not_equal, fill=1.0,
                                    base=0, pattern=[[-1, P]], channel_multiplier=1).then_inc(ident_ok, 1)
            for n in range(PAIR_ROWS // P):
                pool.dma_start(x["y_rows"][n * P:(n + 1) * P, :], zeros).then_inc(zeroed, 16)
            pool.wait_ge(zeroed, 16 * (PAIR_ROWS // P))

        @block.scalar
        def _(act):
            act.dma_start(table[0:NBUCK, :], x["rel_table"]).then_inc(ld_tab, 16)
            for k in range(3):
                act.dma_start(onehot[k], x["onehot"][:, k, :]).then_inc(ld_oh[k], 16)
            act.dma_start(vrows[COL_D:COL_D + 4], x["s5_d"][0].rearrange("(k p) -> k p", p=P)).then_inc(ld_v, 16)
            act.dma_start(vrows[COL_GLU_B:COL_GLU_B + 4], x["s5_glu_b"][0].rearrange("(k p) -> k p", p=P)).then_inc(ld_v, 16)
            act.dma_start(vrows[COL_CONV_W:COL_CONV_W + 16], x["conv_w"][0].rearrange("t (k p) -> (t k) p", p=P)).then_inc(ld_v, 16)
            for at, name in ((COL_CONV_B, "conv_b"), (COL_GA_B, "gate_a_b"), (COL_GX_B, "gate_x_b"), (COL_LAM, "lru_lambda")):
                act.dma_start(vrows[at:at + 4], x[name][0].rearrange("(k p) -> k p", p=P)).then_inc(ld_v, 16)
            for l in range(2):
                act.dma_start(c.gains[:, l, :], x["norm_mix"][l].rearrange("(p k) -> p k", k=KC)).then_inc(ld_v, 16)
                act.dma_start(c.gains[:, 2 + l, :], x["norm_ffn"][l].rearrange("(p k) -> p k", k=KC)).then_inc(ld_v, 16)
            act.dma_start(sraw, x["state_b"][0].rearrange("b (j g) n r -> b j (g n r)", g=2)
                          .rearrange("b j m -> (b j) m")).then_inc(ld_tab, 16)
            act.wait_ge(ld_par, 48)
            nc.scalar.activation(logdt, logdt, ACT.Exp).then_inc(act_ok, 1)
            act.wait_ge(dve_arg, 1)
            nc.scalar.activation(lam[:, 0], rows16[:, 2], ACT.Exp).then_inc(act_ok, 1)
            act.wait_ge(dve_arg, 2)
            nc.scalar.activation(lam[:, 1], lam[:, 3], ACT.Sin).then_inc(act_ok, 1)
            nc.scalar.activation(lam[:, 2], lam[:, 4], ACT.Sin).then_inc(act_ok, 1)
            act.wait_ge(pe_cols, 1)
            nc.scalar.copy(c.cols[:, :], c.bank[0][:, 0:40]).then_inc(cols_ok, 1)
            n = 0
            for k in range(4):
                heads = A_H if k == 0 else D_H
                rows = slice(32 * k, 32 * k + heads)
                for j, (a, b) in enumerate(((0, 512), (512, 1024), (1024, BROW))):
                    act.wait_ge(pe_bias, n + 1)
                    nc.scalar.copy(brow[rows, a:b], c.bank[1 + j][0:heads, 0:b - a]).then_inc(bias_sb, 1)
                    n += 1
                if k == 0:
                    act.dma_start(onehot[0], x["onehot"][:, 3, :]).then_inc(ld_oh[0], 16)
                act.wait_ge(bias_sb, n)
                h0 = 0 if k == 0 else A_H + (k - 1) * D_H
                act.dma_start(x["bias_rows"][h0:h0 + heads, :], brow[rows]).then_inc(bias_out, 16)
            for b in range(8):
                act.wait_ge(pe_win, b + 1)
                nc.scalar.copy(win[:, 2 * b:2 * b + 2, :, :].rearrange("p j r m -> p (j r m)"),
                               c.bank[4 + b % 4][:, :]).then_inc(win_ok, 1)
            for half in range(2):
                if half:
                    act.wait_ge(tau_out, 16 * CH)
                for b in range(4):
                    act.wait_ge(pe_tau, half * 4 + b + 1)
                    q0, par = b // 2 * 4, b % 2
                    nc.scalar.copy(tau[0:GC, :].rearrange("p (q two m) -> p q two m", two=2, m=P)[:, q0:q0 + 4, par, :],
                                   c.bank[b][0:GC, :].rearrange("p (q m) -> p q m", q=4)).then_inc(
                                       tau_ok if b == 3 else tau_part, 1)

        @block.tensor
        def _(pe):
            pe.wait_ge(ident_ok, 1)
            pe.wait_ge(ld_v, 16 * 11)
            nc.tensor.transpose(c.bank[0][:, 0:40], vrows, c.ident[0:40, 0:40]).then_inc(pe_cols, 1)
            def bias(k):
                heads = A_H if k == 0 else D_H
                h0 = 0 if k == 0 else A_H + (k - 1) * D_H
                pe.wait_ge(ld_oh[k % 3], 16 * (k // 3 + 1))
                if k:
                    pe.wait_ge(bias_sb, 3 * k)
                for j, (a, b) in enumerate(((0, 512), (512, 1024), (1024, BROW))):
                    nc.tensor.matmul(c.bank[1 + j][0:heads, 0:b - a], table[:, h0:h0 + heads], onehot[k % 3][:, a:b],
                                     start=True, stop=True).then_inc(pe_bias, 1)

            pe.wait_ge(neg_ok, 1)
            pe.wait_ge(ld_tab, 32)
            bias(0)
            pe.wait_ge(cols_ok, 1)
            sr = sraw.rearrange("p (m r) -> p m r", r=2)
            nc.tensor.transpose(c.bank[0][:, 0:P], sr[:, :, 0], c.ident[:, :])
            nc.tensor.transpose(c.bank[0][:, P:2 * P], sr[:, :, 1], c.ident[:, :]).then_inc(pe_st, 1)
            pe.wait_ge(coef_ok, 1)
            for q in range(4):
                last = nc.tensor.transpose(c.bank[4][:, q * PAIRS:(q + 1) * PAIRS], coef[:, q, :], c.ident[0:PAIRS, 0:PAIRS])
            last.then_inc(pe_prm, 1)
            pe.wait_ge(ld_c, 64)
            for r in range(2):
                for i in range(4):
                    last = nc.tensor.transpose(c.bank[5 + r][:, i * P:(i + 1) * P],
                                               craw[:, r, i].rearrange("p t n -> p (t n)"), c.ident[:, :])
            last.then_inc(pe_ct, 1)
            for k in range(1, 4):
                bias(k)
            pe.wait_ge(wt_ok, 1)
            pe.wait_ge(ct_ok, 1)
            for b in range(8):
                if b >= 4:
                    pe.wait_ge(win_ok, b - 3)
                for j in range(2 * b, 2 * b + 2):
                    for r in range(2):
                        q = (j - 2 * b) * 2 + r
                        last = nc.tensor.transpose(c.bank[4 + b % 4][:, q * P:(q + 1) * P],
                                                   wt[:, r, j].rearrange("p s c -> p (s c)"), c.ident[:, :])
                last.then_inc(pe_win, 1)
            pe.wait_ge(cp_ok, 1)
            pe.wait_ge(st_ok, 1)
            for half in range(2):
                for b in range(4):
                    if half:
                        pe.wait_ge(tau_ok, 1)
                    q0, par = b // 2 * 4, b % 2
                    rows = slice(64 * par, 64 * par + 64)
                    for q in range(4):
                        j = half * 8 + q0 + q
                        out = c.bank[b][0:GC, q * P:(q + 1) * P]
                        nc.tensor.matmul(out, bbar[rows, 0, j, :], cp[rows, 0, j, 0:P], start=True, stop=False)
                        last = nc.tensor.matmul(out, bbar[rows, 1, j, :], cp[rows, 1, j, 0:P], start=False, stop=True)
                    last.then_inc(pe_tau, 1)

        @block.vector
        def _(dve):
            v = nc.vector
            link = Link(dve, dve_own)
            v.memset(table[NBUCK:NBUCK + 1, :], BIG).then_inc(neg_ok, 1)
            v.memset(wuu, 0.0).then_inc(wuu_zero, 1)
            dve.wait_ge(act_ok, 1)
            dtb = logdt.unsqueeze(2).broadcast_to([PAIRS, 2, NST])
            split = lambda ap: ap.rearrange("p (g n) -> p g n", g=2)
            v.tensor_tensor(split(rows16[:, 2]), split(rows16[:, 0]), dtb, ALU.mult).then_inc(dve_arg, 1)
            link(v.tensor_tensor(split(rows16[:, 3]), split(rows16[:, 1]), dtb, ALU.mult))
            th, turns, a, b = rows16[:, 3], lam[:, 5], lam[:, 3], lam[:, 4]
            magic = float(1.5 * 2 ** 23)
            link(v.tensor_scalar(turns, th, float(1 / (2 * math.pi)), magic, ALU.mult, ALU.add))
            link(v.tensor_scalar(turns, turns, -magic, None, ALU.add))
            c1 = 6.28125
            c2 = 0.0019350051879882812
            c3 = 2 * math.pi - c1 - c2
            for part in (c1, c2, c3):
                link(v.scalar_tensor_tensor(th, turns, -part, th, ALU.mult, ALU.add))
            link(v.tensor_scalar(a, th, 3.1415925, -3.1415925, ALU.min, ALU.max))
            link(v.tensor_scalar(b, a, -1.0, None, ALU.mult))
            link(v.tensor_tensor(b, b, a, ALU.max))
            v.tensor_scalar(b, b, -1.0, math.pi / 2, ALU.mult, ALU.add).then_inc(dve_arg, 1)
            dve.wait_ge(act_ok, 4)
            lr, li, cr, ci = (coef[:, q] for q in range(4))
            v.tensor_tensor(lr, lam[:, 0], lam[:, 2], ALU.mult)
            link(v.tensor_tensor(li, lam[:, 0], lam[:, 1], ALU.mult))
            n1, n2, den, t1, t2 = lam[:, 5], lam[:, 6], lam[:, 7], lam[:, 8], lam[:, 9]
            ar_, ai_ = rows16[:, 0], rows16[:, 1]
            v.tensor_scalar(n1, lr, -1.0, None, ALU.add)
            v.tensor_tensor(t1, ar_, ar_, ALU.mult)
            link(v.tensor_tensor(t2, ai_, ai_, ALU.mult))
            link(v.tensor_tensor(den, t1, t2, ALU.add))
            link(v.reciprocal(den, den))
            v.tensor_tensor(t1, n1, ar_, ALU.mult)
            link(v.tensor_tensor(t2, li, ai_, ALU.mult))
            link(v.tensor_tensor(t1, t1, t2, ALU.add))
            v.tensor_tensor(cr, t1, den, ALU.mult)
            link(v.tensor_tensor(t2, li, ar_, ALU.mult))
            link(v.tensor_tensor(t1, n1, ai_, ALU.mult))
            link(v.tensor_tensor(t2, t2, t1, ALU.subtract))
            v.tensor_tensor(ci, t2, den, ALU.mult).then_inc(coef_ok, 1)
            dve.wait_ge(pe_prm, 1)
            link(v.tensor_copy(prm.rearrange("p q j -> p (q j)"), c.bank[4][:, 0:4 * PAIRS]))

            def cmul(outr, outi, xr, xi, yr, yi, tmp1, tmp2):
                v.tensor_tensor(tmp1, xr, yr, ALU.mult)
                link(v.tensor_tensor(tmp2, xi, yi, ALU.mult))
                link(v.tensor_tensor(outr, tmp1, tmp2, ALU.subtract))
                v.tensor_tensor(tmp1, xr, yi, ALU.mult)
                link(v.tensor_tensor(tmp2, xi, yr, ALU.mult))
                link(v.tensor_tensor(outi, tmp1, tmp2, ALU.add))

            v.memset(pw[:, 0, :, 0], 1.0)
            v.memset(pw[:, 1, :, 0], 0.0)
            v.tensor_copy(pw[:, 0, :, 1], prm[:, 0])
            link(v.tensor_copy(pw[:, 1, :, 1], prm[:, 1]))
            for n in (1, 2, 4):
                top = [pw[:, r, :, n:n + 1].broadcast_to([P, PAIRS, n]) for r in range(2)]
                cmul(pw[:, 0, :, n + 1:2 * n + 1], pw[:, 1, :, n + 1:2 * n + 1],
                     pw[:, 0, :, 1:n + 1], pw[:, 1, :, 1:n + 1], top[0], top[1], ptmp[:, 0, :, 0:n], ptmp[:, 1, :, 0:n])
            for s in range(CH):
                last = v.tensor_copy(pwr[:, :, :, s], pw[:, :, :, CH - 1 - s])
            link(last)
            dve.wait_ge(ld_b, 32)
            wide = lambda ap: ap.unsqueeze(2).broadcast_to([P, PAIRS, GC])
            cmul(bbar[:, 0], bbar[:, 1], wide(prm[:, 2]), wide(prm[:, 3]), braw[:, 0], braw[:, 1], btmp,
                 big[:, 0:PAIRS * GC].rearrange("p (j c) -> p j c", c=GC))
            dve.wait_ge(pe_ct, 1)
            for r in range(2):
                for par in range(2):
                    rows = slice(64 * par, 64 * par + 64)
                    src = c.bank[5 + r][rows, :].rearrange("p (j two c) -> p j two c", two=2, c=GC)[:, :, par, :]
                    last = v.tensor_copy(ct[rows, r], src)
            last.then_inc(ct_ok, 1)
            dve.wait_ge(ct_ok, 1)
            shape4 = [P, PAIRS, CH, GC]
            pr = [pwr[:, r].unsqueeze(3).broadcast_to(shape4) for r in range(2)]
            br = [bbar[:, r].unsqueeze(2).broadcast_to(shape4) for r in range(2)]
            bigw = big[:, 0:PAIRS * CH * GC].rearrange("p (j s c) -> p j s c", s=CH, c=GC)
            v.tensor_tensor(wt[:, 0], pr[0], br[0], ALU.mult)
            link(v.tensor_tensor(bigw, pr[1], br[1], ALU.mult))
            link(v.tensor_tensor(wt[:, 0], wt[:, 0], bigw, ALU.subtract))
            v.tensor_tensor(wt[:, 1], pr[0], br[1], ALU.mult)
            link(v.tensor_tensor(bigw, pr[1], br[0], ALU.mult))
            v.tensor_tensor(wt[:, 1], wt[:, 1], bigw, ALU.add).then_inc(wt_ok, 1)
            dve.wait_ge(wt_ok, 1)
            shape5 = [P, PAIRS, CH + 1, GC]
            pk = [pw[:, r].unsqueeze(3).broadcast_to(shape5) for r in range(2)]
            cc = [ct[:, r].unsqueeze(2).broadcast_to(shape5) for r in range(2)]
            cpv = [cp[:, r].rearrange("p j (k c) -> p j k c", c=GC) for r in range(2)]
            bigc = big.rearrange("p (j k c) -> p j k c", k=CH + 1, c=GC)
            v.tensor_tensor(cpv[0], pk[0], cc[0], ALU.mult)
            link(v.tensor_tensor(bigc, pk[1], cc[1], ALU.mult))
            link(v.tensor_tensor(cpv[0], cpv[0], bigc, ALU.subtract))
            v.tensor_tensor(cpv[1], pk[0], cc[1], ALU.mult)
            link(v.tensor_tensor(bigc, pk[1], cc[0], ALU.mult))
            link(v.tensor_tensor(cpv[1], cpv[1], bigc, ALU.add))
            v.tensor_scalar(cp[:, 1], cp[:, 1], -1.0, None, ALU.mult).then_inc(cp_ok, 1)
            l8 = ev["l8"]
            v.tensor_copy(l8[:, 0, 0], pw[:, 0, :, CH])
            v.tensor_copy(l8[:, 0, 1], pw[:, 0, :, CH])
            v.tensor_copy(l8[:, 1, 1], pw[:, 1, :, CH])
            v.tensor_scalar(l8[:, 1, 0], pw[:, 1, :, CH], -1.0, None, ALU.mult)
            dve.wait_ge(pe_st, 1)
            for r in range(2):
                last = v.tensor_copy(state0[:, r], c.bank[0][:, r * P:(r + 1) * P].rearrange("p (b j) -> p b j", j=PAIRS))
            last.then_inc(st_ok, 1)
            dve.wait_ge(st_ok, 1)
    c.recycle()


def bias_steps(c, block, x, name, heads, dst, cached, news, stage_n, flips, banks_free):
    nc = c.nc
    ld, pe_f, ev_f, neg = c.sem(name + "_load"), c.sem(name + "_pe_flip"), c.sem(name + "_evac"), c.sem(name + "_neg")
    n_b = heads[1] // 2
    n_ld = 2 + 4 * len(cached) + len(news)
    rows = x["bias_rows"].tensor
    jobs = [(dst[:, 2 * q:2 * q + 2, :].rearrange("p h k -> p (h k)"), [(flips[:, 0:P], dst[:, 2 * q:2 * q + 2, :]
             .rearrange("p h k -> p (h k)"), 0, 2 * P * 2)], P) for q in range(n_b)]
    for out, st, _, _ in cached:
        n = out.shape[1]
        jobs.append((out, [(flips[0:32, P:2 * P], st, 0, n)], P))
    for i, (out, _) in enumerate(news):
        jobs.append((out, [(flips[0:33, (2 + b) * P:(3 + b) * P], stage_n[0:33, i, :], NS * b, NS) for b in range(4)], P))

    @block.sync
    def _(sp):
        sp.dma_start(flips, x["flips"]).then_inc(ld, 16)
        sp.dma_start(dst, bass.AP(tensor=rows, offset=heads[0] * BROW + DTOP - P - (P - 1),
                                  ap=[[1, P], [BROW, heads[1]], [1, 2 * P]])).then_inc(ld, 16)
        for _, st, ap, off in cached:
            for h in range(4):
                dst_h = st[NS * h:NS * h + NS]
                if len(ap) == 4:
                    dst_h = dst_h.rearrange("p (m r) -> p m r", r=ap[3][1])
                sp.dma_start(dst_h, bass.AP(tensor=rows, offset=off + h * ap[0][0], ap=ap[1:])).then_inc(ld, 16)
        for i, (_, h0) in enumerate(news):
            sp.dma_start(stage_n[0:32, i, :], bass.AP(tensor=rows, offset=h0 * BROW + DTOP - (NS - 1),
                                                      ap=[[BROW, 4], [1, NS], [1, NS]])).then_inc(ld, 16)

    @block.tensor
    def _(pe):
        pe.wait_ge(ld, 16 * n_ld)
        pe.wait_ge(neg, 1)
        pe.wait_ge(banks_free, 6)
        for n, (out, mms, _) in enumerate(jobs):
            if n >= 8:
                pe.wait_ge(ev_f, n - 7)
            for lhs, rhs, at, w in mms:
                last = nc.tensor.matmul(c.bank[n % 8][:, at:at + w], lhs, rhs, start=True, stop=True)
            last.then_inc(pe_f, 1)

    @block.vector
    def _(dve):
        nc.vector.memset(stage_n[32:33], BIG).then_inc(neg, 1)
        for n, (out, mms, _) in enumerate(jobs):
            dve.wait_ge(pe_f, n + 1)
            nc.vector.tensor_copy(out, c.bank[n % 8][:, 0:out.shape[1]]).then_inc(ev_f, 1)


def even_arena(c):
    ar = Carve(c.arena, c.AR)
    t = {}
    t["qT"] = ar.take(4, TOK)
    t["kT"] = ar.take(TOK)
    t["kv"] = ar.take(3, 2 * P)
    t["uT"] = ar.take(4, TOK)
    t["qS"] = ar.take(NB, 32)
    t["oaT_at"] = ar.at
    t["oaT"] = ar.take(4, TOK)
    t["obT"] = ar.take(4, TOK)
    t["after_s5"] = ar.at
    t["l8"] = ar.take(2, 2, PAIRS)
    t["state0"] = ar.take(2, NB, PAIRS)
    t["win"] = ar.take(PAIRS, 2, P)
    t["cp"] = ar.take(2, PAIRS, (CH + 1) * GC)
    t["wuu"] = ar.take(G, P)
    t["u40_at"] = ar.at
    t["u40"] = ar.take(G * P)
    t["end"] = ar.at
    t["kvc"] = ar.take(NB, 4 * HD)
    t["bias"] = ar.take(A_H, 2 * P)
    t["bs"] = ar.take(2, P + 32)
    t["po"] = ar.take(2 * P)
    t["s5_tmp"] = ar.at
    return t


def norm_steps(c, block, name, gain, xn):
    nc = c.nc
    sq_ok, ms_ok, rstd_ok = c.sem(name + "_sq"), c.sem(name + "_ms"), c.sem(name + "_rstd")
    xn_ok, pe_t, own, turned = c.sem(name + "_xn"), c.sem(name + "_pe_t"), c.sem(name + "_own"), c.sem(name + "_turned")

    @block.scalar
    def _(act):
        for t, rows in enumerate(ROWS):
            nc.scalar.activation(xn[0:rows, t], c.resid[0:rows, t], ACT.Square,
                                 accum_out=c.stat[0:rows, t:t + 1]).then_inc(sq_ok, 1)
        act.wait_ge(ms_ok, 1)
        nc.scalar.activation(c.stat[:, 6:9], c.stat[:, 3:6], ACT.Sqrt).then_inc(rstd_ok, 1)

    @block.vector
    def _(dve):
        v, link = nc.vector, Link(dve, own)
        dve.wait_ge(sq_ok, 3)
        link(v.tensor_scalar(c.stat[:, 3:6], c.stat[:, 0:3], 1.0 / D, EPS, ALU.mult, ALU.add))
        v.reciprocal(c.stat[:, 3:6], c.stat[:, 3:6]).then_inc(ms_ok, 1)
        dve.wait_ge(rstd_ok, 1)
        for t, rows in enumerate(ROWS):
            v.tensor_scalar(xn[0:rows, t], c.resid[0:rows, t], c.stat[0:rows, 6 + t:7 + t], None,
                            ALU.mult).then_inc(xn_ok, 1)
        for t, rows in enumerate(ROWS):
            for h in range(2):
                dve.wait_ge(pe_t, 2 * t + h + 1)
                v.tensor_tensor(c.xnT[:, 4 * h:4 * h + 4, t * P:t * P + rows],
                                c.bank[2 * t + h][:, 0:4 * rows].rearrange("p (k r) -> p k r", k=4),
                                c.gains[:, gain, 4 * h:4 * h + 4].unsqueeze(2).broadcast_to([P, 4, rows]), ALU.mult)\
                    .then_inc(turned, 1)

    @block.tensor
    def _(pe):
        for t, rows in enumerate(ROWS):
            pe.wait_ge(xn_ok, t + 1)
            for h in range(2):
                for k in range(4):
                    last = nc.tensor.transpose(c.bank[2 * t + h][:, k * rows:(k + 1) * rows],
                                               xn[0:rows, t, 4 * h + k:D:KC], c.ident[0:rows, 0:rows])
                last.then_inc(pe_t, 1)
    return turned


def norm_block(c, name, gain, xn):
    with c.nc.Block() as block:
        norm_steps(c, block, name, gain, xn)
    c.recycle()


def even_in_s5_block(c, x, ev, copies):
    nc = c.nc
    unit, ev_act, out_a, pre = c.sem("b1_unit"), c.sem("b1_evac"), c.keep_sem("b1_out"), ev["pre"]
    units = [("u", i) for i in range(4)] + [("q", i) for i in range(4)] + [("k", 0)] + [("kv", t) for t in range(3)]
    unit_bank = [n if n < 4 else (n + 2) % 8 for n in range(12)]
    wq = c.slot(IT_QKV).rearrange("p (k n) -> p k n", n=768)
    wu = c.slot(IT_U)[:, 0:KC * 512].rearrange("p (k n) -> p k n", n=512)
    win, cp, wuu, u40 = ev["win"], ev["cp"], ev["wuu"], ev["u40"][0:NCH]
    ar = Carve(c.slot(IT_GLU), SLOT, 4 * 512)
    U = ar.take(G, NCH)
    V = ar.take(2, PAIRS, NCH)
    ar = Carve(c.arena, ev["oaT_at"] + 4 * TOK, ev["oaT_at"])
    H = ar.take(2, PAIRS, NCH)
    ar = Carve(c.arena, c.AR, ev["s5_tmp"])
    h3 = ar.take(2, 3, PAIRS)
    t1, t2 = ar.take(2, PAIRS), ar.take(2, PAIRS)
    fin = ev["obT"][:, 0, 0:2 * NB * PAIRS].rearrange("p (r b j) -> p r b j", r=2, b=NB)
    st_out = ar.take(2 * P)
    f1 = st_out.rearrange("p (r b j) -> p r b j", r=2, b=NB)
    yT = V.rearrange("p r j n -> p (r j n)").rearrange("p (i t) -> p i t", i=4)
    ygT = U.rearrange("p g n -> p (g n)").rearrange("p (i t) -> p i t", i=4)
    obT, uT = ev["obT"], ev["uT"]
    l8, state0 = ev["l8"], ev["state0"]
    glu = c.slot(IT_GLU)[:, 0:4 * 512].rearrange("p (k n) -> p k n", k=4)
    a_pe, a_ev = c.sem("s5_pe_u40"), c.sem("s5_u40")
    b_pe, b_ev = c.sem("s5_pe_u"), c.sem("s5_u")
    v_pe, v_ev = c.sem("s5_pe_v"), c.sem("s5_v")
    own, walked, swalk = c.sem("s5_own"), c.sem("s5_walked"), c.sem("s5_sample_walked")
    y_pe, y_ev = c.sem("s5_pe_y"), c.sem("s5_y")
    z_pe, z_ev, g_ok = c.sem("s5_pe_z"), c.sem("s5_z"), c.sem("s5_gelu")
    o_pe, o_sg, o_ok = c.sem("s5_pe_glu"), c.sem("s5_sigmoid"), c.sem("s5_out")
    f_pe, f_ok, f_out = c.sem("s5_pe_state"), c.sem("s5_state"), c.sem("s5_state_out")
    ugrp = lambda ap: ap.rearrange("p (g s c) -> p g s c", s=CH, c=GC)
    with nc.Block() as block:
        @block.tensor
        def _(pe):
            def project(n):
                kind, i = units[n]
                bank = c.bank[unit_bank[n]]
                for k in range(KC):
                    kw = dict(start=(k == 0), stop=(k == KC - 1))
                    if kind == "kv":
                        last = nc.tensor.matmul(bank[0:ROWS[i], 0:2 * P], c.xnT[:, k, i * P:i * P + ROWS[i]],
                                                wq[:, k, 512:768], **kw)
                    else:
                        lhs = {"q": wq[:, k, i * P:(i + 1) * P], "k": wq[:, k, 512:640]}.get(kind) if kind != "u" \
                            else wu[:, k, i * P:(i + 1) * P]
                        last = nc.tensor.matmul(bank[:, 0:TOK], lhs, c.xnT[:, k, :], **kw)
                last.then_inc(unit, 1)
            c.arrived(pe, IT_U)
            for n in range(4):
                project(n)
            pe.wait_ge(ev_act, 4)
            for n in range(8):
                i, s0 = n // 2, (n % 2) * 4
                for s in range(4):
                    last = nc.tensor.transpose(c.bank[(n + 4) % 8][0:NCH, s * P:(s + 1) * P],
                                               uT[:, i, s0 + s:TOK:CH], c.ident[:, :])
                last.then_inc(a_pe, 1)
            pe.wait_ge(a_ev, 8)
            for n, (g0, g1) in enumerate(((0, 12), (12, 24), (24, 32))):
                for g in range(g0, g1):
                    last = nc.tensor.transpose(c.bank[n][:, (g - g0) * NCH:(g - g0 + 1) * NCH],
                                               u40[:, g * P:(g + 1) * P], c.ident[0:NCH, 0:NCH])
                last.then_inc(b_pe, 1)
            pe.wait_ge(b_ev, 3)
            cols = [(r, j) for r in range(2) for j in range(PAIRS)]
            for n in range(3):
                for q, (r, j) in enumerate(cols[12 * n:12 * n + 12]):
                    for par in range(2):
                        last = nc.tensor.matmul(c.bank[3 + n][64 * par:64 * par + 64, q * NCH:(q + 1) * NCH],
                                                win[:, j, r, 64 * par:64 * par + 64], U[:, 2 * j + par, :],
                                                start=True, stop=True)
                last.then_inc(v_pe, 1)
            c.arrived(pe, IT_QKV)
            for n in range(4, 12):
                if n >= 9:
                    pe.wait_ge(v_ev, n - 8)
                project(n)
            pe.wait_ge(ev_act, 12)
            pe.wait_ge(swalk, 1)
            for n in range(8):
                j0, par = n // 2 * 4, n % 2
                rows = slice(64 * par, 64 * par + 64)
                if n >= 4:
                    pe.wait_ge(y_ev, n - 3)
                for q in range(4):
                    j = j0 + q
                    out = c.bank[n % 4][0:NCH, q * P:(q + 1) * P]
                    nc.tensor.matmul(out, U[:, 2 * j + par, :], wuu[:, 2 * j + par, :], start=True, stop=False)
                    nc.tensor.matmul(out, H[rows, 0, j, :], cp[rows, 0, j, GC:], start=False, stop=False)
                    last = nc.tensor.matmul(out, H[rows, 1, j, :], cp[rows, 1, j, GC:], start=False, stop=True)
                last.then_inc(y_pe, 1)
            for r in range(2):
                nc.tensor.transpose(c.bank[6][:, r * P:(r + 1) * P], fin[:, r].rearrange("p b j -> p (b j)"), c.ident[:, :])
            for r in range(2):
                last = nc.tensor.transpose(c.bank[6][0:PAIRS, (2 + r) * P:(3 + r) * P], h3[:, 0, r, :], c.ident[:, :])
            last.then_inc(f_pe, 1)
            pe.wait_ge(y_ev, 8)
            y40 = u40.rearrange("p (s m) -> p s m", s=CH)
            for i in range(4):
                for s in range(CH):
                    last = nc.tensor.transpose(c.bank[i][:, s:TOK:CH], y40[:, s, i * P:(i + 1) * P], c.ident[0:NCH, 0:NCH])
                last.then_inc(z_pe, 1)
            pe.wait_ge(g_ok, 4)
            c.arrived(pe, IT_GLU)
            for i in range(4):
                if i < 2:
                    bank = c.bank[4 + i]
                else:
                    bank = c.bank[i - 2]
                for k in range(4):
                    last = nc.tensor.matmul(bank[:, 0:TOK], glu[:, k, i * P:(i + 1) * P], ygT[:, k, :],
                                            start=(k == 0), stop=(k == 3))
                last.then_inc(o_pe, 1)

        @block.scalar
        def _(act):
            def evacuate(n):
                kind, i = units[n]
                act.wait_ge(unit, n + 1)
                ps = c.bank[unit_bank[n]]
                if kind == "kv":
                    ins = nc.scalar.copy(ev["kv"][0:ROWS[i], i, :], ps[0:ROWS[i], 0:2 * P])
                elif kind == "k":
                    ins = nc.scalar.copy(ev["kT"], ps[:, 0:TOK])
                elif kind == "u":
                    ins = nc.scalar.copy(uT[:, i, :], ps[:, 0:TOK])
                else:
                    nc.scalar.copy(ev["qS"].rearrange("p b (i s) -> p b i s", i=4)[:, :, i, :],
                                   ps[:, SEQ:TOK].rearrange("p (b s) -> p b s", b=NB))
                    ins = nc.scalar.copy(ev["qT"][:, i, :], ps[:, 0:TOK])
                ins.then_inc(ev_act, 1)
            for n in range(4):
                evacuate(n)
            for n in range(8):
                i, s0 = n // 2, (n % 2) * 4
                act.wait_ge(a_pe, n + 1)
                for s in range(4):
                    ins = nc.scalar.copy(ugrp(u40)[:, 8 * i:8 * i + 8, s0 + s, :],
                                         c.bank[(n + 4) % 8][0:NCH, s * P:(s + 1) * P].rearrange("p (g c) -> p g c", g=8))
                ins.then_inc(a_ev, 1)
            for n, (g0, g1) in enumerate(((0, 12), (12, 24), (24, 32))):
                act.wait_ge(b_pe, n + 1)
                nc.scalar.copy(U.rearrange("p g n -> p (g n)")[:, g0 * NCH:g1 * NCH],
                               c.bank[n][:, 0:(g1 - g0) * NCH]).then_inc(b_ev, 1)
            Vf = V.rearrange("p r j n -> p (r j n)")
            for n in range(3):
                m = (12, 12, 8)[n] * NCH
                act.wait_ge(v_pe, n + 1)
                nc.scalar.copy(Vf[:, 12 * NCH * n:12 * NCH * n + m], c.bank[3 + n][:, 0:m]).then_inc(v_ev, 1)
            for n in range(4, 12):
                evacuate(n)
            y40 = u40.rearrange("p (s g c) -> p g s c", s=CH, c=GC)
            for n in range(8):
                j0, par = n // 2 * 4, n % 2
                act.wait_ge(y_pe, n + 1)
                for q in range(4):
                    ins = nc.scalar.copy(y40[:, 2 * (j0 + q) + par],
                                         c.bank[n % 4][0:NCH, q * P:(q + 1) * P].rearrange("p (s c) -> p s c", s=CH))
                ins.then_inc(y_ev, 1)
            for i in range(4):
                act.wait_ge(z_ev, i + 1)
                nc.scalar.activation(ygT[:, i], yT[:, i], ACT.Gelu_apprx_tanh).then_inc(g_ok, 1)
            for i in range(4):
                act.wait_ge(o_pe, i + 1)
                bank = c.bank[4 + i] if i < 2 else c.bank[i - 2]
                nc.scalar.activation(obT[:, i], bank[:, 0:TOK], ACT.Sigmoid,
                                     bias=c.cols[:, COL_GLU_B + i:COL_GLU_B + i + 1]).then_inc(o_sg, 1)

        @block.vector
        def _(dve):
            v, link = nc.vector, Link(dve, own)
            pf = slice(0, PCH)
            v.memset(H[:, :, :, 0], 0.0)
            link(v.memset(h3[:, 0], 0.0))
            link(v.tensor_copy(H[:, :, :, PCH:NCH], state0.rearrange("p r b j -> p r j b")))
            dve.wait_ge(v_ev, 3)
            for n in range(PCH):
                a, b = h3[:, n % 2], h3[:, (n + 1) % 2]
                v.tensor_tensor(t1, l8[:, 0], a[:, 0:2], ALU.mult)
                link(v.tensor_tensor(t2, l8[:, 1], a[:, 1:3], ALU.mult))
                link(v.tensor_tensor(t1, t1, V[:, :, :, n], ALU.add))
                v.tensor_tensor(b[:, 0:2], t1, t2, ALU.add)
                link(v.tensor_tensor(b[:, 2], t1[:, 0], t2[:, 0], ALU.add))
                if n + 1 < PCH:
                    last = v.tensor_copy(H[:, :, :, n + 1], b[:, 0:2])
            s8 = [l8[:, q].unsqueeze(2).broadcast_to([P, 2, NB, PAIRS]) for q in range(2)]
            v.tensor_tensor(fin, s8[0], state0, ALU.mult)
            v.tensor_tensor(f1[:, 0], s8[1][:, 0], state0[:, 1], ALU.mult)
            link(v.tensor_tensor(f1[:, 1], s8[1][:, 1], state0[:, 0], ALU.mult))
            link(v.tensor_tensor(fin, fin, f1, ALU.add))
            v.tensor_tensor(fin, fin, V[:, :, :, PCH:NCH].rearrange("p r j b -> p r b j"), ALU.add).then_inc(swalk, 1)
            dve.wait_ge(f_pe, 1)
            so = st_out.rearrange("p (m r) -> p m r", r=2)
            po = ev["po"][0:PAIRS].rearrange("p (m r) -> p m r", r=2)
            for r in range(2):
                v.tensor_copy(so[:, :, r], c.bank[6][:, r * P:(r + 1) * P])
                last = v.tensor_copy(po[:, :, r], c.bank[6][0:PAIRS, (2 + r) * P:(3 + r) * P])
            last.then_inc(f_ok, 1)
            for i in range(4):
                dve.wait_ge(z_pe, i + 1)
                v.scalar_tensor_tensor(yT[:, i], uT[:, i], c.cols[:, COL_D + i:COL_D + i + 1], c.bank[i][:, 0:TOK],
                                       ALU.mult, ALU.add).then_inc(z_ev, 1)
            for i in range(4):
                dve.wait_ge(o_sg, i + 1)
                v.tensor_tensor(obT[:, i], obT[:, i], ygT[:, i], ALU.mult).then_inc(o_ok, 1)

        @block.gpsimd
        def _(pool):
            for g in (2, 1, 0):
                cache_copies(c, x, pool, g, range(NB), copies)
            pool.wait_ge(ev_act, 12)
            kv = ev["kv"]
            pool.dma_start(x["o_a_p"][0, 0].rearrange("w t h d -> w (t h d)"), kv[:, 1, :]).then_inc(out_a, 16)
            pool.dma_start(x["o_a_s"][0, :, P - NS:P].rearrange("b s t h d -> b s (t h d)"),
                           kv[0:NB * NS, 2, :]).then_inc(out_a, 16)
            for b in range(NB):
                pool.dma_start(x["o_a_s"][0, b, 0:P - NS].rearrange("s t h d -> s (t h d)"),
                               x["cache_a_kv"][0, b, NS:P].rearrange("s t h d -> s (t h d)")).then_inc(out_a, 16)
            pool.wait_ge(out_a, 16 * 10)

        @block.sync
        def _(sp):
            for b in range(NB):
                sp.dma_start(ev["kvc"][:, b, :], x["cache_a_kv"][0, b].rearrange("w t h d -> w (t h d)")).then_inc(pre, 16)
            sp.wait_ge(unit, 4)
            c.load_item(sp, IT_U + RING)
            sp.wait_ge(unit, 12)
            c.load_item(sp, IT_QKV + RING)
            sp.wait_ge(f_ok, 1)
            sp.dma_start(x["o_b_s"][0].rearrange("b (j g) n r -> b j (g n r)", g=2).rearrange("b j m -> (b j) m"),
                         st_out).then_inc(f_out, 16)
            sp.dma_start(x["o_b_p"][0, 0].rearrange("(j g) n r -> j (g n r)", g=2), ev["po"][0:PAIRS]).then_inc(f_out, 16)
            sp.wait_ge(o_ok, 4)
            c.load_item(sp, IT_GLU + RING)
            sp.wait_ge(f_out, 32)
    c.recycle()


def softmax_stats(v, dve, link, S, m, nm, sm, sink, arg_ok):
    link(v.tensor_reduce(m, S, AX.X, ALU.max))
    link(v.tensor_tensor(m, m, sink, ALU.max))
    v.tensor_scalar(nm, m, -1.0, None, ALU.mult)
    v.tensor_tensor(sm, sink, m, ALU.subtract).then_inc(arg_ok, 1)


def attn_a_block(c, x, ev):
    nc = c.nc
    qT, kT, kv, qS, oaT, kvc, bias = (ev[n] for n in ("qT", "kT", "kv", "qS", "oaT", "kvc", "bias"))
    ar = Carve(c.arena, ev["end"], ev["after_s5"])
    SK = P + 32
    S = {"s": ar.take(2, 2, SK), "0": ar.take(A_H, P), "1": ar.take(A_H, 2 * P)}
    PT = {"s": ar.take(4, P), "0": ar.take(A_H, P), "1": ar.take(A_H, 2, P)}
    PTn = ar.take(4, P)[0:NB * NS]
    kcT = ar.take(NB, P)
    bs = ev["bs"]
    sinks, sinks_s = ar.take(A_H), ar.take(2, 2)
    st = {k: ar.take(4, 8) for k in "s01"}
    kvs = "s01"
    pre, ld, kc_pe, kc_ok = ev["pre"], c.sem("aa_load"), c.sem("aa_pe_kc"), c.sem("aa_kc")
    sc_pe = {k: c.sem(f"aa_pe_scores_{k}") for k in kvs}
    arg_ok = {k: c.sem(f"aa_arg_{k}") for k in kvs}
    ex_ok = {k: c.sem(f"aa_exp_{k}") for k in kvs}
    p_ok = {k: c.sem(f"aa_probs_{k}") for k in kvs}
    t_pe = {k: c.sem(f"aa_pe_turned_{k}") for k in kvs}
    t_ok = {k: c.sem(f"aa_turned_{k}") for k in kvs}
    o_pe = {k: c.sem(f"aa_pe_out_{k}") for k in kvs}
    own, z_ok = c.sem("aa_own"), c.sem("aa_zero")
    NH = {"s": 4, "0": 8, "1": 8}

    with nc.Block() as block:
        @block.sync
        def _(sp):
            sp.dma_start(sinks, bass.AP(tensor=x["sinks_a"].tensor, offset=0, ap=[[0, P], [1, A_H]])).then_inc(ld, 16)
            for b in range(4):
                for kvh in range(2):
                    sp.dma_start(sinks_s[32 * b:32 * b + 32, kvh, 0:1],
                                 bass.AP(tensor=x["sinks_a"].tensor, offset=4 * kvh,
                                         ap=[[1, 4], [0, NS], [1, 1]])).then_inc(ld, 16)

        @block.tensor
        def _(pe):
            pe.wait_ge(pre, 16 * 8)
            for b in range(NB):
                last = nc.tensor.transpose(c.bank[b // 4][:, (b % 4) * P:(b % 4 + 1) * P], kvc[:, b, 0:P], c.ident[:, :])
            last.then_inc(kc_pe, 1)
            for h in range(A_H):
                rows = slice(64 * (h // 4), 64 * (h // 4) + 64)
                last = nc.tensor.matmul(c.bank[6 + h // 4][:, (h % 4) * P:(h % 4 + 1) * P], qT[rows, h % 4, 0:P],
                                        kT[rows, 0:P], start=True, stop=True)
            last.then_inc(sc_pe["0"], 1)
            pe.wait_ge(kc_ok, 2)
            for half in range(2):
                for kvh in range(2):
                    rows = slice(64 * kvh, 64 * kvh + 64)
                    for b in range(4):
                        lhs = qS[rows, 4 * half + b, :]
                        out = c.bank[4 + kvh][32 * b:32 * b + 32, half * SK:(half + 1) * SK]
                        nc.tensor.matmul(out[:, 0:P], lhs, kcT[rows, 4 * half + b, :], start=True, stop=True)
                        last = nc.tensor.matmul(out[:, P:SK], lhs, kT[rows, SEQ + 32 * half:SEQ + 32 * half + 32],
                                                start=True, stop=True)
            last.then_inc(sc_pe["s"], 1)
            for h in range(A_H):
                rows = slice(64 * (h // 4), 64 * (h // 4) + 64)
                last = nc.tensor.matmul(c.bank[h // 2][:, (h % 2) * 2 * P:(h % 2 + 1) * 2 * P], qT[rows, h % 4, P:2 * P],
                                        kT[rows, 0:2 * P], start=True, stop=True)
            last.then_inc(sc_pe["1"], 1)
            pe.wait_ge(p_ok["0"], 1)
            for h in range(A_H):
                last = nc.tensor.transpose(c.bank[6 + h // 4][:, (h % 4) * P:(h % 4 + 1) * P], S["0"][:, h, :], c.ident[:, :])
            last.then_inc(t_pe["0"], 1)
            pe.wait_ge(p_ok["s"], 1)
            for n in range(4):
                nc.tensor.transpose(c.bank[4][:, n * P:(n + 1) * P], S["s"][:, n // 2, n % 2, 0:P], c.ident[:, :])
                last = nc.tensor.transpose(c.bank[5][0:32, n * P:(n + 1) * P], S["s"][:, n // 2, n % 2, P:SK], c.ident[:, :])
            last.then_inc(t_pe["s"], 1)
            pe.wait_ge(t_ok["0"], 2)
            for h in range(A_H):
                v_cols = slice(P + 64 * (h // 4), P + 64 * (h // 4) + 64)
                last = nc.tensor.matmul(c.bank[6][64 * (h % 2):64 * (h % 2) + 64, (h // 2) * P:(h // 2 + 1) * P],
                                        kv[:, 0, v_cols], PT["0"][:, h, :], start=True, stop=True)
            last.then_inc(o_pe["0"], 1)
            pe.wait_ge(p_ok["1"], 1)
            for h in range(A_H):
                for kb in range(2):
                    n = 2 * h + kb
                    last = nc.tensor.transpose(c.bank[n // 4][:, (n % 4) * P:(n % 4 + 1) * P],
                                               S["1"][:, h, kb * P:(kb + 1) * P], c.ident[:, :])
            last.then_inc(t_pe["1"], 1)
            pe.wait_ge(t_ok["s"], 2)
            pe.wait_ge(z_ok, 1)
            for kvh in range(2):
                for half in range(2):
                    n = 2 * kvh + half
                    for b in range(4):
                        for par in range(2):
                            out = c.bank[7][64 * par:64 * par + 64, :].rearrange("p (i t) -> p i t", t=P)[
                                :, 2 * kvh:2 * kvh + 2, 32 * half + 8 * b:32 * half + 8 * b + 8]
                            sel = lambda ap: ap.rearrange("p (i s) -> p i s", s=NS)[:, par::2, :]
                            v_cols = slice(P + 64 * kvh, P + 64 * kvh + 64)
                            nc.tensor.matmul(out, kvc[:, 4 * half + b, v_cols], sel(PT["s"][:, n, 32 * b:32 * b + 32]),
                                             start=True, stop=False)
                            last = nc.tensor.matmul(out, kv[0:64, 2, v_cols], sel(PTn[:, n, 32 * b:32 * b + 32]),
                                                    start=False, stop=True)
            last.then_inc(o_pe["s"], 1)
            pe.wait_ge(t_ok["1"], 4)
            for h in range(A_H):
                v_cols = slice(P + 64 * (h // 4), P + 64 * (h // 4) + 64)
                out = c.bank[0][64 * (h % 2):64 * (h % 2) + 64, (h // 2) * P:(h // 2 + 1) * P]
                for kb in range(2):
                    last = nc.tensor.matmul(out, kv[:, kb, v_cols], PT["1"][:, h, kb, :], start=(kb == 0), stop=(kb == 1))
            last.then_inc(o_pe["1"], 1)

        @block.scalar
        def _(act):
            for q in range(2):
                act.wait_ge(kc_pe, 1)
                nc.scalar.copy(kcT[:, 4 * q:4 * q + 4, :].rearrange("p b k -> p (b k)"), c.bank[q][:, :]).then_inc(kc_ok, 1)

            def exps(k, rows_of):
                act.wait_ge(arg_ok[k], 1)
                for n in range(NH[k]):
                    nc.scalar.activation(rows_of(n), rows_of(n), ACT.Exp, bias=st[k][:, 1, n:n + 1],
                                         accum_out=st[k][:, 3, n:n + 1])
                nc.scalar.activation(st[k][:, 2, 0:NH[k]], st[k][:, 2, 0:NH[k]], ACT.Exp).then_inc(ex_ok[k], 1)
            exps("0", lambda n: S["0"][:, n, :])
            exps("s", lambda n: S["s"][:, n // 2, n % 2, :])
            exps("1", lambda n: S["1"][:, n, :])
            act.wait_ge(t_pe["0"], 1)
            for q in range(2):
                nc.scalar.copy(PT["0"][:, 4 * q:4 * q + 4, :].rearrange("p h k -> p (h k)"), c.bank[6 + q][:, :])\
                    .then_inc(t_ok["0"], 1)
            act.wait_ge(o_pe["0"], 1)
            nc.scalar.copy(oaT[:, :, 0:P], c.bank[6][:, :].rearrange("p (i t) -> p i t", i=4))
            act.wait_ge(t_pe["1"], 1)
            for q in range(4):
                nc.scalar.copy(PT["1"][:, 2 * q:2 * q + 2, :, :].rearrange("p h b k -> p (h b k)"), c.bank[q][:, :])\
                    .then_inc(t_ok["1"], 1)
            act.wait_ge(o_pe["1"], 1)
            nc.scalar.copy(oaT[:, :, P:2 * P], c.bank[0][:, :].rearrange("p (i t) -> p i t", i=4))

        @block.vector
        def _(dve):
            v, link = nc.vector, Link(dve, own)
            v.memset(PTn, 0.0).then_inc(z_ok, 1)
            dve.wait_ge(pre, 16 * 8)
            dve.wait_ge(ld, 16 * 9)
            dve.wait_ge(sc_pe["0"], 1)
            for q in range(2):
                ins = v.scalar_tensor_tensor(S["0"][:, 4 * q:4 * q + 4, :], c.bank[6 + q][:, :].rearrange("p (h k) -> p h k", h=4),
                                             SCALE, bias[:, 4 * q:4 * q + 4, P:2 * P], ALU.mult, ALU.add)
            link(ins)
            softmax_stats(v, dve, link, S["0"], st["0"][:, 0], st["0"][:, 1], st["0"][:, 2], sinks, arg_ok["0"])
            dve.wait_ge(sc_pe["s"], 1)
            for kvh in range(2):
                ins = v.scalar_tensor_tensor(S["s"][:, kvh], c.bank[4 + kvh][:, 0:2 * SK].rearrange("p (h k) -> p h k", h=2),
                                             SCALE, bs[:, kvh].unsqueeze(1).broadcast_to([P, 2, SK]), ALU.mult, ALU.add)
            link(ins)
            softmax_stats(v, dve, link, S["s"], st["s"][:, 0, 0:4].rearrange("p (a b) -> p a b", a=2),
                          st["s"][:, 1, 0:4].rearrange("p (a b) -> p a b", a=2),
                          st["s"][:, 2, 0:4].rearrange("p (a b) -> p a b", a=2),
                          sinks_s[:, :, 0:1].broadcast_to([P, 2, 2]), arg_ok["s"])
            dve.wait_ge(sc_pe["1"], 1)
            for q in range(4):
                ins = v.scalar_tensor_tensor(S["1"][:, 2 * q:2 * q + 2, :], c.bank[q][:, :].rearrange("p (h k) -> p h k", h=2),
                                             SCALE, bias[:, 2 * q:2 * q + 2, :], ALU.mult, ALU.add)
            link(ins)
            softmax_stats(v, dve, link, S["1"], st["1"][:, 0], st["1"][:, 1], st["1"][:, 2], sinks, arg_ok["1"])

            def normalise(k, view, shape):
                dve.wait_ge(ex_ok[k], 1)
                n = NH[k]
                link(v.tensor_tensor(st[k][:, 3, 0:n], st[k][:, 3, 0:n], st[k][:, 2, 0:n], ALU.add))
                link(v.reciprocal(st[k][:, 3, 0:n], st[k][:, 3, 0:n]))
                v.tensor_tensor(view, view, st[k][:, 3, 0:n].unsqueeze(2).broadcast_to(shape), ALU.mult).then_inc(p_ok[k], 1)
            normalise("0", S["0"], [P, 8, P])
            normalise("s", S["s"].rearrange("p a b k -> p (a b) k"), [P, 4, SK])
            normalise("1", S["1"], [P, 8, 2 * P])
            dve.wait_ge(t_pe["s"], 1)
            v.tensor_copy(PT["s"].rearrange("p n k -> p (n k)"), c.bank[4][:, :]).then_inc(t_ok["s"], 1)
            dve.wait_ge(z_ok, 1)
            for half in range(2):
                ins = v.tensor_copy(PTn[32 * half:32 * half + 32].rearrange("p (k h) m -> p k h m", h=2)[:, :, half, :],
                                    c.bank[5][0:32, :].rearrange("p (k h m) -> p k h m", k=2, h=2)[:, :, half, :])
            ins.then_inc(t_ok["s"], 1)
            dve.wait_ge(o_pe["s"], 1)
            v.tensor_copy(oaT[:, :, SEQ:TOK], c.bank[7][:, :].rearrange("p (i t) -> p i t", i=4)[:, :, 0:64])
    c.recycle()


def out_proj_block(c, name, parts, items):
    nc = c.nc
    done, added = c.sem(name + "_pe"), c.sem(name + "_added")
    n_parts = len(parts)
    where = {}
    for item, k0, n in items:
        w = c.slot(item)[:, 0:n * D].rearrange("p (k n) -> p k n", k=n)
        for k in range(n):
            where[k0 + k] = w[:, k, :]
    with nc.Block() as block:
        @block.tensor
        def _(pe):
            for item, _, _ in items:
                c.arrived(pe, item)
            for t, rows in enumerate(ROWS):
                for h in range(2):
                    for k in range(n_parts):
                        last = nc.tensor.matmul(c.bank[2 * t + h][0:rows, :], parts[k][:, t * P:t * P + rows],
                                                where[k][:, h * 512:(h + 1) * 512], start=(k == 0), stop=(k == n_parts - 1))
                    last.then_inc(done, 1)

        @block.vector
        def _(dve):
            for t, rows in enumerate(ROWS):
                for h in range(2):
                    dve.wait_ge(done, 2 * t + h + 1)
                    r = c.resid[0:rows, t, h * 512:(h + 1) * 512]
                    nc.vector.tensor_tensor(r, c.bank[2 * t + h][0:rows, :], r, ALU.add).then_inc(added, 1)

        @block.sync
        def _(sp):
            sp.wait_ge(done, 6)
            for item, _, _ in items:
                c.load_item(sp, item + RING)
    c.recycle()


OVER = True
PAIR_ROWS = 2 * TOK
SKIP = 1.0e6


def route_consts():
    k = np.zeros((P, 3 * P + 4), np.float32)
    k[:, 0:P] = np.arange(P)[None, :]
    k[:, P:2 * P] = np.arange(P)[:, None] < np.arange(P)[None, :]
    k[:, 2 * P:3 * P] = 1.0
    for t in range(3):
        k[:, 3 * P + t] = t * P + np.arange(P)
    return k


def moe_arena(c):
    ar = Carve(c.arena, c.AR)
    t = {"k": ar.take(3 * P + 4), "xn": ar.take(3, D), "wr": ar.take(KC, 20), "rb": ar.take(20), "lg": ar.take(3, 20),
         "S_room": ar.take(3 * 2 * D), "R": ar.take(3, E_N, 2), "idx": ar.take(2, E_N), "xg": ar.take(3, D),
         "xgT": ar.take(2, KC, CAP), "sg": ar.take(2, FF), "hid": ar.take(2, FF), "hidT": ar.take(2, 2, P),
         "yo": ar.take(3, D), "gmax": ar.take(3, 8), "g8": ar.take(3, 8), "gi": ar.take(3, 8), "e8": ar.take(3, 8),
         "emax": ar.take(3, 8), "ei": ar.take(3, 8), "ge": ar.take(3, 4), "gs": ar.take(3), "gidx": ar.take(3),
         "oh": ar.take(3, 4), "pick": ar.take(3, 4, 4), "q": ar.take(3), "r": ar.take(3), "w": ar.take(2, 3),
         "eid": ar.take(2, 3), "sel": ar.take(2, 3, E_N), "sum": ar.take(3, E_N), "pos": ar.take(3, E_N),
         "tmp": ar.take(3, E_N), "pk": ar.take(2, 3), "ok": ar.take(2, 3), "gov": ar.take(3, E_N), "cnt": ar.take(1),
         "zero": ar.take(E_N), "off": ar.take(2, E_N)}
    t["yp"] = t["S_room"].rearrange("p (t m) -> p t m", t=3)
    t["S"] = t["S_room"][:, 0:3 * E_N * CAP].rearrange("p (t e s) -> p t e s", t=3, e=E_N)
    assert ar.at <= c.AR - SLOT, ar.at
    t["wov"] = c.arena[:, c.AR - SLOT:c.AR]
    return t


def route_block(c, x, layer, m):
    nc = c.nc
    n = f"r{layer}_"
    ld, rows_out = c.sem(n + "load"), c.sem(n + "rows_out")
    lg_pe, own, earg, eok = c.sem(n + "pe_logits"), c.sem(n + "own"), c.sem(n + "exp_arg"), c.sem(n + "exp")
    sel_ok, pos_pe, S_ok, idx_pe = c.sem(n + "sel"), c.sem(n + "pe_pos"), c.sem(n + "onehot"), c.sem(n + "pe_idx")
    k = m["k"]
    iota, tri, ones, tokno = k[:, 0:P], k[:, P:2 * P], k[:, 2 * P:3 * P], k[:, 3 * P:3 * P + 3]
    with nc.Block() as block:
        @block.sync
        def _(sp):
            sp.dma_start(k, x["route_consts"]).then_inc(ld, 16)
            sp.dma_start(m["wr"][:, :, 0:4], x["moe_router_g"][layer].rearrange("(p k) g -> p k g", k=KC)).then_inc(ld, 16)
            sp.dma_start(m["wr"][:, :, 4:20], x["moe_router_e"][layer].rearrange("(p k) g -> p k g", k=KC)).then_inc(ld, 16)
            sp.dma_start(m["rb"][:, 0:4], bass.AP(tensor=x["moe_router_g_b"].tensor, offset=4 * layer, ap=[[0, P], [1, 4]])).then_inc(ld, 16)
            sp.dma_start(m["rb"][:, 4:20], bass.AP(tensor=x["moe_router_e_b"].tensor, offset=E_N * layer, ap=[[0, P], [1, E_N]])).then_inc(ld, 16)
            for t, rows in enumerate(ROWS):
                sp.dma_start(x["x_rows"][t * P:t * P + rows, :], m["xn"][0:rows, t]).then_inc(rows_out, 16)
            sp.wait_ge(rows_out, 48)

        @block.tensor
        def _(pe):
            pe.wait_ge(ld, 80)
            for t, rows in enumerate(ROWS):
                for q in range(KC):
                    last = nc.tensor.matmul(c.bank[6][0:rows, 32 * t:32 * t + 20], c.xnT[:, q, t * P:t * P + rows],
                                            m["wr"][:, q, :], start=(q == 0), stop=(q == KC - 1))
            last.then_inc(lg_pe, 1)
            pe.wait_ge(sel_ok, 1)
            for t in range(3):
                for s in range(t + 1):
                    nc.tensor.matmul(c.bank[7][:, 16 * t:16 * t + 16], tri if s == t else ones, m["sum"][:, s, :],
                                     start=(s == 0), stop=(s == t))
            for s in range(3):
                last = nc.tensor.matmul(c.bank[7][:, 64:80], ones, m["sum"][:, s, :], start=(s == 0), stop=(s == 2))
            last.then_inc(pos_pe, 1)
            for e in range(E_N):
                if e == 0:
                    pe.wait_ge(S_ok, 3)
                for t in range(3):
                    last = nc.tensor.matmul(c.bank[5][0:CAP, 2 * e:2 * e + 2], m["S"][:, t, e, :], m["R"][:, t, e, :],
                                            start=(t == 0), stop=(t == 2))
            last.then_inc(idx_pe, 1)

        @block.scalar
        def _(act):
            act.wait_ge(earg, 1)
            nc.scalar.activation(m["ge"], m["ge"], ACT.Exp).then_inc(eok, 1)
            act.wait_ge(earg, 2)
            nc.scalar.activation(m["q"], m["q"], ACT.Exp).then_inc(eok, 1)

        @block.vector
        def _(dve):
            v, link = nc.vector, Link(dve, own)
            v.memset(m["g8"], -3e38)
            v.memset(m["e8"], -3e38)
            link(v.memset(m["lg"], 0.0))
            dve.wait_ge(lg_pe, 1)
            for t, rows in enumerate(ROWS):
                ins = v.tensor_tensor(m["lg"][0:rows, t], c.bank[6][0:rows, 32 * t:32 * t + 20], m["rb"][0:rows], ALU.add)
            link(ins)
            link(v.tensor_copy(m["g8"][:, :, 0:4], m["lg"][:, :, 0:4]))
            for t in range(3):
                ins = v.max(m["gmax"][:, t], m["g8"][:, t])
            link(ins)
            for t in range(3):
                ins = v.max_index(m["gi"].bitcast(U32)[:, t], m["gmax"][:, t], m["g8"][:, t])
            link(ins)
            v.tensor_tensor(m["ge"], m["lg"][:, :, 0:4], m["gmax"][:, :, 0:1].broadcast_to([P, 3, 4]), ALU.subtract)\
                .then_inc(earg, 1)
            link(v.tensor_copy(m["gidx"], m["gi"].bitcast(U32)[:, :, 0]))
            link(v.tensor_tensor(m["oh"], iota[:, 0:4].unsqueeze(1).broadcast_to([P, 3, 4]),
                                 m["gidx"].unsqueeze(2).broadcast_to([P, 3, 4]), ALU.is_equal))
            link(v.tensor_tensor(m["pick"], m["lg"][:, :, 4:20].rearrange("p t (g e) -> p t e g", g=4),
                                 m["oh"].unsqueeze(2).broadcast_to([P, 3, 4, 4]), ALU.mult))
            link(v.tensor_reduce(m["e8"][:, :, 0:4], m["pick"], AX.X, ALU.add))
            for t in range(3):
                ins = v.max(m["emax"][:, t], m["e8"][:, t])
            link(ins)
            for t in range(3):
                ins = v.max_index(m["ei"].bitcast(U32)[:, t], m["emax"][:, t], m["e8"][:, t])
            link(ins)
            v.tensor_tensor(m["q"], m["emax"][:, :, 1], m["emax"][:, :, 0], ALU.subtract).then_inc(earg, 1)
            for q in range(2):
                ins = v.tensor_copy(m["eid"][:, q], m["ei"].bitcast(U32)[:, :, q])
            link(ins)
            for q in range(2):
                ins = v.scalar_tensor_tensor(m["eid"][:, q], m["gidx"], 4.0, m["eid"][:, q], ALU.mult, ALU.add)
            link(ins)
            for q in range(2):
                ins = v.tensor_tensor(m["sel"][:, q], iota[:, 0:E_N].unsqueeze(1).broadcast_to([P, 3, E_N]),
                                      m["eid"][:, q].unsqueeze(2).broadcast_to([P, 3, E_N]), ALU.is_equal)
            link(ins)
            link(v.memset(m["sel"][64:P, :, 2, :], 0.0))
            v.tensor_tensor(m["sum"], m["sel"][:, 0], m["sel"][:, 1], ALU.add).then_inc(sel_ok, 1)
            dve.wait_ge(eok, 2)
            link(v.tensor_reduce(m["gs"], m["ge"], AX.X, ALU.add))
            v.reciprocal(m["gs"], m["gs"])
            link(v.tensor_scalar(m["r"], m["q"], 1.0, None, ALU.add))
            link(v.reciprocal(m["r"], m["r"]))
            link(v.tensor_tensor(m["w"][:, 0], m["r"], m["gs"], ALU.mult))
            link(v.tensor_tensor(m["w"][:, 1], m["w"][:, 0], m["q"], ALU.mult))
            link(v.tensor_copy(m["R"][:, :, :, 0], tokno.unsqueeze(2).broadcast_to([P, 3, E_N])))
            link(v.tensor_scalar(m["R"][:, :, :, 1], m["R"][:, :, :, 0], 2.0, 1.0, ALU.mult, ALU.add))
            link(v.tensor_tensor(m["R"][:, :, :, 1], m["R"][:, :, :, 1], m["sel"][:, 1], ALU.add))
            link(v.tensor_scalar(m["R"][:, :, :, 0], m["R"][:, :, :, 0], 1.0, None, ALU.add))
            dve.wait_ge(pos_pe, 1)
            link(v.tensor_copy(m["pos"], c.bank[7][:, 0:48].rearrange("p (t e) -> p t e", t=3)))
            link(v.scalar_tensor_tensor(m["tmp"], m["pos"], 1.0, m["sum"], ALU.add, ALU.mult))
            link(v.tensor_scalar(m["tmp"], m["tmp"], -1.0, None, ALU.add))
            for t in range(3):
                v.tensor_tensor(m["S"][:, t], iota[:, 0:CAP].unsqueeze(1).broadcast_to([P, E_N, CAP]),
                                m["tmp"][:, t].unsqueeze(2).broadcast_to([P, E_N, CAP]), ALU.is_equal).then_inc(S_ok, 1)
            dve.wait_ge(S_ok, 3)
            for q in range(2):
                link(v.tensor_tensor(m["tmp"], m["sel"][:, q], m["pos"], ALU.mult))
                link(v.tensor_reduce(m["pk"][:, q], m["tmp"], AX.X, ALU.add))
            link(v.tensor_scalar(m["ok"], m["pk"], float(CAP), None, ALU.is_lt))
            link(v.tensor_tensor(m["ok"], m["ok"], m["w"], ALU.mult))
            link(v.tensor_tensor(m["pk"], m["w"], m["ok"], ALU.subtract))
            link(v.tensor_tensor(m["gov"], m["sel"][:, 0], m["pk"][:, 0].unsqueeze(2).broadcast_to([P, 3, E_N]), ALU.mult))
            link(v.tensor_tensor(m["tmp"], m["sel"][:, 1], m["pk"][:, 1].unsqueeze(2).broadcast_to([P, 3, E_N]), ALU.mult))
            link(v.tensor_tensor(m["gov"], m["gov"], m["tmp"], ALU.add))
            link(v.tensor_reduce(m["gs"][:, 0:1], c.bank[7][:, 64:80], AX.X, ALU.max))
            link(v.tensor_scalar(m["gs"][:, 0:1], m["gs"][:, 0:1], float(CAP), 0.0, ALU.subtract, ALU.max))
            link(v.tensor_copy(m["cnt"].bitcast(I32), m["gs"][:, 0:1]))
            dve.wait_ge(idx_pe, 1)
            ps = c.bank[5][0:CAP, 0:2 * E_N].rearrange("p (e q) -> p q e", q=2)
            off = m["off"][0:CAP]
            link(v.tensor_scalar(off, ps, 0.0, SKIP, ALU.is_equal, ALU.mult))
            link(v.scalar_tensor_tensor(off, ps, -1.0, off, ALU.add, ALU.add))
            link(v.tensor_copy(m["idx"].bitcast(U32)[0:CAP], off))
            for q in range(3):
                v.memset(m["xg"][:, q], 0.0)
    c.recycle()


def experts_block(c, x, layer, m, item0):
    nc = c.nc
    n = f"x{layer}_"
    xg_in, y_out = c.xg_in, c.y_out
    base = [16 * layer * len(range(i, E_N, 3)) for i in range(3)]
    xt_pe, xt_ok = c.sem(n + "pe_xT"), c.sem(n + "xT")
    up_pe, sg_ok, hid_ok = c.sem(n + "pe_up"), c.sem(n + "silu"), c.sem(n + "hidden")
    dn_pe, yo_a, yo_b = c.sem(n + "pe_down"), c.sem(n + "yo_lo"), c.sem(n + "yo_hi")
    yp_in, own = [c.sem(f"{n}rows_in{t}") for t in range(3)], c.sem(n + "own")
    gather_idx, scatter_idx = m["idx"].bitcast(U32)[0:CAP, 0], m["idx"].bitcast(U32)[0:CAP, 1]
    xg, xgT, yo = m["xg"], m["xgT"], m["yo"]
    sg = [m["sg"][:, b, 0:2 * CAP] for b in range(2)]
    hidT = [m["hid"][:, b, 0:2 * CAP] for b in range(2)]
    with nc.Block() as block:
        @block.gpsimd
        def _(pool):
            def scatter(e):
                pool.wait_ge(yo_a, e + 1)
                pool.wait_ge(yo_b, e + 1)
                pool.indirect_dma_start(out=x["y_rows"], out_offset=bass.IndirectOffsetOnAxis(ap=scatter_idx[:, e:e + 1], axis=0),
                                        in_=yo[0:CAP, e % 3], in_offset=None, bounds_check=PAIR_ROWS - 1,
                                        oob_is_err=False).then_inc(y_out[e % 3], 16)
            for e in range(E_N):
                if e >= 3:
                    pool.wait_ge(xt_pe, e - 2)
                pool.indirect_dma_start(out=xg[0:CAP, e % 3], out_offset=None, in_=x["x_rows"],
                                        in_offset=bass.IndirectOffsetOnAxis(ap=gather_idx[:, e:e + 1], axis=0),
                                        bounds_check=TOK - 1, oob_is_err=False).then_inc(xg_in[e % 3], 16)
                if e >= 3:
                    scatter(e - 3)
            for e in range(E_N - 3, E_N):
                scatter(e)

        @block.sync
        def _(sp):
            for e in range(E_N - 1):
                sp.wait_ge(dn_pe, e + 1)
                c.load_item(sp, item0 + e + RING)
            for i in range(3):
                sp.wait_ge(y_out[i], base[i] + 16 * len(range(i, E_N, 3)))
            for t, rows in enumerate(ROWS):
                sp.dma_start(m["yp"][0:rows, t], x["y_rows"].rearrange("(t two) d -> t (two d)", two=2)
                             [t * P:t * P + rows, :]).then_inc(yp_in[t], 16)
            c.load_item(sp, item0 + E_N - 1 + RING)

        @block.tensor
        def _(pe):
            def turn(e):
                pe.wait_ge(xg_in[e % 3], base[e % 3] + 16 * (e // 3 + 1))
                if e >= 1:
                    pe.wait_ge(xt_ok, 2 * e)
                for q in range(KC):
                    last = nc.tensor.transpose(c.bank[q // 4][:, (q % 4) * CAP:(q % 4 + 1) * CAP], xg[0:CAP, e % 3, q:D:KC],
                                               c.ident[0:CAP, 0:CAP])
                last.then_inc(xt_pe, 1)

            def up(e):
                w = c.slot(item0 + e)[:, 0:KC * 2 * FF].rearrange("p (k n) -> p k n", k=KC)
                c.arrived(pe, item0 + e)
                pe.wait_ge(xt_ok, 2 * e + 2)
                if e >= 2:
                    pe.wait_ge(hid_ok, e - 1)
                for j in range(4):
                    for q in range(KC):
                        last = nc.tensor.matmul(c.bank[2 + e % 2][:, j * CAP:(j + 1) * CAP], w[:, q, j * P:(j + 1) * P],
                                                xgT[:, e % 2, q, :], start=(q == 0), stop=(q == KC - 1))
                last.then_inc(up_pe, 1)

            def down(e):
                w = c.slot(item0 + e)[:, KC * 2 * FF:SLOT].rearrange("p (k n) -> p k n", k=2)
                pe.wait_ge(hid_ok, e + 1)
                if e >= 2:
                    pe.wait_ge(yo_a, e - 1)
                    pe.wait_ge(yo_b, e - 1)
                for h in range(2):
                    for q in range(2):
                        last = nc.tensor.matmul(c.bank[4 + 2 * (e % 2) + h][0:CAP, :], hidT[e % 2][:, q * CAP:(q + 1) * CAP],
                                                w[:, q, h * 512:(h + 1) * 512], start=(q == 0), stop=(q == 1))
                last.then_inc(dn_pe, 1)

            turn(0)
            for e in range(E_N):
                up(e)
                if e + 1 < E_N:
                    turn(e + 1)
                down(e)

        @block.scalar
        def _(act):
            def out_half(e):
                act.wait_ge(dn_pe, e + 1)
                if e >= 3:
                    act.wait_ge(y_out[e % 3], base[e % 3] + 16 * (e // 3))
                nc.scalar.copy(yo[0:CAP, e % 3, 0:512], c.bank[4 + 2 * (e % 2)][0:CAP, :]).then_inc(yo_a, 1)
            for e in range(E_N):
                act.wait_ge(up_pe, e + 1)
                if e >= 2:
                    act.wait_ge(hid_ok, e - 1)
                nc.scalar.activation(sg[e % 2], c.bank[2 + e % 2][:, 0:2 * CAP], ACT.Silu).then_inc(sg_ok, 1)
                out_half(e)

        @block.vector
        def _(dve):
            v, link = nc.vector, Link(dve, own)

            def turned(e):
                dve.wait_ge(xt_pe, e + 1)
                if e >= 2:
                    dve.wait_ge(up_pe, e - 1)
                for h in range(2):
                    v.tensor_tensor(xgT[:, e % 2, 4 * h:4 * h + 4, :],
                                    c.bank[h][:, 0:4 * CAP].rearrange("p (k r) -> p k r", k=4),
                                    c.gains[:, 2 + layer, 4 * h:4 * h + 4].unsqueeze(2).broadcast_to([P, 4, CAP]), ALU.mult)\
                        .then_inc(xt_ok, 1)

            def out_half(e):
                dve.wait_ge(dn_pe, e + 1)
                if e >= 3:
                    dve.wait_ge(y_out[e % 3], base[e % 3] + 16 * (e // 3))
                v.tensor_copy(yo[0:CAP, e % 3, 512:D], c.bank[5 + 2 * (e % 2)][0:CAP, :]).then_inc(yo_b, 1)
            turned(0)
            for e in range(E_N):
                dve.wait_ge(sg_ok, e + 1)
                if e >= 2:
                    dve.wait_ge(dn_pe, e - 1)
                v.tensor_tensor(hidT[e % 2], sg[e % 2], c.bank[2 + e % 2][:, 2 * CAP:4 * CAP], ALU.mult).then_inc(hid_ok, 1)
                if e + 1 < E_N:
                    turned(e + 1)
                out_half(e)
            for t, rows in enumerate(ROWS):
                dve.wait_ge(yp_in[t], 16)
                for q in range(2):
                    r = c.resid[0:rows, t]
                    link(v.scalar_tensor_tensor(r, m["yp"][0:rows, t, q * D:(q + 1) * D], m["ok"][0:rows, q, t:t + 1], r,
                                                ALU.mult, ALU.add))
    c.recycle()


def overflow_block(c, x, layer, m):
    nc = c.nc
    n = f"v{layer}_"
    w_in, up_pe, sg_ok, hid_ok = c.sem(n + "w"), c.sem(n + "pe_up"), c.sem(n + "silu"), c.sem(n + "hid")
    hid2, ht_pe, ht_ok, dn_pe, added = c.sem(n + "hid_gated"), c.sem(n + "pe_hT"), c.sem(n + "hT"), c.sem(n + "pe_down"), c.sem(n + "added")
    wov = m["wov"]
    gu = wov[:, 0:KC * 2 * FF].rearrange("p (k n) -> p k n", k=KC)
    dn = wov[:, KC * 2 * FF:SLOT].rearrange("p (k n) -> p k n", k=2)
    parts = c.items[IT_MOE0 if layer == 0 else IT_MOE1]

    def overflow(eng):
        return eng.value_load(m["cnt"].bitcast(I32)[0:1, :], min_val=0, max_val=TOK)

    with nc.Block() as block:
        @block.sync
        def _(sp):
            with sp.If(overflow(sp) > 0):
                with sp.Fori(0, E_N) as e:
                    sp.wait_ge(added, 3 * e + 1)
                    for view, src in zip((gu[:, :, 0:FF], gu[:, :, FF:2 * FF], dn),
                                         (x["moe_w_gate"][layer], x["moe_w_up"][layer], x["moe_w_down"][layer])):
                        k = KC if src.shape[1] == D else 2
                        sp.dma_start(view, src.rearrange("e (p k) f -> e p k f", k=k)[bass.ds(e, 1)]
                                     .rearrange("o p k f -> (o p) k f")).then_inc(w_in, 16)

        @block.tensor
        def _(pe):
            with pe.If(overflow(pe) > 0):
                with pe.Fori(0, E_N) as e:
                    pe.wait_ge(w_in, 48 * e + 48)
                    for t, rows in enumerate(ROWS):
                        pe.wait_ge(added, 3 * e + t + 1)
                        for q in range(KC):
                            last = nc.tensor.matmul(c.bank[2][0:rows, :], c.xnT[:, q, t * P:t * P + rows], gu[:, q, :],
                                                    start=(q == 0), stop=(q == KC - 1))
                        last.then_inc(up_pe, 1)
                        pe.wait_ge(hid2, 3 * e + t + 1)
                        for q in range(2):
                            last = nc.tensor.transpose(c.bank[4][:, q * P:(q + 1) * P], m["hid"][:, 0, q:FF:2], c.ident[:, :])
                        last.then_inc(ht_pe, 1)
                        pe.wait_ge(ht_ok, 3 * e + t + 1)
                        for h in range(2):
                            for q in range(2):
                                last = nc.tensor.matmul(c.bank[5 + h][0:rows, :], m["hidT"][:, 0, q, 0:rows],
                                                        dn[:, q, h * 512:(h + 1) * 512], start=(q == 0), stop=(q == 1))
                        last.then_inc(dn_pe, 1)

        @block.scalar
        def _(act):
            with act.If(overflow(act) > 0):
                with act.Fori(0, E_N) as e:
                    for t, rows in enumerate(ROWS):
                        act.wait_ge(up_pe, 3 * e + t + 1)
                        nc.scalar.activation(m["sg"][0:rows, 0], c.bank[2][0:rows, 0:FF], ACT.Silu).then_inc(sg_ok, 1)
                        act.wait_ge(ht_pe, 3 * e + t + 1)
                        nc.scalar.copy(m["hidT"][:, 0].rearrange("p k m -> p (k m)"), c.bank[4][:, 0:2 * P]).then_inc(ht_ok, 1)

        @block.vector
        def _(dve):
            with dve.If(overflow(dve) > 0):
                v = nc.vector
                v.tensor_copy(m["zero"][:, 0:1], m["gov"][:, 0, 0:1]).then_inc(added, 1)
                with dve.Fori(0, E_N) as e:
                    for t, rows in enumerate(ROWS):
                        dve.wait_ge(sg_ok, 3 * e + t + 1)
                        v.tensor_tensor(m["hid"][0:rows, 0], m["sg"][0:rows, 0], c.bank[2][0:rows, FF:2 * FF], ALU.mult)\
                            .then_inc(hid_ok, 1)
                        dve.wait_ge(hid_ok, 3 * e + t + 1)
                        v.tensor_tensor(m["hid"][0:rows, 0], m["hid"][0:rows, 0],
                                        m["gov"][0:rows, t, bass.ds(e, 1)].broadcast_to([rows, FF]), ALU.mult).then_inc(hid2, 1)
                        dve.wait_ge(dn_pe, 3 * e + t + 1)
                        for h in range(2):
                            r = c.resid[0:rows, t, h * 512:(h + 1) * 512]
                            ins = v.tensor_tensor(r, c.bank[5 + h][0:rows, :], r, ALU.add)
                        ins.then_inc(added, 1)
    c.recycle()


def moe(c, x, layer):
    m = moe_arena(c)
    norm_block(c, f"nf{layer}", 2 + layer, m["xn"])
    route_block(c, x, layer, m)
    experts_block(c, x, layer, m, IT_MOE0 if layer == 0 else IT_MOE1)
    if OVER:
        overflow_block(c, x, layer, m)


NKEY = 2 * 512 + P
NALL = NKEY + 3 * 32
NCHUNK = NKEY // P
LOADS = 6 * 16


def odd_arena(c):
    ar = Carve(c.arena, c.AR)
    t = {"kT": ar.take(6, TOK),
         "vt": ar.take(3, 768), "ocT": ar.take(4, TOK), "odT": ar.take(2, TOK),
         "qbd": ar.take(2, 3, NB, 32),
         "bs": ar.take(NALL)}
    t["after_keep"] = ar.at
    t["qT"] = ar.take(6, SEQ)
    t["bias"] = ar.take(12, 2 * P)
    t["work"] = ar.at
    t["xp"] = ar.take(4, SEQ + 3)
    t["xs"] = ar.take(4, NB, NS + 3)
    t["gT"] = ar.take(4, TOK)
    t["ktok"] = ar.take(3, 768)
    t["K"] = c.arena[:, c.AR - 2 * NCHUNK * 256:c.AR].rearrange("p (b n f) -> p b n f", b=2, f=256)
    return t


def cache_copies(c, x, eng, g, seqs, done):
    w = CACHE[g]
    out, src = x[f"o_d{g}_s"][0], x[f"cache_d_g{g}"][0]
    row = 2 * D_H * HD
    n = (w - NS) // 16 * 16
    flat = lambda ap: ap.rearrange("w t h d -> w (t h d)")
    for b in seqs:
        eng.dma_start(flat(out[b])[0:n, :].rearrange("(a r) f -> a r f", a=16),
                      flat(src[b])[NS:NS + n, :].rearrange("(a r) f -> a r f", a=16)).then_inc(done, 16)
        eng.dma_start(flat(out[b])[n:w - NS, :], flat(src[b])[NS + n:w, :]).then_inc(done, 16)
    return 32 * len(seqs)


def odd_norm_bias(c, x, od):
    st = Carve(c.arena, c.AR, od["work"])
    xn = st.take(3, D)
    flips, s1, s2, s0 = st.take(6 * P), st.take(512)[0:32], st.take(512)[0:32], st.take(P)[0:32]
    stage_n = st.take(3, NS)
    h = lambda g: (A_H + g * D_H) * BROW
    step = [BROW, 4], [1, NS]
    top = DTOP - (NS - 1)
    cached = [(od["bs"][:, 0:512], s1, [*step, [1, 512]], h(1) + top - 512),
              (od["bs"][:, 512:1024], s2, [*step, [16, 64], [1, 8]], h(2) + top - 1024),
              (od["bs"][:, 1024:NKEY], s0, [*step, [1, P]], h(0) + top - P)]
    with c.nc.Block() as block:
        turned = norm_steps(c, block, "n1", 1, xn)
        bias_steps(c, block, x, "bd", (A_H, 12), od["bias"], cached,
                   [(od["bs"][:, NKEY + 32 * g:NKEY + 32 * g + 32], A_H + g * D_H) for g in range(3)], stage_n, flips, turned)
    c.recycle()


def odd_in_block(c, x, od):
    nc = c.nc
    unit, evac, out_d, zero_ok = c.sem("b2_unit"), c.sem("b2_evac"), c.keep_sem("b2_out"), c.sem("b2_zero")
    units = [("x", i) for i in range(4)] + [("g", i) for i in range(4)] + [("q", i) for i in range(6)] \
        + [("k", i) for i in range(6)] + [("v", i) for i in range(6)] + [("t", i) for i in range(6)]
    item = {"x": IT_XR, "g": IT_GATE, "q": IT_Q, "k": IT_K, "v": IT_V}
    w = {kind: c.slot(it)[:, 0:KC * (512 if kind in "xg" else 768)].rearrange("p (k n) -> p k n", k=KC)
         for kind, it in item.items()}
    first = {kind: [u[0] for u in units].index(kind) for kind in "xgqkvt"}
    with nc.Block() as block:
        @block.sync
        def _(sp):
            def caches_out(half, rows_of):
                n = 0
                for g in range(3):
                    w_p = min(WIN[g][0], SEQ)
                    cols = slice(256 * g, 256 * g + 256)
                    for t in range(2):
                        at = t * P - (SEQ - w_p)
                        if at >= 0:
                            sp.dma_start(x[f"o_d{g}_p"][0, 0, at:at + P, half].rearrange("w h d -> w (h d)"),
                                         rows_of[:, t, cols]).then_inc(out_d, 16)
                            n += 1
                    sp.dma_start(x[f"o_d{g}_s"][0, :, CACHE[g] - NS:CACHE[g], half].rearrange("b s h d -> b s (h d)"),
                                 rows_of[0:64, 2, cols]).then_inc(out_d, 16)
                    n += 1
                return n
            n = 0
            for kind, after in (("x", "g"), ("g", "q"), ("q", "k"), ("k", "v"), ("v", "t")):
                sp.wait_ge(unit, first[after])
                c.load_item(sp, item[kind] + RING)
                if kind in "kv":
                    sp.wait_ge(evac, first[after])
                    n += caches_out("kv".index(kind), od["ktok"] if kind == "k" else od["vt"])
            sp.wait_ge(out_d, 16 * n)

        @block.gpsimd
        def _(pool):
            nc.gpsimd.memset(od["qbd"], 0.0)
            nc.gpsimd.memset(od["xp"][:, :, 0:3], 0.0).then_inc(zero_ok, 1)

        @block.tensor
        def _(pe):
            for n, (kind, i) in enumerate(units):
                if n == first[kind] and kind in item:
                    c.arrived(pe, item[kind])
                if n >= 8:
                    pe.wait_ge(evac, n - 7)
                if kind == "t" and i == 0:
                    pe.wait_ge(evac, first["v"])
                bank = c.bank[n % 8]
                if kind == "t":
                    for t, rows in enumerate(ROWS):
                        last = nc.tensor.transpose(bank[:, t * P:t * P + rows], od["ktok"][0:rows, t, i * P:(i + 1) * P],
                                                   c.ident[0:rows, 0:rows])
                for k in range(KC if kind != "t" else 0):
                    kw = dict(start=(k == 0), stop=(k == KC - 1))
                    if kind in "kv":
                        t, c0, m = i // 2, (i % 2) * 512, (512, 256)[i % 2]
                        last = nc.tensor.matmul(bank[0:ROWS[t], 0:m], c.xnT[:, k, t * P:t * P + ROWS[t]],
                                                w[kind][:, k, c0:c0 + m], **kw)
                    else:
                        last = nc.tensor.matmul(bank[:, 0:TOK], w[kind][:, k, i * P:(i + 1) * P], c.xnT[:, k, :], **kw)
                last.then_inc(unit, 1)

        @block.scalar
        def _(act):
            act.wait_ge(zero_ok, 1)
            for n, (kind, i) in enumerate(units):
                act.wait_ge(unit, n + 1)
                ps = c.bank[n % 8]
                if kind == "x":
                    nc.scalar.copy(od["xp"][:, i, 3:SEQ + 3], ps[:, 0:SEQ])
                    ins = nc.scalar.copy(od["xs"][:, i, :, 3:], ps[:, SEQ:TOK].rearrange("p (b s) -> p b s", b=NB))
                elif kind == "g":
                    ins = nc.scalar.activation(od["gT"][:, i, :], ps[:, 0:TOK], ACT.Gelu_apprx_tanh)
                elif kind == "q":
                    nc.scalar.copy(od["qT"][:, i, :], ps[:, 0:SEQ])
                    g, t = i // 2, i % 2
                    for par in range(2):
                        rows = slice(64 * par, 64 * par + 64)
                        ins = nc.scalar.copy(od["qbd"][rows, t, g, :, 16 * t + 8 * par:16 * t + 8 * par + 8],
                                             ps[rows, SEQ:TOK].rearrange("p (b s) -> p b s", b=NB))
                elif kind in "kv":
                    t, c0, m = i // 2, (i % 2) * 512, (512, 256)[i % 2]
                    ins = nc.scalar.copy(od["ktok" if kind == "k" else "vt"][0:ROWS[t], t, c0:c0 + m], ps[0:ROWS[t], 0:m])
                else:
                    ins = nc.scalar.copy(od["kT"][:, i, :], ps[:, 0:TOK])
                ins.then_inc(evac, 1)
    c.recycle()


def load_cache(x, eng, dst, b, half, done):
    row = 2 * D_H * HD
    eng.dma_start(dst[:, 0:4, :], x["cache_d_g1"][0, b].rearrange("(n p) t h d -> p n t (h d)", p=P)[:, :, half, :]).then_inc(done, 16)
    for n in range(4):
        eng.dma_start(dst[:, 4 + n, :], bass.AP(tensor=x["cache_d_g2"].tensor,
                                                offset=(b * CACHE[2] + 256 * n) * row + half * row // 2,
                                                ap=[[16 * row, 16], [row, 8], [1, row // 2]])).then_inc(done, 16)
    eng.dma_start(dst[:, 8, :], x["cache_d_g0"][0, b].rearrange("p t h d -> p t (h d)")[:, half, :]).then_inc(done, 16)


def rglru_block(c, x, od):
    nc = c.nc
    ar = Carve(c.arena, c.AR - 2 * NCHUNK * 256, od["work"])
    xp, xs, gT = ar.take(4, SEQ + 3), ar.take(4, NB, NS + 3), ar.take(4, TOK)
    xc, r, a = ar.take(4, TOK), ar.take(4, TOK), ar.take(4, TOK)
    flat = c.xnT[:, :, :].rearrange("p k t -> p (k t)")
    ig, th = (flat[:, q * 4 * TOK:(q + 1) * 4 * TOK].rearrange("p (i t) -> p i t", i=4) for q in range(2))
    ga, gx = ar.take(4, P), ar.take(4, P)
    srow = ar.take(512)[0:32]
    h0T, sp_, st = ar.take(4, NB), ar.take(6, 4), ar.take(4, 36)
    orow = ar.take(512)[0:36]
    ocT = od["ocT"]
    ld, zero_ok, own = c.sem("lr_load"), c.sem("lr_zero"), c.sem("lr_own")
    st_pe, conv_ok, gate_pe = c.sem("lr_pe_state"), c.sem("lr_conv"), c.sem("lr_pe_gate")
    sg_ok, earg, e_ok = c.sem("lr_sigmoid"), c.sem("lr_exp_arg"), c.sem("lr_exp")
    la_ok, a_ok, sq_arg, sq_ok = c.sem("lr_log_a"), c.sem("lr_a"), c.sem("lr_sqrt_arg"), c.sem("lr_sqrt")
    fin_ok, fin_pe, row_ok, out = c.sem("lr_final"), c.sem("lr_pe_final"), c.sem("lr_rows"), c.sem("lr_out")
    with nc.Block() as block:
        @block.sync
        def _(sp):
            sp.dma_start(srow[0:24], x["state_c_conv"][0].rearrange("b j c -> (b j) c")).then_inc(ld, 16)
            sp.dma_start(srow[24:32], x["state_c_h"][0]).then_inc(ld, 16)
            sp.wait_ge(zero_ok, 1)
            for w, name in ((ga, "gate_a_w"), (gx, "gate_x_w")):
                for par in range(2):
                    sp.dma_start(w[64 * par:64 * par + 64, :, 64 * par:64 * par + 64],
                                 x[name][0].rearrange("(i two) j k -> j two i k", two=2)[:, par]).then_inc(ld, 16)
            for b in range(2):
                load_cache(x, sp, od["K"][:, b], b, 0, od["k_in"][b])
            sp.wait_ge(row_ok, 1)
            sp.dma_start(x["o_h_p"][0], orow[0:1]).then_inc(out, 16)
            sp.dma_start(x["o_h_s"][0], orow[1:9]).then_inc(out, 16)
            sp.dma_start(x["o_c_p"][0, 0], orow[9:12]).then_inc(out, 16)
            sp.dma_start(x["o_c_s"][0].rearrange("b j c -> (b j) c"), orow[12:36]).then_inc(out, 16)
            sp.wait_ge(out, 64)

        @block.gpsimd
        def _(pool):
            nc.gpsimd.memset(ga, 0.0)
            nc.gpsimd.memset(gx, 0.0).then_inc(zero_ok, 1)

        @block.tensor
        def _(pe):
            pe.wait_ge(ld, 16 * 6)
            for i in range(4):
                last = nc.tensor.transpose(c.bank[0][:, 32 * i:32 * i + 32], srow[:, i * P:(i + 1) * P], c.ident[0:32, 0:32])
            last.then_inc(st_pe, 1)
            for i in range(4):
                pe.wait_ge(conv_ok, i + 1)
                nc.tensor.matmul(c.bank[i][:, 0:TOK], ga[:, i, :], xc[:, i, :], start=True, stop=True)
                nc.tensor.matmul(c.bank[4 + i][:, 0:TOK], gx[:, i, :], xc[:, i, :], start=True, stop=True).then_inc(gate_pe, 1)
            pe.wait_ge(fin_ok, 1)
            for i in range(4):
                last = nc.tensor.transpose(c.bank[0][0:36, i * P:(i + 1) * P], st[:, i, :], c.ident[:, :])
            last.then_inc(fin_pe, 1)

        @block.scalar
        def _(act):
            act.wait_ge(earg, 1)
            nc.scalar.activation(sp_[:, 1], sp_[:, 1], ACT.Exp).then_inc(e_ok, 1)
            for i in range(4):
                act.wait_ge(gate_pe, i + 1)
                nc.scalar.activation(r[:, i], c.bank[i][:, 0:TOK], ACT.Sigmoid,
                                     bias=c.cols[:, COL_GA_B + i:COL_GA_B + i + 1])
                nc.scalar.activation(ig[:, i], c.bank[4 + i][:, 0:TOK], ACT.Sigmoid,
                                     bias=c.cols[:, COL_GX_B + i:COL_GX_B + i + 1]).then_inc(sg_ok, 1)
            act.wait_ge(la_ok, 1)
            nc.scalar.activation(a, r, ACT.Exp)
            nc.scalar.activation(th, r, ACT.Tanh).then_inc(a_ok, 1)
            act.wait_ge(sq_arg, 1)
            nc.scalar.activation(th, th, ACT.Sqrt).then_inc(sq_ok, 1)

        @block.vector
        def _(dve):
            v, link = nc.vector, Link(dve, own)
            lam, ex, z, w2, p, mx = c.cols[:, COL_LAM:COL_LAM + 4], sp_[:, 1], sp_[:, 2], sp_[:, 3], sp_[:, 4], sp_[:, 5]
            link(v.tensor_scalar(sp_[:, 0], lam, -1.0, None, ALU.mult))
            v.tensor_scalar(mx, sp_[:, 0], 0.0, None, ALU.max)
            v.tensor_tensor(ex, sp_[:, 0], lam, ALU.min).then_inc(earg, 1)
            dve.wait_ge(e_ok, 1)
            link(v.tensor_scalar(z, ex, 2.0, None, ALU.add))
            link(v.reciprocal(z, z))
            link(v.tensor_tensor(z, z, ex, ALU.mult))
            link(v.tensor_tensor(w2, z, z, ALU.mult))
            link(v.tensor_scalar(p, w2, 1.0 / 17, None, ALU.mult))
            for n in range(15, 1, -2):
                link(v.scalar_tensor_tensor(p, p, 1.0 / n, w2, ALU.add, ALU.mult))
            link(v.tensor_scalar(p, p, 1.0, 2.0, ALU.add, ALU.mult))
            link(v.tensor_tensor(p, p, z, ALU.mult))
            link(v.tensor_tensor(p, p, mx, ALU.add))
            link(v.tensor_scalar(p, p, -8.0, None, ALU.mult))
            dve.wait_ge(st_pe, 1)
            ps = c.bank[0][:, 0:P].rearrange("p (i n) -> p i n", i=4)
            for i in range(4):
                v.tensor_copy(xs[:, i, :, 0:3], ps[:, i, 0:24].rearrange("p (b j) -> p b j", b=NB))
            link(v.tensor_copy(h0T, ps[:, :, 24:32]))
            for i in range(4):
                cw = [c.cols[:, COL_CONV_W + 4 * t + i:COL_CONV_W + 4 * t + i + 1] for t in range(4)]
                out_p, out_s = xc[:, i, 0:SEQ], xc[:, i, SEQ:TOK].rearrange("p (b s) -> p b s", b=NB)
                v.tensor_scalar(out_p, xp[:, i, 0:SEQ], cw[0], c.cols[:, COL_CONV_B + i:COL_CONV_B + i + 1], ALU.mult, ALU.add)
                link(v.tensor_scalar(out_s, xs[:, i, :, 0:NS], cw[0], c.cols[:, COL_CONV_B + i:COL_CONV_B + i + 1], ALU.mult, ALU.add))
                for t in range(1, 4):
                    v.scalar_tensor_tensor(out_p, xp[:, i, t:t + SEQ], cw[t], out_p, ALU.mult, ALU.add)
                    ins = v.scalar_tensor_tensor(out_s, xs[:, i, :, t:t + NS], cw[t], out_s, ALU.mult, ALU.add)
                    if t < 3:
                        link(ins)
                ins.then_inc(conv_ok, 1)
            for i in range(4):
                dve.wait_ge(sg_ok, i + 1)
                ins = v.tensor_scalar(r[:, i], r[:, i], p[:, i:i + 1], None, ALU.mult)
            ins.then_inc(la_ok, 1)
            dve.wait_ge(conv_ok, 4)
            link(v.tensor_tensor(ig, ig, xc, ALU.mult))
            dve.wait_ge(a_ok, 1)
            link(v.tensor_tensor(r, a, a, ALU.mult))
            link(v.tensor_scalar(r, r, 1.0, -1.0, ALU.add, ALU.mult))
            v.tensor_tensor(th, th, r, ALU.mult).then_inc(sq_arg, 1)
            dve.wait_ge(sq_ok, 1)
            link(v.tensor_tensor(ig, ig, th, ALU.mult))
            starts = lambda ap: ap[:, :, SEQ:TOK].rearrange("p i (b s) -> p i b s", b=NB)[:, :, :, 0]
            link(v.tensor_tensor(h0T, h0T, starts(a), ALU.mult))
            link(v.tensor_tensor(starts(ig), starts(ig), h0T, ALU.add))
            v.memset(starts(a), 0.0)
            link(v.memset(a[:, :, 0:1], 0.0))
            one = lambda ap: ap.rearrange("p i t -> p (i t)")
            link(v.tensor_tensor_scan(one(r), one(a), one(ig), 0.0, ALU.mult, ALU.add))
            v.tensor_tensor(ocT, r, gT, ALU.mult)
            v.tensor_copy(st[:, :, 0:1], r[:, :, SEQ - 1:SEQ])
            v.tensor_copy(st[:, :, 1:9], r[:, :, SEQ:TOK].rearrange("p i (b s) -> p i b s", b=NB)[:, :, :, NS - 1])
            v.tensor_copy(st[:, :, 9:12], xp[:, :, SEQ:SEQ + 3])
            for i in range(4):
                ins = v.tensor_copy(st[:, i, 12:36].rearrange("p (b j) -> p b j", b=NB), xs[:, i, :, NS:NS + 3])
            ins.then_inc(fin_ok, 1)
            dve.wait_ge(fin_pe, 1)
            v.tensor_copy(orow, c.bank[0][0:36, :]).then_inc(row_ok, 1)
    c.recycle()


def attn_d_prompt_block(c, x, od):
    nc = c.nc
    qT, kT, vt, bias, odT = od["qT"], od["kT"], od["vt"], od["bias"], od["odT"]
    ar = Carve(c.arena, c.AR - 2 * NCHUNK * 256, od["work"])
    S = [ar.take(4, 3, P), ar.take(4, 3, 2 * P)]
    PT = [ar.take(4, 3, P), ar.take(4, 6, P)]
    st = [ar.take(3, 4) for _ in range(2)]
    kb = (1, 2)
    sc_pe = [c.sem(f"dp_pe_scores{t}") for t in range(2)]
    sc_ok = [c.sem(f"dp_scores{t}") for t in range(2)]
    arg, ex, p_ok = ([c.sem(f"dp_{w}{t}") for t in range(2)] for w in ("arg", "exp", "probs"))
    t_pe, t_ok, o_pe = ([c.sem(f"dp_{w}{t}") for t in range(2)] for w in ("pe_turned", "turned", "pe_out"))
    own = c.sem("dp_own")

    def score_banks(t, h):
        if t == 0:
            return [(h, 0, 3)]
        b = (4, 6, 0, 2)[h]
        return [(b, 0, 2), (b + 1, 2, 1)]

    def turn_place(t, n):
        return (4 if t == 0 else 0) + n // 4, (n % 4) * P
    with nc.Block() as block:
        @block.tensor
        def _(pe):
            def scores(t, h):
                rows = slice(64 * (h % 2), 64 * (h % 2) + 64)
                for bank, g0, n in score_banks(t, h):
                    for g in range(g0, g0 + n):
                        w = kb[t] * P
                        last = nc.tensor.matmul(c.bank[bank][:, (g - g0) * w:(g - g0 + 1) * w],
                                                qT[rows, 2 * g + h // 2, t * P:(t + 1) * P], kT[rows, 2 * g + h // 2, 0:w],
                                                start=True, stop=True)
                last.then_inc(sc_pe[t], 1)

            def turn(t):
                pe.wait_ge(p_ok[t], 1)
                n = 0
                for h in range(4):
                    for g in range(3):
                        for k in range(kb[t]):
                            bank, col = turn_place(t, n)
                            last = nc.tensor.transpose(c.bank[bank][:, col:col + P], S[t][:, h, g, k * P:(k + 1) * P],
                                                       c.ident[:, :])
                            n += 1
                            if n % 4 == 0:
                                last.then_inc(t_pe[t], 1)

            def outs(t):
                pe.wait_ge(t_ok[t], (3, 6)[t])
                for h in range(4):
                    out = c.bank[7][64 * (h % 2):64 * (h % 2) + 64, t * 256 + (h // 2) * P:t * 256 + (h // 2 + 1) * P]
                    n = 3 * kb[t]
                    for i in range(n):
                        g, k = i // kb[t], i % kb[t]
                        last = nc.tensor.matmul(out, vt[:, k, g * 256 + h * 64:g * 256 + h * 64 + 64], PT[t][:, h, i, :],
                                                start=(i == 0), stop=(i == n - 1))
                last.then_inc(o_pe[t], 1)
            for h in range(4):
                scores(0, h)
            for h in range(4):
                if h == 2:
                    pe.wait_ge(sc_ok[0], 2)
                if h == 3:
                    pe.wait_ge(sc_ok[0], 4)
                scores(1, h)
            pe.wait_ge(sc_ok[1], 4)
            turn(0)
            outs(0)
            pe.wait_ge(sc_ok[1], 8)
            pe.wait_ge(t_ok[0], 3)
            turn(1)
            outs(1)

        @block.scalar
        def _(act):
            for t in range(2):
                act.wait_ge(arg[t], 1)
                for h in range(4):
                    row = S[t][:, h].rearrange("p g k -> p (g k)")
                    ins = nc.scalar.activation(row, row, ACT.Exp, bias=st[t][:, 1, h:h + 1], accum_out=st[t][:, 2, h:h + 1])
                ins.then_inc(ex[t], 1)
            for t in range(2):
                for n in range((3, 6)[t]):
                    act.wait_ge(t_pe[t], n + 1)
                    bank, _ = turn_place(t, 4 * n)
                    nc.scalar.copy(PT[t].rearrange("p h n k -> p (h n k)")[:, 512 * n:512 * n + 512], c.bank[bank][:, :])\
                        .then_inc(t_ok[t], 1)
                act.wait_ge(o_pe[t], 1)
                nc.scalar.copy(odT[:, :, t * P:(t + 1) * P], c.bank[7][:, t * 256:t * 256 + 256].rearrange("p (i m) -> p i m", i=2))

        @block.vector
        def _(dve):
            v, link = nc.vector, Link(dve, own)
            bh = bias.rearrange("p (g h) k -> p h g k", g=3)
            for t in range(2):
                for h in range(4):
                    dve.wait_ge(sc_pe[t], h + 1)
                    for bank, g0, n in score_banks(t, h):
                        w = kb[t] * P
                        v.scalar_tensor_tensor(S[t][:, h, g0:g0 + n, :], c.bank[bank][:, 0:n * w].rearrange("p (g k) -> p g k", g=n),
                                               SCALE, bh[:, h, g0:g0 + n, 2 * P - w:2 * P], ALU.mult, ALU.add).then_inc(sc_ok[t], 1)
                dve.wait_ge(sc_ok[t], (4, 8)[t])
                link(v.tensor_reduce(st[t][:, 0], S[t].rearrange("p h g k -> p h (g k)"), AX.X, ALU.max))
                v.tensor_scalar(st[t][:, 1], st[t][:, 0], -1.0, None, ALU.mult).then_inc(arg[t], 1)
            for t in range(2):
                dve.wait_ge(ex[t], 1)
                link(v.reciprocal(st[t][:, 2], st[t][:, 2]))
                rows = S[t].rearrange("p h g k -> p h (g k)")
                v.tensor_tensor(rows, rows, st[t][:, 2].unsqueeze(2).broadcast_to([P, 4, 3 * kb[t] * P]), ALU.mult)\
                    .then_inc(p_ok[t], 1)
    c.recycle()


def attn_d_sample_block(c, x, od):
    nc = c.nc
    kT, vt, qbd, bs, odT, K = od["kT"], od["vt"], od["qbd"], od["bs"], od["odT"], od["K"]
    ar = Carve(c.arena, c.AR - 2 * NCHUNK * 256, od["after_keep"])
    V = ar.take(4, NCHUNK, 256)
    kcT = ar.take(2, NKEY)
    S, PT, PTn = ar.take(NALL), ar.take(NCHUNK, P), ar.take(2, 3, P)[0:64]
    st = ar.take(2, 3)
    rows_o = ar.take(256)
    k_in = od["k_in"]
    v_in = [c.sem(f"ds_v_in{b}") for b in range(4)]
    kt_pe, kt_a, kt_v, sc_pe, sc_ok = (c.sem("ds_pe_kT"), c.sem("ds_kT_act"), c.sem("ds_kT_dve"), c.sem("ds_pe_scores"),
                                       c.sem("ds_scores"))
    arg, ex, t_pe, t_ok, t_new = (c.sem("ds_" + w) for w in ("arg", "exp", "pe_turned", "turned", "turned_new"))
    o_pe, o_ok, own, z_ok = c.sem("ds_pe_out"), c.sem("ds_out"), c.sem("ds_own"), c.sem("ds_zero")
    row_ok, ot_pe = c.sem("ds_out_rows"), c.sem("ds_pe_out_turned")
    banks5 = [(t, q) for t in range(2) for q in range(2)]
    with nc.Block() as block:
        @block.sync
        def _(sp):
            for b in range(4):
                load_cache(x, sp, V[:, b], b, 1, v_in[b])
            for b in range(2, NB):
                sp.wait_ge(kt_pe, 5 * (b - 1))
                load_cache(x, sp, K[:, b % 2], b, 0, k_in[b % 2])
            sp.wait_ge(o_pe, 1)
            for b in range(4):
                load_cache(x, sp, V[:, b], 4 + b, 1, v_in[b])

        @block.tensor
        def _(pe):
            def turn_keys(b):
                pe.wait_ge(k_in[b % 2], LOADS * (b // 2 + 1))
                if b >= 1:
                    pe.wait_ge(kt_a, 3 * b)
                    pe.wait_ge(kt_v, 2 * b)
                for n, (t, q) in enumerate(banks5):
                    for j in range(4):
                        last = nc.tensor.transpose(c.bank[n][:, j * P:(j + 1) * P], K[:, b % 2, 4 * q + j, t * P:(t + 1) * P],
                                                   c.ident[:, :])
                    last.then_inc(kt_pe, 1)
                for t in range(2):
                    last = nc.tensor.transpose(c.bank[4][:, t * P:(t + 1) * P], K[:, b % 2, 8, t * P:(t + 1) * P], c.ident[:, :])
                last.then_inc(kt_pe, 1)

            def scores(b):
                pe.wait_ge(kt_a, 3 * b + 3)
                pe.wait_ge(kt_v, 2 * b + 2)
                if b == 4:
                    pe.wait_ge(sc_ok, 3)
                rows = slice(32 * (b % 4), 32 * (b % 4) + 32)
                for bank, at, g, rhs in [(5, 0, 1, lambda t: kcT[:, t, 0:512]), (6, 0, 2, lambda t: kcT[:, t, 512:1024]),
                                         (7, 0, 0, lambda t: kcT[:, t, 1024:NKEY])] + \
                        [(7, P + 32 * g, g, lambda t, g=g: kT[:, 2 * g + t, SEQ + 32 * (b // 4):SEQ + 32 * (b // 4) + 32])
                         for g in range(3)]:
                    for t in range(2):
                        src = rhs(t)
                        last = nc.tensor.matmul(c.bank[bank][rows, at:at + src.shape[1]], qbd[:, t, g, b, :], src,
                                                start=(t == 0), stop=(t == 1))
                last.then_inc(sc_pe, 1)

            def values(half):
                pe.wait_ge(ex, half + 1)
                pe.wait_ge(kt_a, 12 * (half + 1))
                pe.wait_ge(kt_v, 8 * (half + 1))
                for n in range(NCHUNK):
                    last = nc.tensor.transpose(c.bank[n // 4][:, (n % 4) * P:(n % 4 + 1) * P], S[:, n * P:(n + 1) * P], c.ident[:, :])
                for g in range(3):
                    last = nc.tensor.transpose(c.bank[3][0:32, g * P:(g + 1) * P], S[:, NKEY + 32 * g:NKEY + 32 * g + 32],
                                               c.ident[:, :])
                last.then_inc(t_pe, 1)
                pe.wait_ge(t_ok, 3 * (half + 1))
                pe.wait_ge(t_new, half + 1)
                for g in range(3):
                    nc.tensor.matmul(c.bank[4][:, 0:256], PTn[:, half, g, :], vt[0:64, 2, g * 256:(g + 1) * 256],
                                     start=(g == 0), stop=False)
                for b in range(4):
                    pe.wait_ge(v_in[b], LOADS * (half + 1))
                    for n in range(NCHUNK):
                        last = nc.tensor.matmul(c.bank[4][32 * b:32 * b + 32, 0:256], PT[:, n, 32 * b:32 * b + 32], V[:, b, n, :],
                                                start=False, stop=(n == NCHUNK - 1))
                last.then_inc(o_pe, 1)
                pe.wait_ge(row_ok, half + 1)
                for t in range(2):
                    last = nc.tensor.transpose(c.bank[5][:, t * P:(t + 1) * P], rows_o[:, t * P:(t + 1) * P], c.ident[:, :])
                last.then_inc(ot_pe, 1)
            turn_keys(0)
            for half in range(2):
                for b in range(4 * half, 4 * half + 4):
                    if b % 4 < 3:
                        turn_keys(b + 1)
                    scores(b)
                values(half)
                if half == 0:
                    pe.wait_ge(o_ok, 1)
                    turn_keys(4)

        @block.scalar
        def _(act):
            def keys(b):
                for n in (0, 1, 4):
                    act.wait_ge(kt_pe, 5 * b + n + 1)
                    if b >= 1:
                        act.wait_ge(sc_pe, b)
                    dst = kcT[:, :, 1024:NKEY] if n == 4 else kcT[:, 0, n * 512:(n + 1) * 512]
                    src = c.bank[4][:, 0:2 * P].rearrange("p (t k) -> p t k", t=2) if n == 4 else c.bank[n][:, :]
                    nc.scalar.copy(dst, src).then_inc(kt_a, 1)
            for half in range(2):
                for b in range(4 * half, 4 * half + 4):
                    keys(b)
                act.wait_ge(arg, half + 1)
                nc.scalar.activation(S, S, ACT.Exp, bias=st[:, half, 1:2], accum_out=st[:, half, 2:3]).then_inc(ex, 1)
                act.wait_ge(t_pe, half + 1)
                if half:
                    act.wait_ge(o_pe, half)
                for n, m in enumerate((4, 4, 1)):
                    nc.scalar.copy(PT[:, 4 * n:4 * n + m, :].rearrange("p n k -> p (n k)"), c.bank[n][:, 0:m * P]).then_inc(t_ok, 1)

        @block.vector
        def _(dve):
            v, link = nc.vector, Link(dve, own)
            v.memset(PTn, 0.0).then_inc(z_ok, 1)

            def keys(b):
                for n in (2, 3):
                    dve.wait_ge(kt_pe, 5 * b + n + 1)
                    if b >= 1:
                        dve.wait_ge(sc_pe, b)
                    v.tensor_copy(kcT[:, 1, (n - 2) * 512:(n - 1) * 512], c.bank[n][:, :]).then_inc(kt_v, 1)
            for half in range(2):
                for b in range(4 * half, 4 * half + 4):
                    keys(b)
                dve.wait_ge(sc_pe, 4 * (half + 1))
                if half:
                    dve.wait_ge(t_pe, half)
                for bank, a, b_ in ((5, 0, 512), (6, 512, 1024), (7, 1024, NALL)):
                    v.scalar_tensor_tensor(S[:, a:b_], c.bank[bank][:, 0:b_ - a], SCALE, bs[:, a:b_], ALU.mult, ALU.add)\
                        .then_inc(sc_ok, 1)
                dve.wait_ge(sc_ok, 3 * (half + 1))
                link(v.tensor_reduce(st[:, half, 0:1], S, AX.X, ALU.max))
                v.tensor_scalar(st[:, half, 1:2], st[:, half, 0:1], -1.0, None, ALU.mult).then_inc(arg, 1)
                dve.wait_ge(ex, half + 1)
                link(v.reciprocal(st[:, half, 2:3], st[:, half, 2:3]))
                dve.wait_ge(t_pe, half + 1)
                dve.wait_ge(z_ok, 1)
                v.tensor_copy(PTn[32 * half:32 * half + 32, half].rearrange("p g k -> p (g k)"), c.bank[3][0:32, 0:3 * P])\
                    .then_inc(t_new, 1)
                dve.wait_ge(o_pe, half + 1)
                v.tensor_scalar(rows_o, c.bank[4][:, 0:256], st[:, half, 2:3], None, ALU.mult).then_inc(row_ok, 1)
                dve.wait_ge(ot_pe, half + 1)
                ps = c.bank[5][:, 0:256].rearrange("p (t b m) -> p t b m", t=2, b=4)
                for par in range(2):
                    rows = slice(64 * par, 64 * par + 64)
                    for t in range(2):
                        ins = v.tensor_copy(odT[rows, t, SEQ + 32 * half:SEQ + 32 * half + 32].rearrange("p (b s) -> p b s", b=4),
                                            ps[rows, t, :, 16 * t + 8 * par:16 * t + 8 * par + 8])
                ins.then_inc(o_ok, 1)
    c.recycle()


def final_block(c, x, copies, n_copies):
    nc = c.nc
    g = c.arena[:, 0:D]
    y = c.arena[:, D:4 * D].rearrange("p (t d) -> p t d", t=3)
    ld, sq_ok, ms_ok, rs_ok = c.sem("f_gain"), c.sem("f_sq"), c.sem("f_ms"), c.sem("f_rstd")
    y_ok, out, own = c.sem("f_y"), c.sem("f_out"), c.sem("f_own")
    with nc.Block() as block:
        @block.sync
        def _(sp):
            sp.dma_start(g, bass.AP(tensor=x["norm_final"].tensor, offset=0, ap=[[0, P], [1, D]])).then_inc(ld, 16)
            for t, dst in enumerate((x["y_p"][0, 0:P], x["y_p"][0, P:SEQ], x["y_s"].rearrange("b s d -> (b s) d"))):
                sp.wait_ge(y_ok, t + 1)
                sp.dma_start(dst, y[0:ROWS[t], t]).then_inc(out, 16)
            sp.wait_ge(out, 48)
            sp.wait_ge(copies, n_copies)

        @block.scalar
        def _(act):
            for t, rows in enumerate(ROWS):
                nc.scalar.activation(y[0:rows, t], c.resid[0:rows, t], ACT.Square, accum_out=c.stat[0:rows, t:t + 1]).then_inc(sq_ok, 1)
            act.wait_ge(ms_ok, 1)
            nc.scalar.activation(c.stat[:, 6:9], c.stat[:, 3:6], ACT.Sqrt).then_inc(rs_ok, 1)

        @block.vector
        def _(dve):
            v, link = nc.vector, Link(dve, own)
            dve.wait_ge(sq_ok, 3)
            link(v.tensor_scalar(c.stat[:, 3:6], c.stat[:, 0:3], 1.0 / D, EPS, ALU.mult, ALU.add))
            v.reciprocal(c.stat[:, 3:6], c.stat[:, 3:6]).then_inc(ms_ok, 1)
            dve.wait_ge(rs_ok, 1)
            dve.wait_ge(ld, 16)
            for t, rows in enumerate(ROWS):
                v.scalar_tensor_tensor(y[0:rows, t], c.resid[0:rows, t], c.stat[0:rows, 6 + t:7 + t], g[0:rows], ALU.mult,
                                       ALU.mult).then_inc(y_ok, 1)


def even_norm_bias(c, x, ev):
    xn = c.arena[:, ev["u40_at"]:ev["u40_at"] + 3 * D].rearrange("p (t d) -> p t d", t=3)
    st = Carve(c.arena, ev["after_s5"], ev["oaT_at"])
    flips, stage = st.take(6 * P), st.take(2, P)[0:32]
    stage_n = st.take(2, NS)
    cached = [(ev["bs"][:, kv, 0:P], stage[:, kv, :], [[BROW, 4], [1, NS], [1, P]],
               4 * kv * BROW + DTOP - P - (NS - 1)) for kv in range(2)]
    with c.nc.Block() as block:
        turned = norm_steps(c, block, "n0", 0, xn)
        bias_steps(c, block, x, "ba", (0, A_H), ev["bias"], cached,
                   [(ev["bs"][:, kv, P:P + 32], 4 * kv) for kv in range(2)], stage_n, flips, turned)
    c.recycle()


def program(nc, x):
    with ExitStack() as ctx:
        c = Core(nc, ctx)
        c.set_items(ring_items(x["w_in_even"][0], x["s5_glu_w"][0], x["w_out_even"][0], x["moe_w_gate"], x["moe_w_up"],
                               x["moe_w_down"], x["w_in_odd"][0], x["w_out_odd"][0]))
        x["bias_rows"] = nc.dram_tensor("bias_rows", (20, BROW), F32, kind="Internal").ap()
        x["x_rows"] = nc.dram_tensor("x_rows", (TOK, D), F32, kind="Internal").ap()
        x["y_rows"] = nc.dram_tensor("y_rows", (PAIR_ROWS, D), F32, kind="Internal").ap()
        copies = c.keep_sem("cache_copies")
        constants_block(c, x)
        ev = even_arena(c)
        ev["pre"] = c.keep_sem("ev_prefetched")
        even_norm_bias(c, x, ev)
        even_in_s5_block(c, x, ev, copies)
        attn_a_block(c, x, ev)
        out_proj_block(c, "oe", [ev["oaT"][:, i] for i in range(4)] + [ev["obT"][:, i] for i in range(4)],
                       [(IT_OUT_E, 0, 4), (IT_OUT_E + 1, 4, 4)])
        moe(c, x, 0)
        od = odd_arena(c)
        od["k_in"] = [c.keep_sem(f"od_k_in{b}") for b in range(2)]
        odd_norm_bias(c, x, od)
        odd_in_block(c, x, od)
        rglru_block(c, x, od)
        attn_d_prompt_block(c, x, od)
        attn_d_sample_block(c, x, od)
        out_proj_block(c, "oo", [od["ocT"][:, i] for i in range(4)] + [od["odT"][:, i] for i in range(2)], [(IT_OUT_O, 0, 6)])
        moe(c, x, 1)
        final_block(c, x, copies, 32 * 3 * NB)


_OUTS = [("y_p", (1, 256, 1024)), ("y_s", (8, 8, 1024)), ("o_a_p", (1, 1, 128, 2, 2, 64)), ("o_a_s", (1, 8, 128, 2, 2, 64)),
         ("o_b_p", (1, 1, 32, 64, 2)), ("o_b_s", (1, 8, 32, 64, 2)), ("o_h_p", (1, 1, 512)), ("o_h_s", (1, 8, 512)),
         ("o_c_p", (1, 1, 3, 512)), ("o_c_s", (1, 8, 3, 512)),
         ("o_d0_p", (1, 1, 128, 2, 4, 64)), ("o_d0_s", (1, 8, 128, 2, 4, 64)),
         ("o_d1_p", (1, 1, 256, 2, 4, 64)), ("o_d1_s", (1, 8, 512, 2, 4, 64)),
         ("o_d2_p", (1, 1, 256, 2, 4, 64)), ("o_d2_s", (1, 8, 1024, 2, 4, 64))]


def kernel(**inputs):
    import concourse.bacc as bacc
    from concourse.bass_utils import run_bass_kernel_spmd as run
    nc = bacc.Bacc("TRN2", target_bir_lowering=False, num_devices=1)
    arrays = {name: np.ascontiguousarray(a) for name, a in inputs.items()}
    arrays["onehot"] = bucket_onehots()
    arrays["flips"] = flip_matrices()
    arrays["route_consts"] = route_consts()
    x = {name: nc.dram_tensor("in_" + name, a.shape, F32, kind="ExternalInput").ap() for name, a in arrays.items()}
    for name, shape in _OUTS:
        x[name] = nc.dram_tensor("out_" + name, shape, F32, kind="ExternalOutput").ap()
    program(nc, x)
    r = run(nc, [{"in_" + name: a for name, a in arrays.items()}], core_ids=[0])
    return tuple(r.results[0]["out_" + name] for name, _ in _OUTS)
```

```python
import math
from contextlib import ExitStack

import numpy as np

import concourse.bass as bass
from concourse import mybir

F32 = mybir.dt.float32
I32 = mybir.dt.int32
U32 = mybir.dt.uint32
BF16 = mybir.dt.bfloat16
ALU = mybir.AluOpType
ACT = mybir.ActivationFunctionType
AX = mybir.AxisListType

P = 128
D = 1024
KC = D // P
SEQ, NB, NS = 256, 8, 8
TOK = SEQ + NB * NS
ROWS = (P, P, NB * NS)
HD = 64
BIG = -1e30
EPS = 1e-6
SCALE = HD ** -0.5

G, GC, NST, CH = 32, 16, 64, 8
NCH = TOK // CH
PCH = SEQ // CH
PAIRS = G // 2

DTOP = 1024 + NS - 1
BROW = DTOP + P + 1
NBUCK = 32
A_H, D_H = 8, 4
WIN = ((128, 1), (512, 4), (2048, 16))
CACHE = (128, 512, 1024)

E_N, FF, CAP = 16, 256, 80
SLOT = 6144
RING = 3


def bucket(dist):
    n = max(dist, 0)
    exact = NBUCK // 2
    if n < exact:
        return n
    v = np.log(np.float32(n) / np.float32(exact)).astype(np.float32) / np.float32(math.log(2048 / exact)) * np.float32(exact)
    return min(exact + int(np.float32(v)), NBUCK - 1)


def bucket_onehots():
    oh = np.zeros((NBUCK + 1, 4, BROW), np.float32)
    kinds = ((A_WINDOW_MAX, 1),) + tuple((w, d) for w, d in WIN)
    for k, (far, dil) in enumerate(kinds):
        for x in range(BROW):
            dist = DTOP - x
            ok = 0 <= dist <= far and dist % dil == 0
            oh[bucket(dist) if ok else NBUCK, k, x] = 1.0
    return oh


def flip_matrices():
    f = np.zeros((P, 6, P), np.float32)
    f[np.arange(P), 0, P - 1 - np.arange(P)] = 1.0
    for b in range(4):
        for h in range(4):
            for s in range(NS):
                f[8 * h + NS - 1 - s, 1, 32 * b + 8 * h + s] = 1.0
                f[8 * h + NS - 1 - s, 2 + b, 32 * b + 8 * h + s] = 1.0
        f[32, 2 + b, :] = 1.0
        f[32, 2 + b, 32 * b:32 * b + 32] = 0.0
    return f.reshape(P, 6 * P)


A_WINDOW_MAX = 127


class Carve:

    def __init__(self, tensor, size, at=0):
        self.tensor, self.size, self.at = tensor, size, at

    def take(self, *shape):
        n = int(np.prod(shape))
        assert self.at + n <= self.size, (self.at, n, self.size)
        ap = self.tensor[:, self.at:self.at + n]
        self.at += n
        names = "abcdef"[:len(shape)]
        if len(shape) > 1:
            ap = ap.rearrange("p (" + " ".join(names) + ") -> p " + " ".join(names),
                              **{c: s for c, s in zip(names[1:], shape[1:])})
        return ap


class Link:

    def __init__(self, eng, sem):
        self.eng, self.sem, self.n = eng, sem, 0

    def __call__(self, ins):
        self.n += 1
        ins.then_inc(self.sem, 1)
        self.eng.wait_ge(self.sem, self.n)


class Core:

    def __init__(self, nc, ctx):
        self.nc, self.ctx = nc, ctx
        sb = lambda name, shape, dt=F32: ctx.enter_context(nc.sbuf_tensor(name, shape, dt))
        self.ring = sb("ring", [P, RING * SLOT])
        self.resid = sb("resid", [P, 3, D])
        self.xnT = sb("xnT", [P, KC, TOK])
        self.ident = sb("ident", [P, P])
        self.cols = sb("cols", [P, 40])
        self.gains = sb("gains", [P, 4, KC])
        self.stat = sb("stat", [P, 16])
        self.AR = 28900
        self.arena = sb("arena", [P, self.AR])
        self.bank = [ctx.enter_context(nc.psum_tensor(f"bank{i}", [P, 512], F32)) for i in range(8)]
        self.ring_in = [nc.alloc_semaphore(f"ring_in{i}") for i in range(RING)]

        self.xg_in = [nc.alloc_semaphore(f"xg_in{i}") for i in range(3)]
        self.y_out = [nc.alloc_semaphore(f"y_out{i}") for i in range(3)]
        self.items, self.need, self.temp, self.cleared = None, None, [], []

    def set_items(self, items):
        self.items, self.need = items, []
        landed = [0] * RING
        for i, parts in enumerate(items):
            landed[i % RING] += len(parts)
            self.need.append(landed[i % RING])

    def load_item(self, sp, i):
        if i < len(self.items):
            slot = self.slot(i)
            for view, src in self.items[i]:
                sp.dma_start(view(slot), src).then_inc(self.ring_in[i % RING], 16)

    def sem(self, name):
        self.temp.append(self.nc.alloc_semaphore(name))
        return self.temp[-1]

    def keep_sem(self, name):
        return self.nc.alloc_semaphore(name)

    def recycle(self):
        for sem in self.cleared:
            self.nc.release_semaphore(sem)
        nums = sorted(sem.num for sem in self.temp)
        while nums:
            n = 1
            while n < len(nums) and nums[n] == nums[0] + n:
                n += 1
            self.nc.gpsimd.sem_clear(range(nums[0], nums[0] + n))
            nums = nums[n:]
        self.cleared, self.temp = self.temp, []

    def keep_clock_up(self, bank, n):
        for _ in range(n):
            self.nc.tensor.matmul(bank[:, :], self.ident[:, :], self.resid[:, 0, 0:512], start=True, stop=True)

    def slot(self, i, n=SLOT):
        s = (i % RING) * SLOT
        return self.ring[:, s:s + n]

    def arrived(self, eng, i):
        eng.wait_ge(self.ring_in[i % RING], 16 * self.need[i])


def ring_items(w_in_even, glu, w_out_even, w_gate, w_up, w_down, w_in_odd, w_out_odd):
    items = []

    def kmajor(w, c0, n, k0=0, k1=KC, by_p=True):
        src = w.rearrange("(p k) n -> p k n" if by_p else "(k p) n -> p k n", p=P)[:, k0:k1, c0:c0 + n]
        return lambda s: s[:, 0:(k1 - k0) * n].rearrange("p (k n) -> p k n", n=n), src

    def qkv_parts():
        src = w_in_even.rearrange("(p k) n -> p k n", p=P)
        parts = []
        for kv in range(2):
            for i in range(4):
                parts.append((lambda s, kv=kv, i=i: s[:, 0:KC * 768].rearrange("p (k n) -> p k n", n=768)
                              [:, :, i * 128 + kv * 64:i * 128 + kv * 64 + 64],
                              src[:, :, kv * 256 + i * 64:kv * 256 + i * 64 + 64]))
        parts.append((lambda s: s[:, 0:KC * 768].rearrange("p (k n) -> p k n", n=768)[:, :, 512:768],
                      src[:, :, 512:768]))
        return parts

    def experts(layer, e):
        gu = lambda s: s[:, 0:KC * 2 * FF].rearrange("p (k n) -> p k n", n=2 * FF)
        return [(lambda s: gu(s)[:, :, 0:FF], w_gate[layer, e].rearrange("(p k) f -> p k f", k=KC)),
                (lambda s: gu(s)[:, :, FF:2 * FF], w_up[layer, e].rearrange("(p k) f -> p k f", k=KC)),
                (lambda s: s[:, KC * 2 * FF:SLOT].rearrange("p (k n) -> p k n", n=D),
                 w_down[layer, e].rearrange("(k p) n -> p k n", k=2))]

    items.append(qkv_parts())
    items.append([kmajor(w_in_even, 768, 512)])
    items.append([kmajor(glu, 0, 512, 0, 4, False)])
    items.append([kmajor(w_out_even, 0, D, 0, 4, False)])
    items.append([kmajor(w_out_even, 0, D, 4, 8, False)])
    items += [experts(0, e) for e in range(E_N)]
    for c0, n in ((0, 512), (512, 512), (1024, 768), (1792, 768), (2560, 768)):
        items.append([kmajor(w_in_odd, c0, n)])
    items.append([kmajor(w_out_odd, 0, D, 0, 6, False)])
    items += [experts(1, e) for e in range(E_N)]
    return items


IT_QKV, IT_U, IT_GLU, IT_OUT_E, IT_MOE0 = 0, 1, 2, 3, 5
IT_XR, IT_GATE, IT_Q, IT_K, IT_V, IT_OUT_O, IT_MOE1 = (IT_MOE0 + E_N + i for i in range(7))

COL_D, COL_GLU_B, COL_CONV_W, COL_CONV_B, COL_GA_B, COL_GX_B, COL_LAM = 0, 4, 8, 24, 28, 32, 36


def constants_block(c, x, ev):
    nc = c.nc
    win, cp, wuu, state0 = ev["win"], ev["cp"], ev["wuu"], ev["state0"]
    ar = Carve(c.arena, ev["after_s5"])
    pool_tmp = c.slot(IT_GLU)[:, SLOT - PAIRS * (CH + 1) * GC:SLOT]
    rows16 = ar.take(4, P)[0:PAIRS]
    logdt = ar.take(2)[0:PAIRS]
    lam = ar.take(10, P)[0:PAIRS]
    coef = ar.take(4, P)[0:PAIRS]
    prm = ar.take(4, PAIRS)
    pw = ar.take(2, PAIRS, CH + 1)
    pwr = ar.take(2, PAIRS, CH)
    ptmp = ar.take(2, PAIRS, 4)
    btmp = ar.take(PAIRS, GC)
    vrows = ar.take(P)[0:40]
    sraw = ar.take(2 * P)
    table = ar.take(20)[0:NBUCK + 1]
    flat = c.xnT[:, :, :].rearrange("p k t -> p (k t)")
    onehot = [ar.take(BROW)[0:NBUCK + 1], flat[0:NBUCK + 1, 0:BROW], flat[0:NBUCK + 1, BROW:2 * BROW],
              c.slot(IT_U)[0:NBUCK + 1, KC * 512:KC * 512 + BROW]]
    brow = ar.take(BROW)
    ar = Carve(c.arena, c.AR, ev["end"])
    big = ar.take(PAIRS * (CH + 1) * GC)
    tau = ev["tau"] = big[0:2 * GC, 0:PAIRS * P].rearrange("p (j m) -> p j m", m=P)
    braw = ar.take(2, PAIRS, GC)
    bbar = ar.take(2, PAIRS, GC)
    ct = ar.take(2, PAIRS, GC)
    bbd = c.slot(IT_GLU)[:, 4 * 512:4 * 512 + 4 * PAIRS * GC].rearrange("p (r j m) -> p r j m", r=2, m=2 * GC)
    craw = win.rearrange("p j r m -> p (j r m)")[:, 0:8 * P].rearrange("p (r i t n) -> p r i t n", r=2, i=4, t=2)
    wt = ev["u40"].rearrange("p (r j s c) -> p r j s c", r=2, j=PAIRS, s=CH)

    ld_x, ld_par = c.sem("b0_x"), c.sem("b0_params")
    ld_oh = [c.sem(f"b0_onehot{k}") for k in range(4)]
    ld_b, ld_c, ld_v, ld_tab = c.sem("b0_b"), c.sem("b0_c"), c.sem("b0_vec"), c.sem("b0_table")
    ident_ok, neg_ok, zero_ok = c.sem("b0_ident"), c.sem("b0_neg_row"), c.sem("b0_zero")
    pe_cols, cols_ok = c.sem("b0_pe_cols"), c.sem("b0_cols")
    pe_bias, bias_sb, bias_out = c.sem("b0_pe_bias"), c.sem("b0_bias_sb"), c.sem("b0_bias_out")
    act_ok, dve_arg = c.sem("b0_act"), c.sem("b0_dve_arg")
    dve_own, pool_own, pw_ok = c.sem("b0_dve_own"), c.sem("b0_pool_own"), c.sem("b0_powers")
    coef_ok, pe_prm = c.sem("b0_coef"), c.sem("b0_pe_prm")
    pe_ct, ct_ok = c.sem("b0_pe_ct"), c.sem("b0_ct")
    wt_ok, pe_win, win_ok = c.sem("b0_wt"), c.sem("b0_pe_win"), c.sem("b0_win")
    cp_ok, pe_tau, tau_ok = c.sem("b0_cp"), c.sem("b0_pe_tau"), c.sem("b0_tau")
    zeroed = c.keep_sem("b0_zeroed")
    bbd_zero, bbd_ok = c.sem("b0_bbd_zero"), c.sem("b0_bbd")
    pe_st, st_ok = c.sem("b0_pe_state"), c.sem("b0_state")


    def c_powers():
        shape = [P, PAIRS, CH + 1, GC]
        return ([pw[:, r].unsqueeze(3).broadcast_to(shape) for r in range(2)],
                [ct[:, r].unsqueeze(2).broadcast_to(shape) for r in range(2)],
                [cp[:, r].rearrange("p j (k c) -> p j k c", c=GC) for r in range(2)])

    with nc.Block() as block:
        @block.sync
        def _(sp):
            sp.dma_start(rows16[:, 0, :], x["s5_a_re"][0].rearrange("(j g) n -> j (g n)", g=2)).then_inc(ld_par, 16)
            sp.dma_start(rows16[:, 1, :], x["s5_a_im"][0].rearrange("(j g) n -> j (g n)", g=2)).then_inc(ld_par, 16)
            sp.dma_start(logdt, x["s5_log_dt"][0].rearrange("(j g) -> j g", g=2)).then_inc(ld_par, 16)
            sp.dma_start(table[0:NBUCK, :], x["rel_table"]).then_inc(ld_tab, 16)
            for r, name in enumerate(("s5_b_re", "s5_b_im")):
                sp.dma_start(braw[:, r], x[name][0].rearrange("(j g) n c -> (g n) j c", g=2)).then_inc(ld_b, 16)
            for r, name in enumerate(("s5_c_re", "s5_c_im")):
                for twice in range(2):
                    sp.dma_start(craw[:, r, :, twice, :],
                                 x[name][0].rearrange("(i g) c n -> (g c) i n", g=8)).then_inc(ld_c, 16)
            sp.dma_start(vrows[COL_D:COL_D + 4], x["s5_d"][0].rearrange("(k p) -> k p", p=P)).then_inc(ld_v, 16)
            sp.dma_start(vrows[COL_GLU_B:COL_GLU_B + 4], x["s5_glu_b"][0].rearrange("(k p) -> k p", p=P)).then_inc(ld_v, 16)
            sp.dma_start(vrows[COL_CONV_W:COL_CONV_W + 16], x["conv_w"][0].rearrange("t (k p) -> (t k) p", p=P)).then_inc(ld_v, 16)
            for at, name in ((COL_CONV_B, "conv_b"), (COL_GA_B, "gate_a_b"), (COL_GX_B, "gate_x_b"), (COL_LAM, "lru_lambda")):
                sp.dma_start(vrows[at:at + 4], x[name][0].rearrange("(k p) -> k p", p=P)).then_inc(ld_v, 16)
            for l in range(2):
                sp.dma_start(c.gains[:, l, :], x["norm_mix"][l].rearrange("(p k) -> p k", k=KC)).then_inc(ld_v, 16)
                sp.dma_start(c.gains[:, 2 + l, :], x["norm_ffn"][l].rearrange("(p k) -> p k", k=KC)).then_inc(ld_v, 16)
            sp.dma_start(sraw, x["state_b"][0].rearrange("b (j g) n r -> b j (g n r)", g=2)
                          .rearrange("b j m -> (b j) m")).then_inc(ld_tab, 16)
            for t, src in enumerate((x["x_prompt"][0, 0:P, :], x["x_prompt"][0, P:SEQ, :],
                                     x["x_sample"].rearrange("b s d -> (b s) d"))):
                sp.dma_start(c.resid[0:ROWS[t], t, :], src).then_inc(ld_x, 16)
            sp.wait_ge(ld_v, 16 * 11)
            for i in (IT_U, IT_QKV, IT_GLU):
                c.load_item(sp, i)
            sp.wait_ge(bias_out, 4 * 16)
            sp.wait_ge(ld_x, 48)

        @block.gpsimd
        def _(pool):
            nc.gpsimd.memset(c.stat[:, :], 1.0)
            nc.gpsimd.memset(bbd, 0.0).then_inc(bbd_zero, 1)
            nc.gpsimd.memset(c.ident[:, :], 0.0).then_inc(zero_ok, 1)
            zeros = c.arena[:, c.AR - D:c.AR]
            nc.gpsimd.memset(zeros, 0.0).then_inc(zero_ok, 1)
            pool.wait_ge(zero_ok, 2)
            nc.gpsimd.affine_select(out=c.ident[:, :], in_=c.ident[:, :], compare_op=ALU.not_equal, fill=1.0,
                                    base=0, pattern=[[-1, P]], channel_multiplier=1).then_inc(ident_ok, 1)
            for n in range(PAIR_ROWS // P):
                pool.dma_start(x["y_rows"][n * P:(n + 1) * P, :], zeros).then_inc(zeroed, 16)
            g, link = nc.gpsimd, Link(pool, pool_own)
            pool.wait_ge(pw_ok, 1)
            pool.wait_ge(ct_ok, 1)
            pk, cc, cpv = c_powers()
            tmp = pool_tmp.rearrange("p (j k c) -> p j k c", k=CH + 1, c=GC)
            g.tensor_tensor(cpv[0], pk[0], cc[0], ALU.mult)
            link(g.tensor_tensor(tmp, pk[1], cc[1], ALU.mult))
            g.tensor_tensor(cpv[0], cpv[0], tmp, ALU.subtract).then_inc(cp_ok, 1)
            pool.wait_ge(zeroed, 16 * (PAIR_ROWS // P))

        @block.scalar
        def _(act):
            for k in range(4):
                act.dma_start(onehot[k], x["onehot"][:, k, :]).then_inc(ld_oh[k], 16)
            act.wait_ge(ld_par, 48)
            nc.scalar.activation(logdt, logdt, ACT.Exp).then_inc(act_ok, 1)
            act.wait_ge(dve_arg, 1)
            nc.scalar.activation(lam[:, 0], rows16[:, 2], ACT.Exp).then_inc(act_ok, 1)
            act.wait_ge(dve_arg, 2)
            nc.scalar.activation(lam[:, 1], lam[:, 3], ACT.Sin).then_inc(act_ok, 1)
            nc.scalar.activation(lam[:, 2], lam[:, 4], ACT.Sin).then_inc(act_ok, 1)
            act.wait_ge(pe_cols, 1)
            nc.scalar.copy(c.cols[:, :], c.bank[0][:, 0:40]).then_inc(cols_ok, 1)
            n = 0
            for k in range(4):
                heads = A_H if k == 0 else D_H
                rows = slice(32 * k, 32 * k + heads)
                for j, (a, b) in enumerate(((0, 512), (512, 1024), (1024, BROW))):
                    act.wait_ge(pe_bias, n + 1)
                    nc.scalar.copy(brow[rows, a:b], c.bank[1 + j][0:heads, 0:b - a]).then_inc(bias_sb, 1)
                    n += 1
                act.wait_ge(bias_sb, n)
                h0 = 0 if k == 0 else A_H + (k - 1) * D_H
                act.dma_start(x["bias_rows"][h0:h0 + heads, :], brow[rows]).then_inc(bias_out, 16)
            for b in range(8):
                act.wait_ge(pe_win, b + 1)
                nc.scalar.copy(win[:, 2 * b:2 * b + 2, :, :].rearrange("p j r m -> p (j r m)"),
                               c.bank[4 + b % 4][:, :]).then_inc(win_ok, 1)
            for b in range(4):
                act.wait_ge(pe_tau, b + 1)
                nc.scalar.copy(tau[:, 4 * b:4 * b + 4, :].rearrange("p j m -> p (j m)"), c.bank[b][0:2 * GC, :])\
                    .then_inc(tau_ok, 1)

        @block.tensor
        def _(pe):
            pe.wait_ge(ident_ok, 1)
            pe.wait_ge(coef_ok, 1)
            for q in range(4):
                last = nc.tensor.transpose(c.bank[4][:, q * PAIRS:(q + 1) * PAIRS], coef[:, q, :], c.ident[0:PAIRS, 0:PAIRS])
            last.then_inc(pe_prm, 1)
            pe.wait_ge(ld_c, 64)
            for r in range(2):
                for i in range(4):
                    last = nc.tensor.transpose(c.bank[5 + r][:, i * P:(i + 1) * P],
                                               craw[:, r, i].rearrange("p t n -> p (t n)"), c.ident[:, :])
            last.then_inc(pe_ct, 1)
            pe.wait_ge(ld_v, 16 * 11)
            nc.tensor.transpose(c.bank[0][:, 0:40], vrows, c.ident[0:40, 0:40]).then_inc(pe_cols, 1)
            def bias(k):
                heads = A_H if k == 0 else D_H
                h0 = 0 if k == 0 else A_H + (k - 1) * D_H
                pe.wait_ge(ld_oh[k], 16)
                if k:
                    pe.wait_ge(bias_sb, 3 * k)
                for j, (a, b) in enumerate(((0, 512), (512, 1024), (1024, BROW))):
                    nc.tensor.matmul(c.bank[1 + j][0:heads, 0:b - a], table[:, h0:h0 + heads], onehot[k][:, a:b],
                                     start=True, stop=True).then_inc(pe_bias, 1)

            pe.wait_ge(neg_ok, 1)
            pe.wait_ge(ld_tab, 32)
            bias(0)
            pe.wait_ge(cols_ok, 1)
            sr = sraw.rearrange("p (m r) -> p m r", r=2)
            nc.tensor.transpose(c.bank[0][:, 0:P], sr[:, :, 0], c.ident[:, :])
            nc.tensor.transpose(c.bank[0][:, P:2 * P], sr[:, :, 1], c.ident[:, :]).then_inc(pe_st, 1)
            for k in range(1, 4):
                bias(k)
            pe.wait_ge(ld_x, 48)
            pe.wait_ge(bias_sb, 12)
            c.keep_clock_up(c.bank[3], 2)
            pe.wait_ge(wt_ok, 1)
            pe.wait_ge(ct_ok, 1)
            for b in range(8):
                if b >= 4:
                    pe.wait_ge(win_ok, b - 3)
                for j in range(2 * b, 2 * b + 2):
                    for r in range(2):
                        q = (j - 2 * b) * 2 + r
                        last = nc.tensor.transpose(c.bank[4 + b % 4][:, q * P:(q + 1) * P],
                                                   wt[:, r, j].rearrange("p s c -> p (s c)"), c.ident[:, :])
                last.then_inc(pe_win, 1)
            pe.wait_ge(cp_ok, 2)
            pe.wait_ge(st_ok, 1)
            pe.wait_ge(bbd_ok, 1)
            for b in range(4):
                for q in range(4):
                    j = 4 * b + q
                    out = c.bank[b][0:2 * GC, q * P:(q + 1) * P]
                    nc.tensor.matmul(out, bbd[:, 0, j, :], cp[:, 0, j, 0:P], start=True, stop=False)
                    last = nc.tensor.matmul(out, bbd[:, 1, j, :], cp[:, 1, j, 0:P], start=False, stop=True)
                last.then_inc(pe_tau, 1)

        @block.vector
        def _(dve):
            v = nc.vector
            link = Link(dve, dve_own)
            v.memset(table[NBUCK:NBUCK + 1, :], BIG).then_inc(neg_ok, 1)
            v.memset(wuu, 0.0)
            dve.wait_ge(act_ok, 1)
            dtb = logdt.unsqueeze(2).broadcast_to([PAIRS, 2, NST])
            split = lambda ap: ap.rearrange("p (g n) -> p g n", g=2)
            v.tensor_tensor(split(rows16[:, 2]), split(rows16[:, 0]), dtb, ALU.mult).then_inc(dve_arg, 1)
            link(v.tensor_tensor(split(rows16[:, 3]), split(rows16[:, 1]), dtb, ALU.mult))
            th, turns, a, b = rows16[:, 3], lam[:, 5], lam[:, 3], lam[:, 4]
            magic = float(1.5 * 2 ** 23)
            link(v.tensor_scalar(turns, th, float(1 / (2 * math.pi)), magic, ALU.mult, ALU.add))
            link(v.tensor_scalar(turns, turns, -magic, None, ALU.add))
            c1 = 6.28125
            c2 = 0.0019350051879882812
            c3 = 2 * math.pi - c1 - c2
            for part in (c1, c2, c3):
                link(v.scalar_tensor_tensor(th, turns, -part, th, ALU.mult, ALU.add))
            link(v.tensor_scalar(a, th, 3.1415925, -3.1415925, ALU.min, ALU.max))
            link(v.tensor_scalar(b, a, -1.0, None, ALU.mult))
            link(v.tensor_tensor(b, b, a, ALU.max))
            v.tensor_scalar(b, b, -1.0, math.pi / 2, ALU.mult, ALU.add).then_inc(dve_arg, 1)
            dve.wait_ge(act_ok, 4)
            lr, li, cr, ci = (coef[:, q] for q in range(4))
            v.tensor_tensor(lr, lam[:, 0], lam[:, 2], ALU.mult)
            link(v.tensor_tensor(li, lam[:, 0], lam[:, 1], ALU.mult))
            n1, n2, den, t1, t2 = lam[:, 5], lam[:, 6], lam[:, 7], lam[:, 8], lam[:, 9]
            ar_, ai_ = rows16[:, 0], rows16[:, 1]
            v.tensor_scalar(n1, lr, -1.0, None, ALU.add)
            v.tensor_tensor(t1, ar_, ar_, ALU.mult)
            link(v.tensor_tensor(t2, ai_, ai_, ALU.mult))
            link(v.tensor_tensor(den, t1, t2, ALU.add))
            link(v.reciprocal(den, den))
            v.tensor_tensor(t1, n1, ar_, ALU.mult)
            link(v.tensor_tensor(t2, li, ai_, ALU.mult))
            link(v.tensor_tensor(t1, t1, t2, ALU.add))
            v.tensor_tensor(cr, t1, den, ALU.mult)
            link(v.tensor_tensor(t2, li, ar_, ALU.mult))
            link(v.tensor_tensor(t1, n1, ai_, ALU.mult))
            link(v.tensor_tensor(t2, t2, t1, ALU.subtract))
            v.tensor_tensor(ci, t2, den, ALU.mult).then_inc(coef_ok, 1)
            dve.wait_ge(pe_prm, 1)
            link(v.tensor_copy(prm.rearrange("p q j -> p (q j)"), c.bank[4][:, 0:4 * PAIRS]))

            def cmul(outr, outi, xr, xi, yr, yi, tmp1, tmp2):
                v.tensor_tensor(tmp1, xr, yr, ALU.mult)
                link(v.tensor_tensor(tmp2, xi, yi, ALU.mult))
                link(v.tensor_tensor(outr, tmp1, tmp2, ALU.subtract))
                v.tensor_tensor(tmp1, xr, yi, ALU.mult)
                link(v.tensor_tensor(tmp2, xi, yr, ALU.mult))
                link(v.tensor_tensor(outi, tmp1, tmp2, ALU.add))

            v.memset(pw[:, 0, :, 0], 1.0)
            v.memset(pw[:, 1, :, 0], 0.0)
            v.tensor_copy(pw[:, 0, :, 1], prm[:, 0])
            link(v.tensor_copy(pw[:, 1, :, 1], prm[:, 1]))
            for n in (1, 2, 4):
                top = [pw[:, r, :, n:n + 1].broadcast_to([P, PAIRS, n]) for r in range(2)]
                cmul(pw[:, 0, :, n + 1:2 * n + 1], pw[:, 1, :, n + 1:2 * n + 1],
                     pw[:, 0, :, 1:n + 1], pw[:, 1, :, 1:n + 1], top[0], top[1], ptmp[:, 0, :, 0:n], ptmp[:, 1, :, 0:n])
            for s in range(CH):
                last = v.tensor_copy(pwr[:, :, :, s], pw[:, :, :, CH - 1 - s])
            last.then_inc(pw_ok, 1)
            dve.wait_ge(pw_ok, 1)
            dve.wait_ge(ld_b, 32)
            wide = lambda ap: ap.unsqueeze(2).broadcast_to([P, PAIRS, GC])
            cmul(bbar[:, 0], bbar[:, 1], wide(prm[:, 2]), wide(prm[:, 3]), braw[:, 0], braw[:, 1], btmp,
                 big[:, 0:PAIRS * GC].rearrange("p (j c) -> p j c", c=GC))
            dve.wait_ge(bbd_zero, 1)
            for par in range(2):
                rows = slice(64 * par, 64 * par + 64)
                last = v.tensor_copy(bbd[rows, :, :, par * GC:(par + 1) * GC], bbar[rows])
            last.then_inc(bbd_ok, 1)
            dve.wait_ge(pe_ct, 1)
            for r in range(2):
                for par in range(2):
                    rows = slice(64 * par, 64 * par + 64)
                    src = c.bank[5 + r][rows, :].rearrange("p (j two c) -> p j two c", two=2, c=GC)[:, :, par, :]
                    last = v.tensor_copy(ct[rows, r], src)
            last.then_inc(ct_ok, 1)
            dve.wait_ge(ct_ok, 1)
            shape4 = [P, PAIRS, CH, GC]
            pr = [pwr[:, r].unsqueeze(3).broadcast_to(shape4) for r in range(2)]
            br = [bbar[:, r].unsqueeze(2).broadcast_to(shape4) for r in range(2)]
            bigw = big[:, 0:PAIRS * CH * GC].rearrange("p (j s c) -> p j s c", s=CH, c=GC)
            v.tensor_tensor(wt[:, 0], pr[0], br[0], ALU.mult)
            link(v.tensor_tensor(bigw, pr[1], br[1], ALU.mult))
            link(v.tensor_tensor(wt[:, 0], wt[:, 0], bigw, ALU.subtract))
            v.tensor_tensor(wt[:, 1], pr[0], br[1], ALU.mult)
            link(v.tensor_tensor(bigw, pr[1], br[0], ALU.mult))
            v.tensor_tensor(wt[:, 1], wt[:, 1], bigw, ALU.add).then_inc(wt_ok, 1)
            dve.wait_ge(wt_ok, 1)
            pk, cc, cpv = c_powers()
            tmp = big.rearrange("p (j k c) -> p j k c", k=CH + 1, c=GC)
            v.tensor_tensor(cpv[1], pk[0], cc[1], ALU.mult)
            link(v.tensor_tensor(tmp, pk[1], cc[0], ALU.mult))
            v.scalar_tensor_tensor(cpv[1], cpv[1], -1.0, tmp, ALU.mult, ALU.subtract).then_inc(cp_ok, 1)
            l8 = ev["l8"]
            v.tensor_copy(l8[:, 0, 0], pw[:, 0, :, CH])
            v.tensor_copy(l8[:, 0, 1], pw[:, 0, :, CH])
            v.tensor_copy(l8[:, 1, 1], pw[:, 1, :, CH])
            v.tensor_scalar(l8[:, 1, 0], pw[:, 1, :, CH], -1.0, None, ALU.mult)
            dve.wait_ge(pe_st, 1)
            for r in range(2):
                last = v.tensor_copy(state0[:, r], c.bank[0][:, r * P:(r + 1) * P].rearrange("p (b j) -> p b j", j=PAIRS))
            last.then_inc(st_ok, 1)
            dve.wait_ge(st_ok, 1)
    c.recycle()


def bias_steps(c, block, x, name, heads, dst, cached, news, stage_n, flips, banks_free):
    nc = c.nc
    ld_tiles = c.sem(name + "_load_tiles")
    ld, pe_f, neg = c.sem(name + "_load"), c.sem(name + "_pe_flip"), c.sem(name + "_neg")
    ev_f = [c.sem(name + "_evac_even"), c.sem(name + "_evac_odd")]
    n_b = heads[1] // 2
    n_ld = 4 * len(cached) + len(news)
    rows = x["bias_rows"].tensor
    jobs = [(dst[:, 2 * q:2 * q + 2, :].rearrange("p h k -> p (h k)"), [(flips[:, 0:P], dst[:, 2 * q:2 * q + 2, :]
             .rearrange("p h k -> p (h k)"), 0, 2 * P * 2)], P) for q in range(n_b)]
    for out, st, _, _ in cached:
        n = out.shape[1]
        jobs.append((out, [(flips[0:32, P:2 * P], st, 0, n)], P))
    for i, (out, _) in enumerate(news):
        jobs.append((out, [(flips[0:33, (2 + b) * P:(3 + b) * P], stage_n[0:33, i, :], NS * b, NS) for b in range(4)], P))

    @block.sync
    def _(sp):
        sp.dma_start(flips, x["flips"]).then_inc(ld_tiles, 16)
        sp.dma_start(dst, bass.AP(tensor=rows, offset=heads[0] * BROW + DTOP - P - (P - 1),
                                  ap=[[1, P], [BROW, heads[1]], [1, 2 * P]])).then_inc(ld_tiles, 16)
        for _, st, ap, off in cached:
            for h in range(4):
                dst_h = st[NS * h:NS * h + NS]
                if len(ap) == 4:
                    dst_h = dst_h.rearrange("p (m r) -> p m r", r=ap[3][1])
                sp.dma_start(dst_h, bass.AP(tensor=rows, offset=off + h * ap[0][0], ap=ap[1:])).then_inc(ld, 16)
        for i, (_, h0) in enumerate(news):
            sp.dma_start(stage_n[0:32, i, :], bass.AP(tensor=rows, offset=h0 * BROW + DTOP - (NS - 1),
                                                      ap=[[BROW, 4], [1, NS], [1, NS]])).then_inc(ld, 16)

    @block.tensor
    def _(pe):
        pe.wait_ge(ld_tiles, 32)
        pe.wait_ge(banks_free, 6)
        for n, (out, mms, _) in enumerate(jobs):
            if n == n_b:
                pe.wait_ge(ld, 16 * n_ld)
                pe.wait_ge(neg, 1)
            if n >= 8:
                pe.wait_ge(ev_f[n % 2], (n - 8) // 2 + 1)
            for lhs, rhs, at, w in mms:
                last = nc.tensor.matmul(c.bank[n % 8][:, at:at + w], lhs, rhs, start=True, stop=True)
            last.then_inc(pe_f, 1)

    @block.vector
    def _(dve):
        nc.vector.memset(stage_n[32:33], BIG).then_inc(neg, 1)
        for n, (out, _, _) in enumerate(jobs):
            if n % 2 == 0:
                dve.wait_ge(pe_f, n + 1)
                nc.vector.tensor_copy(out, c.bank[n % 8][:, 0:out.shape[1]]).then_inc(ev_f[0], 1)

    @block.scalar
    def _(act):
        for n, (out, _, _) in enumerate(jobs):
            if n % 2 == 1:
                act.wait_ge(pe_f, n + 1)
                nc.scalar.copy(out, c.bank[n % 8][:, 0:out.shape[1]]).then_inc(ev_f[1], 1)


def even_arena(c):
    ar = Carve(c.arena, c.AR)
    t = {}
    t["qT"] = ar.take(4, TOK)
    t["kT"] = ar.take(TOK)
    t["kv"] = ar.take(3, 2 * P)
    t["uT"] = ar.take(4, TOK)
    t["qS"] = ar.take(NB, 32)
    t["oaT_at"] = ar.at
    t["oaT"] = ar.take(4, TOK)
    t["obT"] = ar.take(4, TOK)
    t["after_s5"] = ar.at
    t["l8"] = ar.take(2, 2, PAIRS)
    t["state0"] = ar.take(2, NB, PAIRS)
    t["win"] = ar.take(PAIRS, 2, P)
    t["cp"] = ar.take(2, PAIRS, (CH + 1) * GC)
    t["wuu"] = ar.take(G, P)
    t["u40_at"] = ar.at
    t["u40"] = ar.take(G * P)
    t["end"] = ar.at
    t["kvc"] = ar.take(NB, 4 * HD)
    t["bias"] = ar.take(A_H, 2 * P)
    t["bs"] = ar.take(2, P + 32)
    t["po"] = ar.take(2 * P)
    t["s5_tmp"] = ar.at
    return t


def norm_steps(c, block, name, gain, xn):
    nc = c.nc
    sq_ok, ms_ok, rstd_ok = c.sem(name + "_sq"), c.sem(name + "_ms"), c.sem(name + "_rstd")
    xn_ok, pe_t, own, turned = c.sem(name + "_xn"), c.sem(name + "_pe_t"), c.sem(name + "_own"), c.sem(name + "_turned")

    @block.scalar
    def _(act):
        for t, rows in enumerate(ROWS):
            nc.scalar.activation(xn[0:rows, t], c.resid[0:rows, t], ACT.Square,
                                 accum_out=c.stat[0:rows, t:t + 1]).then_inc(sq_ok, 1)
        act.wait_ge(ms_ok, 1)
        nc.scalar.activation(c.stat[:, 6:9], c.stat[:, 3:6], ACT.Sqrt).then_inc(rstd_ok, 1)

    @block.vector
    def _(dve):
        v, link = nc.vector, Link(dve, own)
        dve.wait_ge(sq_ok, 3)
        link(v.tensor_scalar(c.stat[:, 3:6], c.stat[:, 0:3], 1.0 / D, EPS, ALU.mult, ALU.add))
        v.reciprocal(c.stat[:, 3:6], c.stat[:, 3:6]).then_inc(ms_ok, 1)
        dve.wait_ge(rstd_ok, 1)
        for t, rows in enumerate(ROWS):
            v.tensor_scalar(xn[0:rows, t], c.resid[0:rows, t], c.stat[0:rows, 6 + t:7 + t], None,
                            ALU.mult).then_inc(xn_ok, 1)
        for t, rows in enumerate(ROWS):
            for h in range(2):
                dve.wait_ge(pe_t, 2 * t + h + 1)
                v.tensor_tensor(c.xnT[:, 4 * h:4 * h + 4, t * P:t * P + rows],
                                c.bank[2 * t + h][:, 0:4 * rows].rearrange("p (k r) -> p k r", k=4),
                                c.gains[:, gain, 4 * h:4 * h + 4].unsqueeze(2).broadcast_to([P, 4, rows]), ALU.mult)\
                    .then_inc(turned, 1)

    @block.tensor
    def _(pe):
        for t, rows in enumerate(ROWS):
            pe.wait_ge(xn_ok, t + 1)
            for h in range(2):
                for k in range(4):
                    last = nc.tensor.transpose(c.bank[2 * t + h][:, k * rows:(k + 1) * rows],
                                               xn[0:rows, t, 4 * h + k:D:KC], c.ident[0:rows, 0:rows])
                last.then_inc(pe_t, 1)
    return turned


def even_in_s5_block(c, x, ev, copies):
    nc = c.nc
    unit, ev_act, out_a, pre = c.sem("b1_unit"), c.sem("b1_evac"), c.keep_sem("b1_out"), ev["pre"]
    units = [("u", i) for i in range(4)] + [("q", i) for i in range(4)] + [("k", 0)] + [("kv", t) for t in range(3)]
    unit_bank = [n if n < 4 else (n + 2) % 8 for n in range(12)]
    wq = c.slot(IT_QKV).rearrange("p (k n) -> p k n", n=768)
    wu = c.slot(IT_U)[:, 0:KC * 512].rearrange("p (k n) -> p k n", n=512)
    win, cp, wuu, u40 = ev["win"], ev["cp"], ev["wuu"], ev["u40"][0:NCH]
    ar = Carve(c.slot(IT_GLU), SLOT, 4 * 512)
    U = ar.take(G, NCH)
    V = ar.take(2, PAIRS, NCH)
    ar = Carve(c.arena, ev["oaT_at"] + 4 * TOK, ev["oaT_at"])
    H = ar.take(2, PAIRS, NCH)
    ar = Carve(c.arena, c.AR, ev["s5_tmp"])
    h3 = ar.take(2, 3, PAIRS)
    t1, t2 = ar.take(2, PAIRS), ar.take(2, PAIRS)
    fin = ev["obT"][:, 0, 0:2 * NB * PAIRS].rearrange("p (r b j) -> p r b j", r=2, b=NB)
    st_out = ar.take(2 * P)
    f1 = st_out.rearrange("p (r b j) -> p r b j", r=2, b=NB)
    yT = V.rearrange("p r j n -> p (r j n)").rearrange("p (i t) -> p i t", i=4)
    ygT = U.rearrange("p g n -> p (g n)").rearrange("p (i t) -> p i t", i=4)
    obT, uT = ev["obT"], ev["uT"]
    l8, state0 = ev["l8"], ev["state0"]
    glu = c.slot(IT_GLU)[:, 0:4 * 512].rearrange("p (k n) -> p k n", k=4)
    a_pe, a_ev = c.sem("s5_pe_u40"), c.sem("s5_u40")
    b_pe, b_ev = c.sem("s5_pe_u"), c.sem("s5_u")
    v_pe, v_ev = c.sem("s5_pe_v"), c.sem("s5_v")
    own, walked, swalk = c.sem("s5_own"), c.sem("s5_walked"), c.sem("s5_sample_walked")
    y_pe, y_ev = c.sem("s5_pe_y"), c.sem("s5_y")
    z_pe, z_ev, g_ok = c.sem("s5_pe_z"), c.sem("s5_z"), c.sem("s5_gelu")
    o_pe, o_sg, o_ok = c.sem("s5_pe_glu"), c.sem("s5_sigmoid"), c.sem("s5_out")
    f_pe, f_ok, f_out = c.sem("s5_pe_state"), c.sem("s5_state"), c.sem("s5_state_out")
    ugrp = lambda ap: ap.rearrange("p (g s c) -> p g s c", s=CH, c=GC)
    with nc.Block() as block:
        @block.tensor
        def _(pe):
            def project(n):
                kind, i = units[n]
                bank = c.bank[unit_bank[n]]
                for k in range(KC):
                    kw = dict(start=(k == 0), stop=(k == KC - 1))
                    if kind == "kv":
                        last = nc.tensor.matmul(bank[0:ROWS[i], 0:2 * P], c.xnT[:, k, i * P:i * P + ROWS[i]],
                                                wq[:, k, 512:768], **kw)
                    else:
                        lhs = {"q": wq[:, k, i * P:(i + 1) * P], "k": wq[:, k, 512:640]}.get(kind) if kind != "u" \
                            else wu[:, k, i * P:(i + 1) * P]
                        last = nc.tensor.matmul(bank[:, 0:TOK], lhs, c.xnT[:, k, :], **kw)
                last.then_inc(unit, 1)
            c.arrived(pe, IT_U)
            for n in range(4):
                project(n)
            pe.wait_ge(ev_act, 4)
            for n in range(8):
                i, s0 = n // 2, (n % 2) * 4
                for s in range(4):
                    last = nc.tensor.transpose(c.bank[(n + 4) % 8][0:NCH, s * P:(s + 1) * P],
                                               uT[:, i, s0 + s:TOK:CH], c.ident[:, :])
                last.then_inc(a_pe, 1)
            pe.wait_ge(a_ev, 8)
            for n, (g0, g1) in enumerate(((0, 12), (12, 24), (24, 32))):
                for g in range(g0, g1):
                    last = nc.tensor.transpose(c.bank[n][:, (g - g0) * NCH:(g - g0 + 1) * NCH],
                                               u40[:, g * P:(g + 1) * P], c.ident[0:NCH, 0:NCH])
                last.then_inc(b_pe, 1)
            pe.wait_ge(b_ev, 3)
            cols = [(r, j) for r in range(2) for j in range(PAIRS)]
            for n in range(3):
                for q, (r, j) in enumerate(cols[12 * n:12 * n + 12]):
                    for par in range(2):
                        last = nc.tensor.matmul(c.bank[3 + n][64 * par:64 * par + 64, q * NCH:(q + 1) * NCH],
                                                win[:, j, r, 64 * par:64 * par + 64], U[:, 2 * j + par, :],
                                                start=True, stop=True)
                last.then_inc(v_pe, 1)
            c.arrived(pe, IT_QKV)
            for n in range(4, 12):
                if n >= 9:
                    pe.wait_ge(v_ev, n - 8)
                project(n)
            pe.wait_ge(ev_act, 12)
            pe.wait_ge(swalk, 1)
            pe.wait_ge(ev["wuu_in"], 2 * 16 * CH)
            for n in range(8):
                j0, par = n // 2 * 4, n % 2
                rows = slice(64 * par, 64 * par + 64)
                if n >= 4:
                    pe.wait_ge(y_ev, n - 3)
                for q in range(4):
                    j = j0 + q
                    out = c.bank[n % 4][0:NCH, q * P:(q + 1) * P]
                    nc.tensor.matmul(out, U[:, 2 * j + par, :], wuu[:, 2 * j + par, :], start=True, stop=False)
                    nc.tensor.matmul(out, H[rows, 0, j, :], cp[rows, 0, j, GC:], start=False, stop=False)
                    last = nc.tensor.matmul(out, H[rows, 1, j, :], cp[rows, 1, j, GC:], start=False, stop=True)
                last.then_inc(y_pe, 1)
            for r in range(2):
                nc.tensor.transpose(c.bank[6][:, r * P:(r + 1) * P], fin[:, r].rearrange("p b j -> p (b j)"), c.ident[:, :])
            for r in range(2):
                last = nc.tensor.transpose(c.bank[6][0:PAIRS, (2 + r) * P:(3 + r) * P], h3[:, 0, r, :], c.ident[:, :])
            last.then_inc(f_pe, 1)
            pe.wait_ge(y_ev, 8)
            y40 = u40.rearrange("p (s m) -> p s m", s=CH)
            for i in range(4):
                for s in range(CH):
                    last = nc.tensor.transpose(c.bank[i][:, s:TOK:CH], y40[:, s, i * P:(i + 1) * P], c.ident[0:NCH, 0:NCH])
                last.then_inc(z_pe, 1)
            pe.wait_ge(g_ok, 4)
            c.arrived(pe, IT_GLU)
            for i in range(4):
                if i < 2:
                    bank = c.bank[4 + i]
                else:
                    bank = c.bank[i - 2]
                for k in range(4):
                    last = nc.tensor.matmul(bank[:, 0:TOK], glu[:, k, i * P:(i + 1) * P], ygT[:, k, :],
                                            start=(k == 0), stop=(k == 3))
                last.then_inc(o_pe, 1)
            c.keep_clock_up(c.bank[7], 3)

        @block.scalar
        def _(act):
            def evacuate(n):
                kind, i = units[n]
                act.wait_ge(unit, n + 1)
                ps = c.bank[unit_bank[n]]
                if kind == "kv":
                    ins = nc.scalar.copy(ev["kv"][0:ROWS[i], i, :], ps[0:ROWS[i], 0:2 * P])
                elif kind == "k":
                    ins = nc.scalar.copy(ev["kT"], ps[:, 0:TOK])
                elif kind == "u":
                    ins = nc.scalar.copy(uT[:, i, :], ps[:, 0:TOK])
                else:
                    nc.scalar.copy(ev["qS"].rearrange("p b (i s) -> p b i s", i=4)[:, :, i, :],
                                   ps[:, SEQ:TOK].rearrange("p (b s) -> p b s", b=NB))
                    ins = nc.scalar.copy(ev["qT"][:, i, :], ps[:, 0:TOK])
                ins.then_inc(ev_act, 1)
            for n in range(4):
                evacuate(n)
            for n in range(8):
                i, s0 = n // 2, (n % 2) * 4
                act.wait_ge(a_pe, n + 1)
                for s in range(4):
                    ins = nc.scalar.copy(ugrp(u40)[:, 8 * i:8 * i + 8, s0 + s, :],
                                         c.bank[(n + 4) % 8][0:NCH, s * P:(s + 1) * P].rearrange("p (g c) -> p g c", g=8))
                ins.then_inc(a_ev, 1)
            for n, (g0, g1) in enumerate(((0, 12), (12, 24), (24, 32))):
                act.wait_ge(b_pe, n + 1)
                nc.scalar.copy(U.rearrange("p g n -> p (g n)")[:, g0 * NCH:g1 * NCH],
                               c.bank[n][:, 0:(g1 - g0) * NCH]).then_inc(b_ev, 1)
            Vf = V.rearrange("p r j n -> p (r j n)")
            for n in range(3):
                m = (12, 12, 8)[n] * NCH
                act.wait_ge(v_pe, n + 1)
                nc.scalar.copy(Vf[:, 12 * NCH * n:12 * NCH * n + m], c.bank[3 + n][:, 0:m]).then_inc(v_ev, 1)
            for n in range(4, 12):
                evacuate(n)
            y40 = u40.rearrange("p (s g c) -> p g s c", s=CH, c=GC)
            for n in range(8):
                j0, par = n // 2 * 4, n % 2
                act.wait_ge(y_pe, n + 1)
                for q in range(4):
                    ins = nc.scalar.copy(y40[:, 2 * (j0 + q) + par],
                                         c.bank[n % 4][0:NCH, q * P:(q + 1) * P].rearrange("p (s c) -> p s c", s=CH))
                ins.then_inc(y_ev, 1)
            for i in range(4):
                act.wait_ge(z_ev, i + 1)
                nc.scalar.activation(ygT[:, i], yT[:, i], ACT.Gelu_apprx_tanh).then_inc(g_ok, 1)
            for i in range(4):
                act.wait_ge(o_pe, i + 1)
                bank = c.bank[4 + i] if i < 2 else c.bank[i - 2]
                nc.scalar.activation(obT[:, i], bank[:, 0:TOK], ACT.Sigmoid,
                                     bias=c.cols[:, COL_GLU_B + i:COL_GLU_B + i + 1]).then_inc(o_sg, 1)

        @block.vector
        def _(dve):
            v, link = nc.vector, Link(dve, own)
            pf = slice(0, PCH)
            v.memset(H[:, :, :, 0], 0.0)
            link(v.memset(h3[:, 0], 0.0))
            link(v.tensor_copy(H[:, :, :, PCH:NCH], state0.rearrange("p r b j -> p r j b")))
            dve.wait_ge(v_ev, 3)
            for n in range(PCH):
                a, b = h3[:, n % 2], h3[:, (n + 1) % 2]
                v.tensor_tensor(t1, l8[:, 0], a[:, 0:2], ALU.mult)
                link(v.tensor_tensor(t2, l8[:, 1], a[:, 1:3], ALU.mult))
                link(v.tensor_tensor(t1, t1, V[:, :, :, n], ALU.add))
                v.tensor_tensor(b[:, 0:2], t1, t2, ALU.add)
                link(v.tensor_tensor(b[:, 2], t1[:, 0], t2[:, 0], ALU.add))
                if n + 1 < PCH:
                    last = v.tensor_copy(H[:, :, :, n + 1], b[:, 0:2])
            s8 = [l8[:, q].unsqueeze(2).broadcast_to([P, 2, NB, PAIRS]) for q in range(2)]
            v.tensor_tensor(fin, s8[0], state0, ALU.mult)
            v.tensor_tensor(f1[:, 0], s8[1][:, 0], state0[:, 1], ALU.mult)
            link(v.tensor_tensor(f1[:, 1], s8[1][:, 1], state0[:, 0], ALU.mult))
            link(v.tensor_tensor(fin, fin, f1, ALU.add))
            v.tensor_tensor(fin, fin, V[:, :, :, PCH:NCH].rearrange("p r j b -> p r b j"), ALU.add).then_inc(swalk, 1)
            dve.wait_ge(f_pe, 1)
            so = st_out.rearrange("p (m r) -> p m r", r=2)
            po = ev["po"][0:PAIRS].rearrange("p (m r) -> p m r", r=2)
            for r in range(2):
                v.tensor_copy(so[:, :, r], c.bank[6][:, r * P:(r + 1) * P])
                last = v.tensor_copy(po[:, :, r], c.bank[6][0:PAIRS, (2 + r) * P:(3 + r) * P])
            last.then_inc(f_ok, 1)
            for i in range(4):
                dve.wait_ge(z_pe, i + 1)
                v.scalar_tensor_tensor(yT[:, i], uT[:, i], c.cols[:, COL_D + i:COL_D + i + 1], c.bank[i][:, 0:TOK],
                                       ALU.mult, ALU.add).then_inc(z_ev, 1)
            for i in range(4):
                dve.wait_ge(o_sg, i + 1)
                v.tensor_tensor(obT[:, i], obT[:, i], ygT[:, i], ALU.mult).then_inc(o_ok, 1)

        @block.gpsimd
        def _(pool):
            for g in (2, 1, 0):
                cache_copies(c, x, pool, g, range(NB), copies)
            pool.wait_ge(ev_act, 12)
            kv = ev["kv"]
            pool.dma_start(x["o_a_p"][0, 0].rearrange("w t h d -> w (t h d)"), kv[:, 1, :]).then_inc(out_a, 16)
            pool.dma_start(x["o_a_s"][0, :, P - NS:P].rearrange("b s t h d -> b s (t h d)"),
                           kv[0:NB * NS, 2, :]).then_inc(out_a, 16)
            for b in range(NB):
                pool.dma_start(x["o_a_s"][0, b, 0:P - NS].rearrange("s t h d -> s (t h d)"),
                               x["cache_a_kv"][0, b, NS:P].rearrange("s t h d -> s (t h d)")).then_inc(out_a, 16)
            pool.wait_ge(out_a, 16 * 10)

        @block.sync
        def _(sp):
            sp.wait_ge(ev["wuu_in"], 2 * 16 * CH)
            for b in range(NB):
                sp.dma_start(ev["kvc"][:, b, :], x["cache_a_kv"][0, b].rearrange("w t h d -> w (t h d)")).then_inc(pre, 16)
            sp.wait_ge(unit, 4)
            c.load_item(sp, IT_U + RING)
            sp.wait_ge(unit, 12)
            c.load_item(sp, IT_QKV + RING)
            sp.wait_ge(f_ok, 1)
            sp.dma_start(x["o_b_s"][0].rearrange("b (j g) n r -> b j (g n r)", g=2).rearrange("b j m -> (b j) m"),
                         st_out).then_inc(f_out, 16)
            sp.dma_start(x["o_b_p"][0, 0].rearrange("(j g) n r -> j (g n r)", g=2), ev["po"][0:PAIRS]).then_inc(f_out, 16)
            sp.wait_ge(o_ok, 4)
            c.load_item(sp, IT_GLU + RING)
            sp.wait_ge(f_out, 32)
    c.recycle()


def softmax_stats(v, dve, link, S, m, nm, sm, sink, arg_ok):
    link(v.tensor_reduce(m, S, AX.X, ALU.max))
    link(v.tensor_tensor(m, m, sink, ALU.max))
    v.tensor_scalar(nm, m, -1.0, None, ALU.mult)
    v.tensor_tensor(sm, sink, m, ALU.subtract).then_inc(arg_ok, 1)


def attn_a_block(c, x, ev):
    nc = c.nc
    qT, kT, kv, qS, oaT, kvc, bias = (ev[n] for n in ("qT", "kT", "kv", "qS", "oaT", "kvc", "bias"))
    ar = Carve(c.arena, ev["end"], ev["after_s5"])
    SK = P + 32
    S = {"s": ar.take(2, 2, SK), "0": ar.take(A_H, P), "1": ar.take(A_H, 2 * P)}
    PT = {"s": ar.take(4, P), "0": ar.take(A_H, P), "1": ar.take(A_H, 2, P)}
    PTn = ar.take(4, P)[0:NB * NS]
    kcT = ar.take(NB, P)
    bs = ev["bs"]
    sinks, sinks_s = ar.take(A_H), ar.take(2, 2)
    st = {k: ar.take(4, 8) for k in "s01"}
    kvs = "s01"
    pre, ld, kc_pe, kc_ok = ev["pre"], c.sem("aa_load"), c.sem("aa_pe_kc"), c.sem("aa_kc")
    sc_pe = {k: c.sem(f"aa_pe_scores_{k}") for k in kvs}
    arg_ok = {k: c.sem(f"aa_arg_{k}") for k in kvs}
    ex_ok = {k: c.sem(f"aa_exp_{k}") for k in kvs}
    p_ok = {k: c.sem(f"aa_probs_{k}") for k in kvs}
    t_pe = {k: c.sem(f"aa_pe_turned_{k}") for k in kvs}
    t_ok = {k: c.sem(f"aa_turned_{k}") for k in kvs}
    o_pe = {k: c.sem(f"aa_pe_out_{k}") for k in kvs}
    own, z_ok = c.sem("aa_own"), c.sem("aa_zero")
    NH = {"s": 4, "0": 8, "1": 8}

    with nc.Block() as block:
        @block.sync
        def _(sp):
            sp.dma_start(sinks, bass.AP(tensor=x["sinks_a"].tensor, offset=0, ap=[[0, P], [1, A_H]])).then_inc(ld, 16)
            for b in range(4):
                for kvh in range(2):
                    sp.dma_start(sinks_s[32 * b:32 * b + 32, kvh, 0:1],
                                 bass.AP(tensor=x["sinks_a"].tensor, offset=4 * kvh,
                                         ap=[[1, 4], [0, NS], [1, 1]])).then_inc(ld, 16)

        @block.tensor
        def _(pe):
            pe.wait_ge(pre, 16 * 8)
            for b in range(NB):
                last = nc.tensor.transpose(c.bank[b // 4][:, (b % 4) * P:(b % 4 + 1) * P], kvc[:, b, 0:P], c.ident[:, :])
            last.then_inc(kc_pe, 1)
            for h in range(A_H):
                rows = slice(64 * (h // 4), 64 * (h // 4) + 64)
                last = nc.tensor.matmul(c.bank[6 + h // 4][:, (h % 4) * P:(h % 4 + 1) * P], qT[rows, h % 4, 0:P],
                                        kT[rows, 0:P], start=True, stop=True)
            last.then_inc(sc_pe["0"], 1)
            pe.wait_ge(kc_ok, 2)
            for half in range(2):
                for kvh in range(2):
                    rows = slice(64 * kvh, 64 * kvh + 64)
                    for b in range(4):
                        lhs = qS[rows, 4 * half + b, :]
                        out = c.bank[4 + kvh][32 * b:32 * b + 32, half * SK:(half + 1) * SK]
                        nc.tensor.matmul(out[:, 0:P], lhs, kcT[rows, 4 * half + b, :], start=True, stop=True)
                        last = nc.tensor.matmul(out[:, P:SK], lhs, kT[rows, SEQ + 32 * half:SEQ + 32 * half + 32],
                                                start=True, stop=True)
            last.then_inc(sc_pe["s"], 1)
            for h in range(A_H):
                rows = slice(64 * (h // 4), 64 * (h // 4) + 64)
                last = nc.tensor.matmul(c.bank[h // 2][:, (h % 2) * 2 * P:(h % 2 + 1) * 2 * P], qT[rows, h % 4, P:2 * P],
                                        kT[rows, 0:2 * P], start=True, stop=True)
            last.then_inc(sc_pe["1"], 1)
            pe.wait_ge(p_ok["0"], 1)
            for h in range(A_H):
                last = nc.tensor.transpose(c.bank[6 + h // 4][:, (h % 4) * P:(h % 4 + 1) * P], S["0"][:, h, :], c.ident[:, :])
            last.then_inc(t_pe["0"], 1)
            pe.wait_ge(p_ok["s"], 1)
            for n in range(4):
                nc.tensor.transpose(c.bank[4][:, n * P:(n + 1) * P], S["s"][:, n // 2, n % 2, 0:P], c.ident[:, :])
                last = nc.tensor.transpose(c.bank[5][0:32, n * P:(n + 1) * P], S["s"][:, n // 2, n % 2, P:SK], c.ident[:, :])
            last.then_inc(t_pe["s"], 1)
            pe.wait_ge(t_ok["0"], 2)
            for h in range(A_H):
                v_cols = slice(P + 64 * (h // 4), P + 64 * (h // 4) + 64)
                last = nc.tensor.matmul(c.bank[6][64 * (h % 2):64 * (h % 2) + 64, (h // 2) * P:(h // 2 + 1) * P],
                                        kv[:, 0, v_cols], PT["0"][:, h, :], start=True, stop=True)
            last.then_inc(o_pe["0"], 1)
            pe.wait_ge(p_ok["1"], 1)
            for h in range(A_H):
                for kb in range(2):
                    n = 2 * h + kb
                    last = nc.tensor.transpose(c.bank[n // 4][:, (n % 4) * P:(n % 4 + 1) * P],
                                               S["1"][:, h, kb * P:(kb + 1) * P], c.ident[:, :])
            last.then_inc(t_pe["1"], 1)
            pe.wait_ge(t_ok["s"], 2)
            pe.wait_ge(z_ok, 1)
            for kvh in range(2):
                for half in range(2):
                    n = 2 * kvh + half
                    for b in range(4):
                        for par in range(2):
                            out = c.bank[7][64 * par:64 * par + 64, :].rearrange("p (i t) -> p i t", t=P)[
                                :, 2 * kvh:2 * kvh + 2, 32 * half + 8 * b:32 * half + 8 * b + 8]
                            sel = lambda ap: ap.rearrange("p (i s) -> p i s", s=NS)[:, par::2, :]
                            v_cols = slice(P + 64 * kvh, P + 64 * kvh + 64)
                            nc.tensor.matmul(out, kvc[:, 4 * half + b, v_cols], sel(PT["s"][:, n, 32 * b:32 * b + 32]),
                                             start=True, stop=False)
                            last = nc.tensor.matmul(out, kv[0:64, 2, v_cols], sel(PTn[:, n, 32 * b:32 * b + 32]),
                                                    start=False, stop=True)
            last.then_inc(o_pe["s"], 1)
            pe.wait_ge(t_ok["1"], 4)
            for h in range(A_H):
                v_cols = slice(P + 64 * (h // 4), P + 64 * (h // 4) + 64)
                out = c.bank[0][64 * (h % 2):64 * (h % 2) + 64, (h // 2) * P:(h // 2 + 1) * P]
                for kb in range(2):
                    last = nc.tensor.matmul(out, kv[:, kb, v_cols], PT["1"][:, h, kb, :], start=(kb == 0), stop=(kb == 1))
            last.then_inc(o_pe["1"], 1)

        @block.scalar
        def _(act):
            for q in range(2):
                act.wait_ge(kc_pe, 1)
                nc.scalar.copy(kcT[:, 4 * q:4 * q + 4, :].rearrange("p b k -> p (b k)"), c.bank[q][:, :]).then_inc(kc_ok, 1)

            def exps(k, rows_of):
                act.wait_ge(arg_ok[k], 1)
                for n in range(NH[k]):
                    nc.scalar.activation(rows_of(n), rows_of(n), ACT.Exp, bias=st[k][:, 1, n:n + 1],
                                         accum_out=st[k][:, 3, n:n + 1])
                nc.scalar.activation(st[k][:, 2, 0:NH[k]], st[k][:, 2, 0:NH[k]], ACT.Exp).then_inc(ex_ok[k], 1)
            exps("0", lambda n: S["0"][:, n, :])
            exps("s", lambda n: S["s"][:, n // 2, n % 2, :])
            exps("1", lambda n: S["1"][:, n, :])
            act.wait_ge(t_pe["0"], 1)
            for q in range(2):
                nc.scalar.copy(PT["0"][:, 4 * q:4 * q + 4, :].rearrange("p h k -> p (h k)"), c.bank[6 + q][:, :])\
                    .then_inc(t_ok["0"], 1)
            act.wait_ge(o_pe["0"], 1)
            nc.scalar.copy(oaT[:, :, 0:P], c.bank[6][:, :].rearrange("p (i t) -> p i t", i=4))
            act.wait_ge(t_pe["1"], 1)
            for q in range(4):
                nc.scalar.copy(PT["1"][:, 2 * q:2 * q + 2, :, :].rearrange("p h b k -> p (h b k)"), c.bank[q][:, :])\
                    .then_inc(t_ok["1"], 1)
            act.wait_ge(o_pe["1"], 1)
            nc.scalar.copy(oaT[:, :, P:2 * P], c.bank[0][:, :].rearrange("p (i t) -> p i t", i=4))

        @block.vector
        def _(dve):
            v, link = nc.vector, Link(dve, own)
            v.memset(PTn, 0.0).then_inc(z_ok, 1)
            dve.wait_ge(pre, 16 * 8)
            dve.wait_ge(ld, 16 * 9)
            dve.wait_ge(sc_pe["0"], 1)
            for q in range(2):
                ins = v.scalar_tensor_tensor(S["0"][:, 4 * q:4 * q + 4, :], c.bank[6 + q][:, :].rearrange("p (h k) -> p h k", h=4),
                                             SCALE, bias[:, 4 * q:4 * q + 4, P:2 * P], ALU.mult, ALU.add)
            link(ins)
            softmax_stats(v, dve, link, S["0"], st["0"][:, 0], st["0"][:, 1], st["0"][:, 2], sinks, arg_ok["0"])
            dve.wait_ge(sc_pe["s"], 1)
            for kvh in range(2):
                ins = v.scalar_tensor_tensor(S["s"][:, kvh], c.bank[4 + kvh][:, 0:2 * SK].rearrange("p (h k) -> p h k", h=2),
                                             SCALE, bs[:, kvh].unsqueeze(1).broadcast_to([P, 2, SK]), ALU.mult, ALU.add)
            link(ins)
            softmax_stats(v, dve, link, S["s"], st["s"][:, 0, 0:4].rearrange("p (a b) -> p a b", a=2),
                          st["s"][:, 1, 0:4].rearrange("p (a b) -> p a b", a=2),
                          st["s"][:, 2, 0:4].rearrange("p (a b) -> p a b", a=2),
                          sinks_s[:, :, 0:1].broadcast_to([P, 2, 2]), arg_ok["s"])
            dve.wait_ge(sc_pe["1"], 1)
            for q in range(4):
                ins = v.scalar_tensor_tensor(S["1"][:, 2 * q:2 * q + 2, :], c.bank[q][:, :].rearrange("p (h k) -> p h k", h=2),
                                             SCALE, bias[:, 2 * q:2 * q + 2, :], ALU.mult, ALU.add)
            link(ins)
            softmax_stats(v, dve, link, S["1"], st["1"][:, 0], st["1"][:, 1], st["1"][:, 2], sinks, arg_ok["1"])

            def normalise(k, view, shape):
                dve.wait_ge(ex_ok[k], 1)
                n = NH[k]
                link(v.tensor_tensor(st[k][:, 3, 0:n], st[k][:, 3, 0:n], st[k][:, 2, 0:n], ALU.add))
                link(v.reciprocal(st[k][:, 3, 0:n], st[k][:, 3, 0:n]))
                v.tensor_tensor(view, view, st[k][:, 3, 0:n].unsqueeze(2).broadcast_to(shape), ALU.mult).then_inc(p_ok[k], 1)
            normalise("0", S["0"], [P, 8, P])
            normalise("s", S["s"].rearrange("p a b k -> p (a b) k"), [P, 4, SK])
            normalise("1", S["1"], [P, 8, 2 * P])
            dve.wait_ge(t_pe["s"], 1)
            v.tensor_copy(PT["s"].rearrange("p n k -> p (n k)"), c.bank[4][:, :]).then_inc(t_ok["s"], 1)
            dve.wait_ge(z_ok, 1)
            for half in range(2):
                ins = v.tensor_copy(PTn[32 * half:32 * half + 32].rearrange("p (k h) m -> p k h m", h=2)[:, :, half, :],
                                    c.bank[5][0:32, :].rearrange("p (k h m) -> p k h m", k=2, h=2)[:, :, half, :])
            ins.then_inc(t_ok["s"], 1)
            dve.wait_ge(o_pe["s"], 1)
            v.tensor_copy(oaT[:, :, SEQ:TOK], c.bank[7][:, :].rearrange("p (i t) -> p i t", i=4)[:, :, 0:64])
    c.recycle()


def out_norm_steps(c, block, name, parts, items, gain, xn, wr):
    nc = c.nc
    done, added = c.sem(name + "_pe"), c.sem(name + "_added")
    sq_ok, ms_ok, rstd_ok = c.sem(name + "_sq"), c.sem(name + "_ms"), c.sem(name + "_rstd")
    xn_ok, pe_t, own, turned = c.sem(name + "_xn"), c.sem(name + "_pe_t"), c.sem(name + "_own"), c.sem(name + "_turned")
    lg_pe = c.sem(name + "_pe_logits")
    n_parts = len(parts)
    where = {}
    for item, k0, n in items:
        w = c.slot(item)[:, 0:n * D].rearrange("p (k n) -> p k n", k=n)
        for k in range(n):
            where[k0 + k] = w[:, k, :]

    @block.tensor
    def _(pe):
        def project(t):
            for h in range(2):
                for k in range(n_parts):
                    last = nc.tensor.matmul(c.bank[2 * t + h][0:ROWS[t], :], parts[k][:, t * P:t * P + ROWS[t]],
                                            where[k][:, h * 512:(h + 1) * 512], start=(k == 0), stop=(k == n_parts - 1))
                last.then_inc(done, 1)

        def turn(t):
            rows = ROWS[t]
            pe.wait_ge(xn_ok, t + 1)
            for h in range(2):
                for k in range(4):
                    last = nc.tensor.transpose(c.bank[2 * t + h][:, k * rows:(k + 1) * rows],
                                               xn[0:rows, t, 4 * h + k:D:KC], c.ident[0:rows, 0:rows])
                last.then_inc(pe_t, 1)

        def logits(t):
            pe.wait_ge(turned, 2 * t + 2)
            for q in range(KC):
                last = nc.tensor.matmul(c.bank[6][0:ROWS[t], 32 * t:32 * t + 20], c.xnT[:, q, t * P:t * P + ROWS[t]],
                                        wr[0][:, q, :], start=(q == 0), stop=(q == KC - 1))
            last.then_inc(lg_pe, 1)
        for item, _, _ in items:
            c.arrived(pe, item)
        project(0)
        project(1)
        pe.wait_ge(wr[1], wr[2])
        turn(0)
        logits(0)
        project(2)
        turn(1)
        logits(1)
        turn(2)
        logits(2)

    @block.scalar
    def _(act):
        for t, rows in enumerate(ROWS):
            act.wait_ge(added, 2 * t + 2)
            nc.scalar.activation(xn[0:rows, t], c.resid[0:rows, t], ACT.Square,
                                 accum_out=c.stat[0:rows, t:t + 1]).then_inc(sq_ok, 1)
            act.wait_ge(ms_ok, t + 1)
            nc.scalar.activation(c.stat[:, 6 + t:7 + t], c.stat[:, 3 + t:4 + t], ACT.Sqrt).then_inc(rstd_ok, 1)

    @block.vector
    def _(dve):
        v, link = nc.vector, Link(dve, own)

        def add(t):
            for h in range(2):
                dve.wait_ge(done, 2 * t + h + 1)
                r = c.resid[0:ROWS[t], t, h * 512:(h + 1) * 512]
                v.tensor_tensor(r, c.bank[2 * t + h][0:ROWS[t], :], r, ALU.add).then_inc(added, 1)

        def normalise(t):
            dve.wait_ge(sq_ok, t + 1)
            link(v.tensor_scalar(c.stat[:, 3 + t:4 + t], c.stat[:, t:t + 1], 1.0 / D, EPS, ALU.mult, ALU.add))
            v.reciprocal(c.stat[:, 3 + t:4 + t], c.stat[:, 3 + t:4 + t]).then_inc(ms_ok, 1)
            dve.wait_ge(rstd_ok, t + 1)
            v.tensor_scalar(xn[0:ROWS[t], t], c.resid[0:ROWS[t], t], c.stat[0:ROWS[t], 6 + t:7 + t], None,
                            ALU.mult).then_inc(xn_ok, 1)

        def apply_gain(t):
            rows = ROWS[t]
            for h in range(2):
                dve.wait_ge(pe_t, 2 * t + h + 1)
                v.tensor_tensor(c.xnT[:, 4 * h:4 * h + 4, t * P:t * P + rows],
                                c.bank[2 * t + h][:, 0:4 * rows].rearrange("p (k r) -> p k r", k=4),
                                c.gains[:, gain, 4 * h:4 * h + 4].unsqueeze(2).broadcast_to([P, 4, rows]), ALU.mult)\
                    .then_inc(turned, 1)
        add(0)
        normalise(0)
        add(1)
        apply_gain(0)
        normalise(1)
        add(2)
        apply_gain(1)
        normalise(2)
        apply_gain(2)

    return xn_ok, lg_pe, done




PAIR_ROWS = 2 * TOK
SKIP = 1.0e6


def route_consts():
    k = np.zeros((P, 3 * P + 4), np.float32)
    k[:, 0:P] = np.arange(P)[None, :]
    k[:, P:2 * P] = np.arange(P)[:, None] < np.arange(P)[None, :]
    k[:, 2 * P:3 * P] = 1.0
    for t in range(3):
        k[:, 3 * P + t] = t * P + np.arange(P)
    return k


ROUTER_LOADS = 5 * 16


def moe_arena(c):
    ar = Carve(c.arena, c.AR)
    t = {"k": ar.take(3 * P + 4), "xn": ar.take(3, D), "wr": ar.take(KC, 20), "rb": ar.take(20), "lg": ar.take(3, 20),
         "S_room": ar.take(3 * 2 * D), "R_room": ar.take(3 * E_N * 2), "idx": ar.take(2, E_N), "xg": ar.take(3, D),
         "xgT": ar.take(2, KC, CAP), "sg": ar.take(2, FF), "hid": ar.take(2, FF), "hidT": ar.take(2, 2, P),
         "yo": ar.take(3, D), "gmax": ar.take(3, 8), "g8": ar.take(3, 8), "gi": ar.take(3, 8), "e8": ar.take(3, 8),
         "emax": ar.take(3, 8), "ei": ar.take(3, 8), "ge": ar.take(3, 4), "gs": ar.take(3), "gidx": ar.take(3),
         "oh": ar.take(3, 4), "pick": ar.take(3, 4, 4), "q": ar.take(3), "r": ar.take(3), "w": ar.take(2, 3),
         "eid": ar.take(2, 3), "sel": ar.take(2, 3, E_N), "sum_room": ar.take(3 * E_N // 2), "tri_room": ar.take(P), "pos": ar.take(3, E_N),
         "tmp": ar.take(3, E_N), "pk": ar.take(2, 3), "ok": ar.take(2, 3), "gov": ar.take(3, E_N), "cnt": ar.take(1),
         "zero": ar.take(E_N), "off": ar.take(2, E_N)}
    t["yp"] = t["S_room"].rearrange("p (t m) -> p t m", t=3)
    t["S"] = t["S_room"][:, 0:3 * E_N * CAP // 2].bitcast(BF16).rearrange("p (t e s) -> p t e s", t=3, e=E_N)
    t["sum"] = t["sum_room"].bitcast(BF16).rearrange("p (t e) -> p t e", t=3)
    t["tri"] = t["tri_room"].bitcast(BF16)
    t["R"] = t["R_room"].bitcast(BF16).rearrange("p (t e q) -> p t e q", t=3, e=E_N)
    assert ar.at <= c.AR - SLOT, ar.at
    t["wov"] = c.arena[:, c.AR - SLOT:c.AR]
    return t


def route_steps(c, block, x, layer, m, ld, xn_ok, lg_pe, done, freed):
    nc = c.nc
    n = f"r{layer}_"
    rows_out = c.sem(n + "rows_out")
    own, earg, eok = c.sem(n + "own"), c.sem(n + "exp_arg"), c.sem(n + "exp")
    sel_ok, pos_pe, S_ok, idx_pe = c.sem(n + "sel"), c.sem(n + "pe_pos"), c.sem(n + "onehot"), c.sem(n + "pe_idx")
    k = m["k"]
    iota, tri, ones = k[:, 0:P], m["tri"][:, 0:P], m["tri"][:, P:2 * P]
    tri_ok = c.sem(n + "tri")

    @block.sync
    def _(sp):
        sp.dma_start(k, x["route_consts"]).then_inc(ld, 16)
        sp.dma_start(m["wr"][:, :, 0:4], x["moe_router_g"][layer].rearrange("(p k) g -> p k g", k=KC)).then_inc(ld, 16)
        sp.dma_start(m["wr"][:, :, 4:20], x["moe_router_e"][layer].rearrange("(p k) g -> p k g", k=KC)).then_inc(ld, 16)
        sp.dma_start(m["rb"][:, 0:4], bass.AP(tensor=x["moe_router_g_b"].tensor, offset=4 * layer, ap=[[0, P], [1, 4]])).then_inc(ld, 16)
        sp.dma_start(m["rb"][:, 4:20], bass.AP(tensor=x["moe_router_e_b"].tensor, offset=E_N * layer, ap=[[0, P], [1, E_N]])).then_inc(ld, 16)
        for t, rows in enumerate(ROWS):
            sp.wait_ge(xn_ok, t + 1)
            sp.dma_start(x["x_rows"][t * P:t * P + rows, :], m["xn"][0:rows, t]).then_inc(rows_out, 16)
        sp.wait_ge(done, 6)
        for item in freed:
            c.load_item(sp, item + RING)
        sp.wait_ge(rows_out, 48)

    @block.gpsimd
    def _(pool):
        nc.gpsimd.memset(m["xg"], 0.0)

    @block.tensor
    def _(pe):
        pe.wait_ge(tri_ok, 1)
        pe.wait_ge(sel_ok, 1)
        for t in range(3):
            for s in range(t + 1):
                nc.tensor.matmul(c.bank[7][:, 16 * t:16 * t + 16], tri if s == t else ones, m["sum"][:, s, :],
                                 start=(s == 0), stop=(s == t))
        for s in range(3):
            last = nc.tensor.matmul(c.bank[7][:, 64:80], ones, m["sum"][:, s, :], start=(s == 0), stop=(s == 2))
        last.then_inc(pos_pe, 1)
        for e in range(E_N):
            if e == 0:
                pe.wait_ge(S_ok, 3)
            for t in range(3):
                last = nc.tensor.matmul(c.bank[5][0:CAP, 4 * e:4 * e + 4], m["S"][:, t, e, :], m["R"][:, t, e, :],
                                        start=(t == 0), stop=(t == 2))
        last.then_inc(idx_pe, 1)

    @block.scalar
    def _(act):
        act.wait_ge(earg, 1)
        nc.scalar.activation(m["ge"], m["ge"], ACT.Exp).then_inc(eok, 1)
        act.wait_ge(earg, 2)
        nc.scalar.activation(m["q"], m["q"], ACT.Exp).then_inc(eok, 1)

    @block.vector
    def _(dve):
        v, link = nc.vector, Link(dve, own)
        dve.wait_ge(ld, ROUTER_LOADS)
        v.tensor_copy(m["tri"], k[:, P:3 * P]).then_inc(tri_ok, 1)
        v.memset(m["g8"], -3e38)
        v.memset(m["e8"], -3e38)
        link(v.memset(m["lg"], 0.0))
        dve.wait_ge(lg_pe, 3)
        for t, rows in enumerate(ROWS):
            ins = v.tensor_tensor(m["lg"][0:rows, t], c.bank[6][0:rows, 32 * t:32 * t + 20], m["rb"][0:rows], ALU.add)
        link(ins)
        link(v.tensor_copy(m["g8"][:, :, 0:4], m["lg"][:, :, 0:4]))
        for t in range(3):
            ins = v.max(m["gmax"][:, t], m["g8"][:, t])
        link(ins)
        for t in range(3):
            ins = v.max_index(m["gi"].bitcast(U32)[:, t], m["gmax"][:, t], m["g8"][:, t])
        link(ins)
        v.tensor_tensor(m["ge"], m["lg"][:, :, 0:4], m["gmax"][:, :, 0:1].broadcast_to([P, 3, 4]), ALU.subtract)\
            .then_inc(earg, 1)
        link(v.tensor_copy(m["gidx"], m["gi"].bitcast(U32)[:, :, 0]))
        link(v.tensor_tensor(m["oh"], iota[:, 0:4].unsqueeze(1).broadcast_to([P, 3, 4]),
                             m["gidx"].unsqueeze(2).broadcast_to([P, 3, 4]), ALU.is_equal))
        link(v.tensor_tensor(m["pick"], m["lg"][:, :, 4:20].rearrange("p t (g e) -> p t e g", g=4),
                             m["oh"].unsqueeze(2).broadcast_to([P, 3, 4, 4]), ALU.mult))
        link(v.tensor_reduce(m["e8"][:, :, 0:4], m["pick"], AX.X, ALU.add))
        for t in range(3):
            ins = v.max(m["emax"][:, t], m["e8"][:, t])
        link(ins)
        for t in range(3):
            ins = v.max_index(m["ei"].bitcast(U32)[:, t], m["emax"][:, t], m["e8"][:, t])
        link(ins)
        v.tensor_tensor(m["q"], m["emax"][:, :, 1], m["emax"][:, :, 0], ALU.subtract).then_inc(earg, 1)
        for q in range(2):
            ins = v.tensor_copy(m["eid"][:, q], m["ei"].bitcast(U32)[:, :, q])
        link(ins)
        for q in range(2):
            ins = v.scalar_tensor_tensor(m["eid"][:, q], m["gidx"], 4.0, m["eid"][:, q], ALU.mult, ALU.add)
        link(ins)
        for q in range(2):
            ins = v.tensor_tensor(m["sel"][:, q], iota[:, 0:E_N].unsqueeze(1).broadcast_to([P, 3, E_N]),
                                  m["eid"][:, q].unsqueeze(2).broadcast_to([P, 3, E_N]), ALU.is_equal)
        link(ins)
        link(v.memset(m["sel"][64:P, :, 2, :], 0.0))
        v.tensor_tensor(m["sum"], m["sel"][:, 0], m["sel"][:, 1], ALU.add).then_inc(sel_ok, 1)
        dve.wait_ge(eok, 2)
        link(v.tensor_reduce(m["gs"], m["ge"], AX.X, ALU.add))
        v.reciprocal(m["gs"], m["gs"])
        link(v.tensor_scalar(m["r"], m["q"], 1.0, None, ALU.add))
        link(v.reciprocal(m["r"], m["r"]))
        link(v.tensor_tensor(m["w"][:, 0], m["r"], m["gs"], ALU.mult))
        link(v.tensor_tensor(m["w"][:, 1], m["w"][:, 0], m["q"], ALU.mult))
        v.tensor_copy(m["R"][:, :, :, 0], k[:, 3 * P:3 * P + 1].unsqueeze(2).broadcast_to([P, 3, E_N]))
        for t in range(3):
            v.memset(m["R"][:, t, :, 1], float(t))
        v.memset(m["R"][:, :, :, 3], 1.0)
        link(v.tensor_copy(m["R"][:, :, :, 2], m["sel"][:, 1]))
        dve.wait_ge(pos_pe, 1)
        link(v.tensor_copy(m["pos"], c.bank[7][:, 0:48].rearrange("p (t e) -> p t e", t=3)))
        link(v.scalar_tensor_tensor(m["tmp"], m["pos"], 1.0, m["sum"], ALU.add, ALU.mult))
        link(v.tensor_scalar(m["tmp"], m["tmp"], -1.0, None, ALU.add))
        for t in range(3):
            v.tensor_tensor(m["S"][:, t], iota[:, 0:CAP].unsqueeze(1).broadcast_to([P, E_N, CAP]),
                            m["tmp"][:, t].unsqueeze(2).broadcast_to([P, E_N, CAP]), ALU.is_equal).then_inc(S_ok, 1)
        dve.wait_ge(S_ok, 3)
        for q in range(2):
            link(v.tensor_tensor(m["tmp"], m["sel"][:, q], m["pos"], ALU.mult))
            link(v.tensor_reduce(m["pk"][:, q], m["tmp"], AX.X, ALU.add))
        link(v.tensor_scalar(m["ok"], m["pk"], float(CAP), None, ALU.is_lt))
        link(v.tensor_tensor(m["ok"], m["ok"], m["w"], ALU.mult))
        link(v.tensor_tensor(m["pk"], m["w"], m["ok"], ALU.subtract))
        link(v.tensor_tensor(m["gov"], m["sel"][:, 0], m["pk"][:, 0].unsqueeze(2).broadcast_to([P, 3, E_N]), ALU.mult))
        link(v.tensor_tensor(m["tmp"], m["sel"][:, 1], m["pk"][:, 1].unsqueeze(2).broadcast_to([P, 3, E_N]), ALU.mult))
        link(v.tensor_tensor(m["gov"], m["gov"], m["tmp"], ALU.add))
        link(v.tensor_reduce(m["gs"][:, 0:1], c.bank[7][:, 64:80], AX.X, ALU.max))
        link(v.tensor_scalar(m["gs"][:, 0:1], m["gs"][:, 0:1], float(CAP), 0.0, ALU.subtract, ALU.max))
        link(v.tensor_copy(m["cnt"].bitcast(I32), m["gs"][:, 0:1]))
        dve.wait_ge(idx_pe, 1)
        ps = c.bank[5][0:CAP, 0:4 * E_N].rearrange("p (e q) -> p q e", q=4)
        off, row = m["off"][0:CAP], m["zero"][0:CAP]
        v.tensor_scalar(off[:, 0], ps[:, 3], 0.0, SKIP, ALU.is_equal, ALU.mult)
        link(v.tensor_copy(row, ps[:, 0]))
        link(v.scalar_tensor_tensor(row, ps[:, 1], float(P), row, ALU.mult, ALU.add))
        link(v.scalar_tensor_tensor(off[:, 1], row, 2.0, off[:, 0], ALU.mult, ALU.add))
        link(v.tensor_tensor(off[:, 1], off[:, 1], ps[:, 2], ALU.add))
        link(v.tensor_tensor(off[:, 0], off[:, 0], row, ALU.add))
        link(v.tensor_copy(m["idx"].bitcast(U32)[0:CAP], off))
    

def experts_block(c, x, layer, m, item0):
    nc = c.nc
    n = f"x{layer}_"
    xg_in, y_out = c.xg_in, c.y_out
    base = [16 * layer * len(range(i, E_N, 3)) for i in range(3)]
    xt_pe, xt_ok = c.sem(n + "pe_xT"), c.sem(n + "xT")
    gate_pe, up_pe, sg_ok, hid_ok = c.sem(n + "pe_gate"), c.sem(n + "pe_up"), c.sem(n + "silu"), c.sem(n + "hidden")
    dn_pe, yo_a, yo_b = c.sem(n + "pe_down"), c.sem(n + "yo_lo"), c.sem(n + "yo_hi")
    yp_in, own = [c.sem(f"{n}rows_in{t}") for t in range(3)], c.sem(n + "own")
    gather_idx, scatter_idx = m["idx"].bitcast(U32)[0:CAP, 0], m["idx"].bitcast(U32)[0:CAP, 1]
    xg, xgT, yo = m["xg"], m["xgT"], m["yo"]
    sg = [m["sg"][:, b, 0:2 * CAP] for b in range(2)]
    hidT = [m["hid"][:, b, 0:2 * CAP] for b in range(2)]
    with nc.Block() as block:
        @block.gpsimd
        def _(pool):
            def scatter(e):
                pool.wait_ge(yo_a, e + 1)
                pool.wait_ge(yo_b, e + 1)
                pool.indirect_dma_start(out=x["y_rows"], out_offset=bass.IndirectOffsetOnAxis(ap=scatter_idx[:, e:e + 1], axis=0),
                                        in_=yo[0:CAP, e % 3], in_offset=None, bounds_check=PAIR_ROWS - 1,
                                        oob_is_err=False).then_inc(y_out[e % 3], 16)
            for e in range(E_N):
                if e >= 3:
                    pool.wait_ge(xt_pe, e - 2)
                pool.indirect_dma_start(out=xg[0:CAP, e % 3], out_offset=None, in_=x["x_rows"],
                                        in_offset=bass.IndirectOffsetOnAxis(ap=gather_idx[:, e:e + 1], axis=0),
                                        bounds_check=TOK - 1, oob_is_err=False).then_inc(xg_in[e % 3], 16)
                if e >= 3:
                    scatter(e - 3)
            for e in range(E_N - 3, E_N):
                scatter(e)

        @block.sync
        def _(sp):
            for e in range(E_N - 1):
                sp.wait_ge(dn_pe, e + 1)
                c.load_item(sp, item0 + e + RING)
            for i in range(3):
                sp.wait_ge(y_out[i], base[i] + 16 * len(range(i, E_N, 3)))
            for t, rows in enumerate(ROWS):
                sp.dma_start(m["yp"][0:rows, t], x["y_rows"].rearrange("(t two) d -> t (two d)", two=2)
                             [t * P:t * P + rows, :]).then_inc(yp_in[t], 16)
            c.load_item(sp, item0 + E_N - 1 + RING)

        @block.tensor
        def _(pe):
            def turn(e):
                pe.wait_ge(xg_in[e % 3], base[e % 3] + 16 * (e // 3 + 1))
                if e >= 1:
                    pe.wait_ge(xt_ok, 2 * e)
                for q in range(KC):
                    last = nc.tensor.transpose(c.bank[q // 4][:, (q % 4) * CAP:(q % 4 + 1) * CAP], xg[0:CAP, e % 3, q:D:KC],
                                               c.ident[0:CAP, 0:CAP])
                last.then_inc(xt_pe, 1)

            def up(e):
                w = c.slot(item0 + e)[:, 0:KC * 2 * FF].rearrange("p (k n) -> p k n", k=KC)
                c.arrived(pe, item0 + e)
                pe.wait_ge(xt_ok, 2 * e + 2)
                for j in range(4):
                    for q in range(KC):
                        last = nc.tensor.matmul(c.bank[2 + j // 2][:, j % 2 * CAP:(j % 2 + 1) * CAP], w[:, q, j * P:(j + 1) * P],
                                                xgT[:, e % 2, q, :], start=(q == 0), stop=(q == KC - 1))
                    if j == 1:
                        last.then_inc(gate_pe, 1)
                last.then_inc(up_pe, 1)

            def down(e):
                w = c.slot(item0 + e)[:, KC * 2 * FF:SLOT].rearrange("p (k n) -> p k n", k=2)
                pe.wait_ge(hid_ok, e + 1)
                if e >= 2:
                    pe.wait_ge(yo_a, e - 1)
                    pe.wait_ge(yo_b, e - 1)
                for h in range(2):
                    for q in range(2):
                        last = nc.tensor.matmul(c.bank[4 + 2 * (e % 2) + h][0:CAP, :], hidT[e % 2][:, q * CAP:(q + 1) * CAP],
                                                w[:, q, h * 512:(h + 1) * 512], start=(q == 0), stop=(q == 1))
                last.then_inc(dn_pe, 1)

            c.keep_clock_up(c.bank[7], 5)
            turn(0)
            for e in range(E_N):
                up(e)
                if e + 1 < E_N:
                    turn(e + 1)
                down(e)

        @block.scalar
        def _(act):
            def out_half(e):
                act.wait_ge(dn_pe, e + 1)
                if e >= 3:
                    act.wait_ge(y_out[e % 3], base[e % 3] + 16 * (e // 3))
                nc.scalar.copy(yo[0:CAP, e % 3, 0:512], c.bank[4 + 2 * (e % 2)][0:CAP, :]).then_inc(yo_a, 1)
            for e in range(E_N):
                act.wait_ge(gate_pe, e + 1)
                if e >= 2:
                    act.wait_ge(hid_ok, e - 1)
                nc.scalar.activation(sg[e % 2], c.bank[2][:, 0:2 * CAP], ACT.Silu).then_inc(sg_ok, 1)
                out_half(e)

        @block.vector
        def _(dve):
            v, link = nc.vector, Link(dve, own)

            def turned(e):
                dve.wait_ge(xt_pe, e + 1)
                if e >= 2:
                    dve.wait_ge(up_pe, e - 1)
                for h in range(2):
                    v.tensor_tensor(xgT[:, e % 2, 4 * h:4 * h + 4, :],
                                    c.bank[h][:, 0:4 * CAP].rearrange("p (k r) -> p k r", k=4),
                                    c.gains[:, 2 + layer, 4 * h:4 * h + 4].unsqueeze(2).broadcast_to([P, 4, CAP]), ALU.mult)\
                        .then_inc(xt_ok, 1)

            def out_half(e):
                dve.wait_ge(dn_pe, e + 1)
                if e >= 3:
                    dve.wait_ge(y_out[e % 3], base[e % 3] + 16 * (e // 3))
                v.tensor_copy(yo[0:CAP, e % 3, 512:D], c.bank[5 + 2 * (e % 2)][0:CAP, :]).then_inc(yo_b, 1)
            turned(0)
            for e in range(E_N):
                dve.wait_ge(sg_ok, e + 1)
                dve.wait_ge(up_pe, e + 1)
                if e >= 2:
                    dve.wait_ge(dn_pe, e - 1)
                v.tensor_tensor(hidT[e % 2], sg[e % 2], c.bank[3][:, 0:2 * CAP], ALU.mult).then_inc(hid_ok, 1)
                if e + 1 < E_N:
                    turned(e + 1)
                out_half(e)
            for t, rows in enumerate(ROWS):
                dve.wait_ge(yp_in[t], 16)
                for q in range(2):
                    r = c.resid[0:rows, t]
                    link(v.scalar_tensor_tensor(r, m["yp"][0:rows, t, q * D:(q + 1) * D], m["ok"][0:rows, q, t:t + 1], r,
                                                ALU.mult, ALU.add))
    c.recycle()


def overflow_block(c, x, layer, m):
    nc = c.nc
    n = f"v{layer}_"
    w_in, up_pe, sg_ok, hid_ok = c.sem(n + "w"), c.sem(n + "pe_up"), c.sem(n + "silu"), c.sem(n + "hid")
    hid2, ht_pe, ht_ok, dn_pe, added = c.sem(n + "hid_gated"), c.sem(n + "pe_hT"), c.sem(n + "hT"), c.sem(n + "pe_down"), c.sem(n + "added")
    wov = m["wov"]
    gu = wov[:, 0:KC * 2 * FF].rearrange("p (k n) -> p k n", k=KC)
    dn = wov[:, KC * 2 * FF:SLOT].rearrange("p (k n) -> p k n", k=2)
    parts = c.items[IT_MOE0 if layer == 0 else IT_MOE1]

    def overflow(eng):
        return eng.value_load(m["cnt"].bitcast(I32)[0:1, :], min_val=0, max_val=TOK)

    with nc.Block() as block:
        @block.sync
        def _(sp):
            with sp.If(overflow(sp) > 0):
                with sp.Fori(0, E_N) as e:
                    sp.wait_ge(added, 3 * e + 1)
                    for view, src in zip((gu[:, :, 0:FF], gu[:, :, FF:2 * FF], dn),
                                         (x["moe_w_gate"][layer], x["moe_w_up"][layer], x["moe_w_down"][layer])):
                        k = KC if src.shape[1] == D else 2
                        sp.dma_start(view, src.rearrange("e (p k) f -> e p k f", k=k)[bass.ds(e, 1)]
                                     .rearrange("o p k f -> (o p) k f")).then_inc(w_in, 16)

        @block.tensor
        def _(pe):
            with pe.If(overflow(pe) > 0):
                with pe.Fori(0, E_N) as e:
                    pe.wait_ge(w_in, 48 * e + 48)
                    for t, rows in enumerate(ROWS):
                        pe.wait_ge(added, 3 * e + t + 1)
                        for q in range(KC):
                            last = nc.tensor.matmul(c.bank[2][0:rows, :], c.xnT[:, q, t * P:t * P + rows], gu[:, q, :],
                                                    start=(q == 0), stop=(q == KC - 1))
                        last.then_inc(up_pe, 1)
                        pe.wait_ge(hid2, 3 * e + t + 1)
                        for q in range(2):
                            last = nc.tensor.transpose(c.bank[4][:, q * P:(q + 1) * P], m["hid"][:, 0, q:FF:2], c.ident[:, :])
                        last.then_inc(ht_pe, 1)
                        pe.wait_ge(ht_ok, 3 * e + t + 1)
                        for h in range(2):
                            for q in range(2):
                                last = nc.tensor.matmul(c.bank[5 + h][0:rows, :], m["hidT"][:, 0, q, 0:rows],
                                                        dn[:, q, h * 512:(h + 1) * 512], start=(q == 0), stop=(q == 1))
                        last.then_inc(dn_pe, 1)

        @block.scalar
        def _(act):
            with act.If(overflow(act) > 0):
                with act.Fori(0, E_N) as e:
                    for t, rows in enumerate(ROWS):
                        act.wait_ge(up_pe, 3 * e + t + 1)
                        nc.scalar.activation(m["sg"][0:rows, 0], c.bank[2][0:rows, 0:FF], ACT.Silu).then_inc(sg_ok, 1)
                        act.wait_ge(ht_pe, 3 * e + t + 1)
                        nc.scalar.copy(m["hidT"][:, 0].rearrange("p k m -> p (k m)"), c.bank[4][:, 0:2 * P]).then_inc(ht_ok, 1)

        @block.vector
        def _(dve):
            with dve.If(overflow(dve) > 0):
                v = nc.vector
                v.tensor_copy(m["zero"][:, 0:1], m["gov"][:, 0, 0:1]).then_inc(added, 1)
                with dve.Fori(0, E_N) as e:
                    for t, rows in enumerate(ROWS):
                        dve.wait_ge(sg_ok, 3 * e + t + 1)
                        v.tensor_tensor(m["hid"][0:rows, 0], m["sg"][0:rows, 0], c.bank[2][0:rows, FF:2 * FF], ALU.mult)\
                            .then_inc(hid_ok, 1)
                        dve.wait_ge(hid_ok, 3 * e + t + 1)
                        v.tensor_tensor(m["hid"][0:rows, 0], m["hid"][0:rows, 0],
                                        m["gov"][0:rows, t, bass.ds(e, 1)].broadcast_to([rows, FF]), ALU.mult).then_inc(hid2, 1)
                        dve.wait_ge(dn_pe, 3 * e + t + 1)
                        for h in range(2):
                            r = c.resid[0:rows, t, h * 512:(h + 1) * 512]
                            ins = v.tensor_tensor(r, c.bank[5 + h][0:rows, :], r, ALU.add)
                        ins.then_inc(added, 1)
    c.recycle()


def out_and_moe(c, x, layer, name, parts, items):
    m = moe_arena(c)
    with c.nc.Block() as block:
        ld = c.sem(name + "_router_in")
        xn_ok, lg_pe, done = out_norm_steps(c, block, name, parts, items, 2 + layer, m["xn"], (m["wr"], ld, ROUTER_LOADS))
        route_steps(c, block, x, layer, m, ld, xn_ok, lg_pe, done, [item for item, _, _ in items])
    c.recycle()
    experts_block(c, x, layer, m, IT_MOE0 if layer == 0 else IT_MOE1)
    overflow_block(c, x, layer, m)


NKEY = 2 * 512 + P
NALL = NKEY + 3 * 32
NCHUNK = NKEY // P
CACHE_OUTS = sum(1 + min(w, SEQ) // P for w, _ in WIN)
LOADS = 6 * 16


def odd_arena(c):
    ar = Carve(c.arena, c.AR)
    t = {"kT": ar.take(6, TOK),
         "vt": ar.take(3, 768), "ocT": ar.take(4, TOK), "odT": ar.take(2, TOK),
         "qbd": ar.take(2, 3, NB, 32),
         "bs": ar.take(NALL)}
    t["after_keep"] = ar.at
    t["qT"] = ar.take(6, SEQ)
    t["bias"] = ar.take(12, 2 * P)
    t["work"] = ar.at
    t["xp"] = ar.take(4, SEQ + 3)
    t["xs"] = ar.take(4, NB, NS + 3)
    t["gT"] = ar.take(4, TOK)
    t["ktok"] = ar.take(3, 768)
    t["free"] = ar.at
    t["K"] = c.arena[:, c.AR - 2 * NCHUNK * 256:c.AR].rearrange("p (b n f) -> p b n f", b=2, f=256)
    return t


def cache_copies(c, x, eng, g, seqs, done):
    w = CACHE[g]
    out, src = x[f"o_d{g}_s"][0], x[f"cache_d_g{g}"][0]
    row = 2 * D_H * HD
    n = (w - NS) // 16 * 16
    flat = lambda ap: ap.rearrange("w t h d -> w (t h d)")
    for b in seqs:
        eng.dma_start(flat(out[b])[0:n, :].rearrange("(a r) f -> a r f", a=16),
                      flat(src[b])[NS:NS + n, :].rearrange("(a r) f -> a r f", a=16)).then_inc(done, 16)
        eng.dma_start(flat(out[b])[n:w - NS, :], flat(src[b])[NS + n:w, :]).then_inc(done, 16)
    return 32 * len(seqs)


def odd_norm_bias(c, x, od):
    st = Carve(c.arena, c.AR, od["work"])
    xn = st.take(3, D)
    flips, s1, s2, s0 = st.take(6 * P), st.take(512)[0:32], st.take(512)[0:32], st.take(P)[0:32]
    stage_n = st.take(3, NS)
    h = lambda g: (A_H + g * D_H) * BROW
    step = [BROW, 4], [1, NS]
    top = DTOP - (NS - 1)
    cached = [(od["bs"][:, 0:512], s1, [*step, [1, 512]], h(1) + top - 512),
              (od["bs"][:, 512:1024], s2, [*step, [16, 64], [1, 8]], h(2) + top - 1024),
              (od["bs"][:, 1024:NKEY], s0, [*step, [1, P]], h(0) + top - P)]
    with c.nc.Block() as block:
        turned = norm_steps(c, block, "n1", 1, xn)
        bias_steps(c, block, x, "bd", (A_H, 12), od["bias"], cached,
                   [(od["bs"][:, NKEY + 32 * g:NKEY + 32 * g + 32], A_H + g * D_H) for g in range(3)], stage_n, flips, turned)
    c.recycle()


def caches_out(x, sp, half, rows_of, out_d):
    for g in range(3):
        w_p = min(WIN[g][0], SEQ)
        cols = slice(256 * g, 256 * g + 256)
        for t in range(2):
            at = t * P - (SEQ - w_p)
            if at >= 0:
                sp.dma_start(x[f"o_d{g}_p"][0, 0, at:at + P, half].rearrange("w h d -> w (h d)"),
                             rows_of[:, t, cols]).then_inc(out_d, 16)
        sp.dma_start(x[f"o_d{g}_s"][0, :, CACHE[g] - NS:CACHE[g], half].rearrange("b s h d -> b s (h d)"),
                     rows_of[0:64, 2, cols]).then_inc(out_d, 16)


def odd_in_rglru_block(c, x, od):
    nc = c.nc
    unit, evac, k_out, zero_ok = c.sem("b2_unit"), c.sem("b2_evac"), c.sem("b2_k_out"), c.sem("b2_zero")
    units = [("x", i) for i in range(4)] + [("g", i) for i in range(4)] + [("q", i) for i in range(6)] \
        + [("k", i) for i in range(6)] + [("t", i) for i in range(6)] + [("v", i) for i in range(6)]
    item = {"x": IT_XR, "g": IT_GATE, "q": IT_Q, "k": IT_K, "v": IT_V}
    w = {kind: c.slot(it)[:, 0:KC * (512 if kind in "xg" else 768)].rearrange("p (k n) -> p k n", k=KC)
         for kind, it in item.items()}
    GATE_AFTER = 8
    first = {kind: [u[0] for u in units].index(kind) for kind in "xgqkvt"}
    ar = Carve(c.arena, c.AR, od["free"])
    xp, xs, gT = od["xp"], od["xs"], od["gT"]
    xc, r, a = ar.take(4, TOK), ar.take(4, TOK), ar.take(4, TOK)
    ig, th = ar.take(4, TOK), ar.take(4, TOK)
    ga, gx = ar.take(4, P), ar.take(4, P)
    srow = ar.take(512)[0:32]
    h0T, sp_, st = ar.take(4, NB), ar.take(6, 4), ar.take(4, 36)
    orow = ar.take(512)[0:36]
    ocT = od["ocT"]
    ld, lr_zero, own = c.sem("lr_load"), c.sem("lr_zero"), c.sem("lr_own")
    st_pe, conv_ok, gate_pe = c.sem("lr_pe_state"), c.sem("lr_conv"), c.sem("lr_pe_gate")
    sg_ok, earg, e_ok = c.sem("lr_sigmoid"), c.sem("lr_exp_arg"), c.sem("lr_exp")
    la_ok, a_ok, sq_arg, sq_ok = c.sem("lr_log_a"), c.sem("lr_a"), c.sem("lr_sqrt_arg"), c.sem("lr_sqrt")
    fin_ok, fin_pe, row_ok, out = c.sem("lr_final"), c.sem("lr_pe_final"), c.sem("lr_rows"), c.sem("lr_out")
    st_sb = c.sem("lr_state_rows")
    with nc.Block() as block:
        @block.sync
        def _(sp):
            sp.dma_start(srow[0:24], x["state_c_conv"][0].rearrange("b j c -> (b j) c")).then_inc(ld, 16)
            sp.dma_start(srow[24:32], x["state_c_h"][0]).then_inc(ld, 16)
            sp.wait_ge(lr_zero, 1)
            for w, name in ((ga, "gate_a_w"), (gx, "gate_x_w")):
                for par in range(2):
                    sp.dma_start(w[64 * par:64 * par + 64, :, 64 * par:64 * par + 64],
                                 x[name][0].rearrange("(i two) j k -> j two i k", two=2)[:, par]).then_inc(ld, 16)
            for kind, after in (("x", "g"), ("g", "q"), ("q", "k"), ("k", "t"), ("v", None)):
                if kind == "v":
                    sp.wait_ge(evac, first["v"])
                    caches_out(x, sp, 0, od["ktok"], k_out)
                    sp.wait_ge(row_ok, 1)
                    sp.dma_start(x["o_h_p"][0], orow[0:1]).then_inc(out, 16)
                    sp.dma_start(x["o_h_s"][0], orow[1:9]).then_inc(out, 16)
                    sp.dma_start(x["o_c_p"][0, 0], orow[9:12]).then_inc(out, 16)
                    sp.dma_start(x["o_c_s"][0].rearrange("b j c -> (b j) c"), orow[12:36]).then_inc(out, 16)
                sp.wait_ge(unit, first[after] if after else len(units))
                c.load_item(sp, item[kind] + RING)
            sp.wait_ge(out, 64)
            sp.wait_ge(k_out, 16 * CACHE_OUTS)

        @block.gpsimd
        def _(pool):
            nc.gpsimd.memset(od["qbd"], 0.0)
            nc.gpsimd.memset(od["xp"][:, :, 0:3], 0.0).then_inc(zero_ok, 1)
            nc.gpsimd.memset(ga, 0.0)
            nc.gpsimd.memset(gx, 0.0).then_inc(lr_zero, 1)

        @block.tensor
        def _(pe):
            def gates(i):
                pe.wait_ge(conv_ok, i + 1)
                if i == 0:
                    pe.wait_ge(st_sb, 1)
                else:
                    pe.wait_ge(sg_ok, i)
                nc.tensor.matmul(c.bank[6][:, 0:TOK], ga[:, i, :], xc[:, i, :], start=True, stop=True)
                nc.tensor.matmul(c.bank[7][:, 0:TOK], gx[:, i, :], xc[:, i, :], start=True, stop=True).then_inc(gate_pe, 1)
            for n, (kind, i) in enumerate(units):
                if n == 2:
                    pe.wait_ge(ld, 16 * 6)
                    for m in range(4):
                        last = nc.tensor.transpose(c.bank[6][:, 32 * m:32 * m + 32], srow[:, m * P:(m + 1) * P],
                                                   c.ident[0:32, 0:32])
                    last.then_inc(st_pe, 1)
                if n == len(units) - 5:
                    pe.wait_ge(fin_ok, 1)
                    for m in range(4):
                        last = nc.tensor.transpose(c.bank[6][0:36, m * P:(m + 1) * P], st[:, m, :], c.ident[:, :])
                    last.then_inc(fin_pe, 1)
                if n == first[kind] and kind in item:
                    c.arrived(pe, item[kind])
                if n >= 6:
                    pe.wait_ge(evac, n - 5)
                if kind == "t" and i == 0:
                    pe.wait_ge(evac, first["t"])
                bank = c.bank[n % 6]
                if kind == "t":
                    t, rows = i // 2, ROWS[i // 2]
                    for m, tile in enumerate((range(4), range(4, 6))[i % 2]):
                        last = nc.tensor.transpose(bank[0:rows, m * P:(m + 1) * P], od["kT"][:, tile, t * P:t * P + rows],
                                                   c.ident[:, :])
                for k in range(KC if kind != "t" else 0):
                    kw = dict(start=(k == 0), stop=(k == KC - 1))
                    if kind == "v":
                        t, c0, m = i // 2, (i % 2) * 512, (512, 256)[i % 2]
                        last = nc.tensor.matmul(bank[0:ROWS[t], 0:m], c.xnT[:, k, t * P:t * P + ROWS[t]],
                                                w[kind][:, k, c0:c0 + m], **kw)
                    else:
                        last = nc.tensor.matmul(bank[:, 0:TOK], w[kind][:, k, i * P:(i + 1) * P], c.xnT[:, k, :], **kw)
                last.then_inc(unit, 1)
                if n in range(GATE_AFTER, GATE_AFTER + 8, 2):
                    gates((n - GATE_AFTER) // 2)
            pe.wait_ge(sg_ok, 4)
            c.keep_clock_up(c.bank[7], 3)

        @block.scalar
        def _(act):
            act.wait_ge(earg, 1)
            nc.scalar.activation(sp_[:, 1], sp_[:, 1], ACT.Exp).then_inc(e_ok, 1)
            act.wait_ge(zero_ok, 1)
            for n, (kind, i) in enumerate(units):
                act.wait_ge(unit, n + 1)
                ps = c.bank[n % 6]
                if kind == "x":
                    nc.scalar.copy(od["xp"][:, i, 3:SEQ + 3], ps[:, 0:SEQ])
                    ins = nc.scalar.copy(od["xs"][:, i, :, 3:], ps[:, SEQ:TOK].rearrange("p (b s) -> p b s", b=NB))
                elif kind == "g":
                    ins = nc.scalar.activation(od["gT"][:, i, :], ps[:, 0:TOK], ACT.Gelu_apprx_tanh)
                elif kind == "q":
                    nc.scalar.copy(od["qT"][:, i, :], ps[:, 0:SEQ])
                    g, t = i // 2, i % 2
                    for par in range(2):
                        rows = slice(64 * par, 64 * par + 64)
                        ins = nc.scalar.copy(od["qbd"][rows, t, g, :, 16 * t + 8 * par:16 * t + 8 * par + 8],
                                             ps[rows, SEQ:TOK].rearrange("p (b s) -> p b s", b=NB))
                elif kind in "tv":
                    t, c0, m = i // 2, (i % 2) * 512, (512, 256)[i % 2]
                    ins = nc.scalar.copy(od["ktok" if kind == "t" else "vt"][0:ROWS[t], t, c0:c0 + m], ps[0:ROWS[t], 0:m])
                else:
                    ins = nc.scalar.copy(od["kT"][:, i, :], ps[:, 0:TOK])
                ins.then_inc(evac, 1)
                if n in range(GATE_AFTER, GATE_AFTER + 8, 2):
                    g = (n - GATE_AFTER) // 2
                    act.wait_ge(gate_pe, g + 1)
                    nc.scalar.activation(r[:, g], c.bank[6][:, 0:TOK], ACT.Sigmoid,
                                         bias=c.cols[:, COL_GA_B + g:COL_GA_B + g + 1])
                    nc.scalar.activation(ig[:, g], c.bank[7][:, 0:TOK], ACT.Sigmoid,
                                         bias=c.cols[:, COL_GX_B + g:COL_GX_B + g + 1]).then_inc(sg_ok, 1)
                if n == GATE_AFTER + 7:
                    act.wait_ge(la_ok, 1)
                    nc.scalar.activation(a, r, ACT.Exp)
                    nc.scalar.activation(th, r, ACT.Tanh).then_inc(a_ok, 1)
                if n == GATE_AFTER + 9:
                    act.wait_ge(sq_arg, 1)
                    nc.scalar.activation(th, th, ACT.Sqrt).then_inc(sq_ok, 1)

        @block.vector
        def _(dve):
            v, link = nc.vector, Link(dve, own)
            lam, ex, z, w2, p, mx = c.cols[:, COL_LAM:COL_LAM + 4], sp_[:, 1], sp_[:, 2], sp_[:, 3], sp_[:, 4], sp_[:, 5]
            link(v.tensor_scalar(sp_[:, 0], lam, -1.0, None, ALU.mult))
            v.tensor_scalar(mx, sp_[:, 0], 0.0, None, ALU.max)
            v.tensor_tensor(ex, sp_[:, 0], lam, ALU.min).then_inc(earg, 1)
            dve.wait_ge(e_ok, 1)
            link(v.tensor_scalar(z, ex, 2.0, None, ALU.add))
            link(v.reciprocal(z, z))
            link(v.tensor_tensor(z, z, ex, ALU.mult))
            link(v.tensor_tensor(w2, z, z, ALU.mult))
            link(v.tensor_scalar(p, w2, 1.0 / 17, None, ALU.mult))
            for n in range(15, 1, -2):
                link(v.scalar_tensor_tensor(p, p, 1.0 / n, w2, ALU.add, ALU.mult))
            link(v.tensor_scalar(p, p, 1.0, 2.0, ALU.add, ALU.mult))
            link(v.tensor_tensor(p, p, z, ALU.mult))
            link(v.tensor_tensor(p, p, mx, ALU.add))
            link(v.tensor_scalar(p, p, -8.0, None, ALU.mult))
            dve.wait_ge(st_pe, 1)
            ps = c.bank[6][:, 0:P].rearrange("p (i n) -> p i n", i=4)
            for i in range(4):
                v.tensor_copy(xs[:, i, :, 0:3], ps[:, i, 0:24].rearrange("p (b j) -> p b j", b=NB))
            v.tensor_copy(h0T, ps[:, :, 24:32]).then_inc(st_sb, 1)
            dve.wait_ge(st_sb, 1)
            dve.wait_ge(zero_ok, 1)
            dve.wait_ge(evac, 4)
            for i in range(4):
                cw = [c.cols[:, COL_CONV_W + 4 * t + i:COL_CONV_W + 4 * t + i + 1] for t in range(4)]
                out_p, out_s = xc[:, i, 0:SEQ], xc[:, i, SEQ:TOK].rearrange("p (b s) -> p b s", b=NB)
                v.tensor_scalar(out_p, xp[:, i, 0:SEQ], cw[0], c.cols[:, COL_CONV_B + i:COL_CONV_B + i + 1], ALU.mult, ALU.add)
                link(v.tensor_scalar(out_s, xs[:, i, :, 0:NS], cw[0], c.cols[:, COL_CONV_B + i:COL_CONV_B + i + 1], ALU.mult, ALU.add))
                for t in range(1, 4):
                    v.scalar_tensor_tensor(out_p, xp[:, i, t:t + SEQ], cw[t], out_p, ALU.mult, ALU.add)
                    ins = v.scalar_tensor_tensor(out_s, xs[:, i, :, t:t + NS], cw[t], out_s, ALU.mult, ALU.add)
                    if t < 3:
                        link(ins)
                ins.then_inc(conv_ok, 1)
            for i in range(4):
                dve.wait_ge(sg_ok, i + 1)
                ins = v.tensor_scalar(r[:, i], r[:, i], p[:, i:i + 1], None, ALU.mult)
            ins.then_inc(la_ok, 1)
            dve.wait_ge(conv_ok, 4)
            link(v.tensor_tensor(ig, ig, xc, ALU.mult))
            dve.wait_ge(a_ok, 1)
            link(v.tensor_tensor(r, a, a, ALU.mult))
            link(v.tensor_scalar(r, r, 1.0, -1.0, ALU.add, ALU.mult))
            v.tensor_tensor(th, th, r, ALU.mult).then_inc(sq_arg, 1)
            dve.wait_ge(sq_ok, 1)
            link(v.tensor_tensor(ig, ig, th, ALU.mult))
            starts = lambda ap: ap[:, :, SEQ:TOK].rearrange("p i (b s) -> p i b s", b=NB)[:, :, :, 0]
            link(v.tensor_tensor(h0T, h0T, starts(a), ALU.mult))
            link(v.tensor_tensor(starts(ig), starts(ig), h0T, ALU.add))
            v.memset(starts(a), 0.0)
            link(v.memset(a[:, :, 0:1], 0.0))
            one = lambda ap: ap.rearrange("p i t -> p (i t)")
            link(v.tensor_tensor_scan(one(r), one(a), one(ig), 0.0, ALU.mult, ALU.add))
            dve.wait_ge(evac, 8)
            v.tensor_tensor(ocT, r, gT, ALU.mult)
            v.tensor_copy(st[:, :, 0:1], r[:, :, SEQ - 1:SEQ])
            v.tensor_copy(st[:, :, 1:9], r[:, :, SEQ:TOK].rearrange("p i (b s) -> p i b s", b=NB)[:, :, :, NS - 1])
            v.tensor_copy(st[:, :, 9:12], xp[:, :, SEQ:SEQ + 3])
            for i in range(4):
                ins = v.tensor_copy(st[:, i, 12:36].rearrange("p (b j) -> p b j", b=NB), xs[:, i, :, NS:NS + 3])
            ins.then_inc(fin_ok, 1)
            dve.wait_ge(fin_pe, 1)
            v.tensor_copy(orow, c.bank[6][0:36, :]).then_inc(row_ok, 1)
    c.recycle()


def load_cache(x, eng, dst, b, half, done):
    row = 2 * D_H * HD
    eng.dma_start(dst[:, 0:4, :], x["cache_d_g1"][0, b].rearrange("(n p) t h d -> p n t (h d)", p=P)[:, :, half, :]).then_inc(done, 16)
    for n in range(4):
        eng.dma_start(dst[:, 4 + n, :], bass.AP(tensor=x["cache_d_g2"].tensor,
                                                offset=(b * CACHE[2] + 256 * n) * row + half * row // 2,
                                                ap=[[16 * row, 16], [row, 8], [1, row // 2]])).then_inc(done, 16)
    eng.dma_start(dst[:, 8, :], x["cache_d_g0"][0, b].rearrange("p t h d -> p t (h d)")[:, half, :]).then_inc(done, 16)


def attn_d_prompt_block(c, x, od):
    nc = c.nc
    qT, kT, vt, bias, odT = od["qT"], od["kT"], od["vt"], od["bias"], od["odT"]
    ar = Carve(c.arena, c.AR - 2 * NCHUNK * 256, od["work"])
    S = [ar.take(4, 3, P), ar.take(4, 3, 2 * P)]
    PT = [ar.take(4, 3, P), ar.take(4, 6, P)]
    st = [ar.take(3, 4) for _ in range(2)]
    kb = (1, 2)
    sc_pe = [c.sem(f"dp_pe_scores{t}") for t in range(2)]
    sc_ok = [c.sem(f"dp_scores{t}") for t in range(2)]
    arg, ex, p_ok = ([c.sem(f"dp_{w}{t}") for t in range(2)] for w in ("arg", "exp", "probs"))
    t_pe, t_ok, o_pe = ([c.sem(f"dp_{w}{t}") for t in range(2)] for w in ("pe_turned", "turned", "pe_out"))
    own = c.sem("dp_own")

    def score_banks(t, h):
        if t == 0:
            return [(h, 0, 3)]
        b = (4, 6, 0, 2)[h]
        return [(b, 0, 2), (b + 1, 2, 1)]

    def turn_place(t, n):
        return (4 if t == 0 else 0) + n // 4, (n % 4) * P
    with nc.Block() as block:
        @block.sync
        def _(sp):
            caches_out(x, sp, 1, vt, od["v_out"])
            for b in range(2):
                load_cache(x, sp, od["K"][:, b], b, 0, od["k_in"][b])

        @block.tensor
        def _(pe):
            def scores(t, h):
                rows = slice(64 * (h % 2), 64 * (h % 2) + 64)
                for bank, g0, n in score_banks(t, h):
                    for g in range(g0, g0 + n):
                        w = kb[t] * P
                        last = nc.tensor.matmul(c.bank[bank][:, (g - g0) * w:(g - g0 + 1) * w],
                                                qT[rows, 2 * g + h // 2, t * P:(t + 1) * P], kT[rows, 2 * g + h // 2, 0:w],
                                                start=True, stop=True)
                last.then_inc(sc_pe[t], 1)

            def turn(t):
                pe.wait_ge(p_ok[t], 1)
                n = 0
                for h in range(4):
                    for g in range(3):
                        for k in range(kb[t]):
                            bank, col = turn_place(t, n)
                            last = nc.tensor.transpose(c.bank[bank][:, col:col + P], S[t][:, h, g, k * P:(k + 1) * P],
                                                       c.ident[:, :])
                            n += 1
                            if n % 4 == 0:
                                last.then_inc(t_pe[t], 1)

            def outs(t):
                pe.wait_ge(t_ok[t], (3, 6)[t])
                for h in range(4):
                    out = c.bank[7][64 * (h % 2):64 * (h % 2) + 64, t * 256 + (h // 2) * P:t * 256 + (h // 2 + 1) * P]
                    n = 3 * kb[t]
                    for i in range(n):
                        g, k = i // kb[t], i % kb[t]
                        last = nc.tensor.matmul(out, vt[:, k, g * 256 + h * 64:g * 256 + h * 64 + 64], PT[t][:, h, i, :],
                                                start=(i == 0), stop=(i == n - 1))
                last.then_inc(o_pe[t], 1)
            for h in range(4):
                scores(0, h)
            for h in range(4):
                if h == 2:
                    pe.wait_ge(sc_ok[0], 2)
                if h == 3:
                    pe.wait_ge(sc_ok[0], 4)
                scores(1, h)
            pe.wait_ge(sc_ok[1], 4)
            turn(0)
            outs(0)
            pe.wait_ge(sc_ok[1], 8)
            pe.wait_ge(t_ok[0], 3)
            turn(1)
            outs(1)

        @block.scalar
        def _(act):
            for t in range(2):
                act.wait_ge(arg[t], 1)
                for h in range(4):
                    row = S[t][:, h].rearrange("p g k -> p (g k)")
                    ins = nc.scalar.activation(row, row, ACT.Exp, bias=st[t][:, 1, h:h + 1], accum_out=st[t][:, 2, h:h + 1])
                ins.then_inc(ex[t], 1)
            for t in range(2):
                for n in range((3, 6)[t]):
                    act.wait_ge(t_pe[t], n + 1)
                    bank, _ = turn_place(t, 4 * n)
                    nc.scalar.copy(PT[t].rearrange("p h n k -> p (h n k)")[:, 512 * n:512 * n + 512], c.bank[bank][:, :])\
                        .then_inc(t_ok[t], 1)
                act.wait_ge(o_pe[t], 1)
                nc.scalar.copy(odT[:, :, t * P:(t + 1) * P], c.bank[7][:, t * 256:t * 256 + 256].rearrange("p (i m) -> p i m", i=2))

        @block.vector
        def _(dve):
            v, link = nc.vector, Link(dve, own)
            bh = bias.rearrange("p (g h) k -> p h g k", g=3)
            for t in range(2):
                for h in range(4):
                    dve.wait_ge(sc_pe[t], h + 1)
                    for bank, g0, n in score_banks(t, h):
                        w = kb[t] * P
                        v.scalar_tensor_tensor(S[t][:, h, g0:g0 + n, :], c.bank[bank][:, 0:n * w].rearrange("p (g k) -> p g k", g=n),
                                               SCALE, bh[:, h, g0:g0 + n, 2 * P - w:2 * P], ALU.mult, ALU.add).then_inc(sc_ok[t], 1)
                dve.wait_ge(sc_ok[t], (4, 8)[t])
                link(v.tensor_reduce(st[t][:, 0], S[t].rearrange("p h g k -> p h (g k)"), AX.X, ALU.max))
                v.tensor_scalar(st[t][:, 1], st[t][:, 0], -1.0, None, ALU.mult).then_inc(arg[t], 1)
            for t in range(2):
                dve.wait_ge(ex[t], 1)
                link(v.reciprocal(st[t][:, 2], st[t][:, 2]))
                rows = S[t].rearrange("p h g k -> p h (g k)")
                v.tensor_tensor(rows, rows, st[t][:, 2].unsqueeze(2).broadcast_to([P, 4, 3 * kb[t] * P]), ALU.mult)\
                    .then_inc(p_ok[t], 1)
    c.recycle()


def attn_d_sample_block(c, x, od):
    nc = c.nc
    kT, vt, qbd, bs, odT, K = od["kT"], od["vt"], od["qbd"], od["bs"], od["odT"], od["K"]
    ar = Carve(c.arena, c.AR - 2 * NCHUNK * 256, od["after_keep"])
    V = ar.take(4, NCHUNK, 256)
    kcT = ar.take(2, NKEY)
    S, PT, PTn = ar.take(NALL), ar.take(NCHUNK, P), ar.take(2, 3, P)[0:64]
    st = ar.take(2, 3)
    rows_o = ar.take(256)
    k_in = od["k_in"]
    v_in = [c.sem(f"ds_v_in{b}") for b in range(4)]
    kt_pe, kt_a, kt_v, sc_pe, sc_ok = (c.sem("ds_pe_kT"), c.sem("ds_kT_act"), c.sem("ds_kT_dve"), c.sem("ds_pe_scores"),
                                       c.sem("ds_scores"))
    arg, ex, t_pe, t_ok, t_new = (c.sem("ds_" + w) for w in ("arg", "exp", "pe_turned", "turned", "turned_new"))
    o_pe, o_ok, own, z_ok = c.sem("ds_pe_out"), c.sem("ds_out"), c.sem("ds_own"), c.sem("ds_zero")
    row_ok, ot_pe = c.sem("ds_out_rows"), c.sem("ds_pe_out_turned")
    banks5 = [(t, q) for t in range(2) for q in range(2)]
    with nc.Block() as block:
        @block.sync
        def _(sp):
            def keys(b):
                sp.wait_ge(kt_pe, 5 * (b - 1))
                load_cache(x, sp, K[:, b % 2], b, 0, k_in[b % 2])
            for b in range(4):
                load_cache(x, sp, V[:, b], b, 1, v_in[b])
                keys(b + 2)
            for b in range(6, NB):
                keys(b)
            sp.wait_ge(o_pe, 1)
            for b in range(4):
                load_cache(x, sp, V[:, b], 4 + b, 1, v_in[b])
            sp.wait_ge(od["v_out"], 16 * CACHE_OUTS)

        @block.tensor
        def _(pe):
            def turn_keys(b):
                pe.wait_ge(k_in[b % 2], LOADS * (b // 2 + 1))
                if b >= 1:
                    pe.wait_ge(kt_a, 3 * b)
                    pe.wait_ge(kt_v, 2 * b)
                for n, (t, q) in enumerate(banks5):
                    for j in range(4):
                        last = nc.tensor.transpose(c.bank[n][:, j * P:(j + 1) * P], K[:, b % 2, 4 * q + j, t * P:(t + 1) * P],
                                                   c.ident[:, :])
                    last.then_inc(kt_pe, 1)
                for t in range(2):
                    last = nc.tensor.transpose(c.bank[4][:, t * P:(t + 1) * P], K[:, b % 2, 8, t * P:(t + 1) * P], c.ident[:, :])
                last.then_inc(kt_pe, 1)

            def scores(b):
                pe.wait_ge(kt_a, 3 * b + 3)
                pe.wait_ge(kt_v, 2 * b + 2)
                if b == 4:
                    pe.wait_ge(sc_ok, 3)
                    pe.wait_ge(o_ok, 1)
                rows = slice(32 * (b % 4), 32 * (b % 4) + 32)
                for bank, at, g, rhs in [(5, 0, 1, lambda t: kcT[:, t, 0:512]), (6, 0, 2, lambda t: kcT[:, t, 512:1024]),
                                         (7, 0, 0, lambda t: kcT[:, t, 1024:NKEY])] + \
                        [(7, P + 32 * g, g, lambda t, g=g: kT[:, 2 * g + t, SEQ + 32 * (b // 4):SEQ + 32 * (b // 4) + 32])
                         for g in range(3)]:
                    for t in range(2):
                        src = rhs(t)
                        last = nc.tensor.matmul(c.bank[bank][rows, at:at + src.shape[1]], qbd[:, t, g, b, :], src,
                                                start=(t == 0), stop=(t == 1))
                last.then_inc(sc_pe, 1)

            def values(half):
                pe.wait_ge(ex, half + 1)
                pe.wait_ge(kt_a, (15, 24)[half])
                pe.wait_ge(kt_v, (10, 16)[half])
                for n in range(NCHUNK):
                    last = nc.tensor.transpose(c.bank[n // 4][:, (n % 4) * P:(n % 4 + 1) * P], S[:, n * P:(n + 1) * P], c.ident[:, :])
                for g in range(3):
                    last = nc.tensor.transpose(c.bank[3][0:32, g * P:(g + 1) * P], S[:, NKEY + 32 * g:NKEY + 32 * g + 32],
                                               c.ident[:, :])
                last.then_inc(t_pe, 1)
                pe.wait_ge(t_ok, 3 * (half + 1))
                pe.wait_ge(t_new, half + 1)
                for g in range(3):
                    nc.tensor.matmul(c.bank[4][:, 0:256], PTn[:, half, g, :], vt[0:64, 2, g * 256:(g + 1) * 256],
                                     start=(g == 0), stop=False)
                for b in range(4):
                    pe.wait_ge(v_in[b], LOADS * (half + 1))
                    for n in range(NCHUNK):
                        last = nc.tensor.matmul(c.bank[4][32 * b:32 * b + 32, 0:256], PT[:, n, 32 * b:32 * b + 32], V[:, b, n, :],
                                                start=False, stop=(n == NCHUNK - 1))
                last.then_inc(o_pe, 1)
                pe.wait_ge(row_ok, half + 1)
                for t in range(2):
                    last = nc.tensor.transpose(c.bank[5][:, t * P:(t + 1) * P], rows_o[:, t * P:(t + 1) * P], c.ident[:, :])
                last.then_inc(ot_pe, 1)
            turn_keys(0)
            for half in range(2):
                for b in range(4 * half, 4 * half + 4):
                    if b % 4 < 3:
                        turn_keys(b + 1)
                    scores(b)
                if half == 0:
                    turn_keys(4)
                values(half)

        @block.scalar
        def _(act):
            def keys(b):
                for n in (0, 1, 4):
                    act.wait_ge(kt_pe, 5 * b + n + 1)
                    if b >= 1:
                        act.wait_ge(sc_pe, b)
                    dst = kcT[:, :, 1024:NKEY] if n == 4 else kcT[:, 0, n * 512:(n + 1) * 512]
                    src = c.bank[4][:, 0:2 * P].rearrange("p (t k) -> p t k", t=2) if n == 4 else c.bank[n][:, :]
                    nc.scalar.copy(dst, src).then_inc(kt_a, 1)
            for half in range(2):
                for b in (range(5), range(5, NB))[half]:
                    keys(b)
                act.wait_ge(arg, half + 1)
                nc.scalar.activation(S, S, ACT.Exp, bias=st[:, half, 1:2], accum_out=st[:, half, 2:3]).then_inc(ex, 1)
                act.wait_ge(t_pe, half + 1)
                if half:
                    act.wait_ge(o_pe, half)
                for n, m in enumerate((4, 4, 1)):
                    nc.scalar.copy(PT[:, 4 * n:4 * n + m, :].rearrange("p n k -> p (n k)"), c.bank[n][:, 0:m * P]).then_inc(t_ok, 1)

        @block.vector
        def _(dve):
            v, link = nc.vector, Link(dve, own)
            v.memset(PTn, 0.0).then_inc(z_ok, 1)

            def keys(b):
                for n in (2, 3):
                    dve.wait_ge(kt_pe, 5 * b + n + 1)
                    if b >= 1:
                        dve.wait_ge(sc_pe, b)
                    v.tensor_copy(kcT[:, 1, (n - 2) * 512:(n - 1) * 512], c.bank[n][:, :]).then_inc(kt_v, 1)
            for half in range(2):
                for b in (range(4), range(5, NB))[half]:
                    keys(b)
                dve.wait_ge(sc_pe, 4 * (half + 1))
                if half:
                    dve.wait_ge(t_pe, half)
                for bank, a, b_ in ((5, 0, 512), (6, 512, 1024), (7, 1024, NALL)):
                    v.scalar_tensor_tensor(S[:, a:b_], c.bank[bank][:, 0:b_ - a], SCALE, bs[:, a:b_], ALU.mult, ALU.add)\
                        .then_inc(sc_ok, 1)
                dve.wait_ge(sc_ok, 3 * (half + 1))
                link(v.tensor_reduce(st[:, half, 0:1], S, AX.X, ALU.max))
                v.tensor_scalar(st[:, half, 1:2], st[:, half, 0:1], -1.0, None, ALU.mult).then_inc(arg, 1)
                if half == 0:
                    keys(4)
                dve.wait_ge(ex, half + 1)
                link(v.reciprocal(st[:, half, 2:3], st[:, half, 2:3]))
                dve.wait_ge(t_pe, half + 1)
                dve.wait_ge(z_ok, 1)
                v.tensor_copy(PTn[32 * half:32 * half + 32, half].rearrange("p g k -> p (g k)"), c.bank[3][0:32, 0:3 * P])\
                    .then_inc(t_new, 1)
                dve.wait_ge(o_pe, half + 1)
                v.tensor_scalar(rows_o, c.bank[4][:, 0:256], st[:, half, 2:3], None, ALU.mult).then_inc(row_ok, 1)
                dve.wait_ge(ot_pe, half + 1)
                ps = c.bank[5][:, 0:256].rearrange("p (t b m) -> p t b m", t=2, b=4)
                for par in range(2):
                    rows = slice(64 * par, 64 * par + 64)
                    for t in range(2):
                        ins = v.tensor_copy(odT[rows, t, SEQ + 32 * half:SEQ + 32 * half + 32].rearrange("p (b s) -> p b s", b=4),
                                            ps[rows, t, :, 16 * t + 8 * par:16 * t + 8 * par + 8])
                ins.then_inc(o_ok, 1)
    c.recycle()


def final_block(c, x, copies, n_copies):
    nc = c.nc
    g = c.arena[:, 0:D]
    y = c.arena[:, D:4 * D].rearrange("p (t d) -> p t d", t=3)
    ld, sq_ok, ms_ok, rs_ok = c.sem("f_gain"), c.sem("f_sq"), c.sem("f_ms"), c.sem("f_rstd")
    y_ok, out, own = c.sem("f_y"), c.sem("f_out"), c.sem("f_own")
    with nc.Block() as block:
        @block.sync
        def _(sp):
            sp.dma_start(g, bass.AP(tensor=x["norm_final"].tensor, offset=0, ap=[[0, P], [1, D]])).then_inc(ld, 16)
            for t, dst in enumerate((x["y_p"][0, 0:P], x["y_p"][0, P:SEQ], x["y_s"].rearrange("b s d -> (b s) d"))):
                sp.wait_ge(y_ok, t + 1)
                sp.dma_start(dst, y[0:ROWS[t], t]).then_inc(out, 16)
            sp.wait_ge(out, 48)
            sp.wait_ge(copies, n_copies)

        @block.scalar
        def _(act):
            for t, rows in enumerate(ROWS):
                nc.scalar.activation(y[0:rows, t], c.resid[0:rows, t], ACT.Square, accum_out=c.stat[0:rows, t:t + 1]).then_inc(sq_ok, 1)
            act.wait_ge(ms_ok, 1)
            nc.scalar.activation(c.stat[:, 6:9], c.stat[:, 3:6], ACT.Sqrt).then_inc(rs_ok, 1)

        @block.vector
        def _(dve):
            v, link = nc.vector, Link(dve, own)
            dve.wait_ge(sq_ok, 3)
            link(v.tensor_scalar(c.stat[:, 3:6], c.stat[:, 0:3], 1.0 / D, EPS, ALU.mult, ALU.add))
            v.reciprocal(c.stat[:, 3:6], c.stat[:, 3:6]).then_inc(ms_ok, 1)
            dve.wait_ge(rs_ok, 1)
            dve.wait_ge(ld, 16)
            for t, rows in enumerate(ROWS):
                v.scalar_tensor_tensor(y[0:rows, t], c.resid[0:rows, t], c.stat[0:rows, 6 + t:7 + t], g[0:rows], ALU.mult,
                                       ALU.mult).then_inc(y_ok, 1)


def even_norm_bias(c, x, ev):
    xn = c.arena[:, ev["u40_at"]:ev["u40_at"] + 3 * D].rearrange("p (t d) -> p t d", t=3)
    st = Carve(c.arena, ev["after_s5"], ev["oaT_at"])
    flips, stage = st.take(6 * P), st.take(2, P)[0:32]
    stage_n = st.take(2, NS)
    cached = [(ev["bs"][:, kv, 0:P], stage[:, kv, :], [[BROW, 4], [1, NS], [1, P]],
               4 * kv * BROW + DTOP - P - (NS - 1)) for kv in range(2)]
    with c.nc.Block() as block:
        turned = norm_steps(c, block, "n0", 0, xn)
        bias_steps(c, block, x, "ba", (0, A_H), ev["bias"], cached,
                   [(ev["bs"][:, kv, P:P + 32], 4 * kv) for kv in range(2)], stage_n, flips, turned)

        @block.sync
        def _(sp):
            wuu = ev["wuu"].rearrange("p (j two) m -> p j two m", two=2)
            for s in range(CH):
                for par in range(2):
                    sp.dma_start(wuu[s * GC:(s + 1) * GC, :, par, s * GC:P],
                                 ev["tau"][par * GC:(par + 1) * GC, :, 0:P - s * GC]).then_inc(ev["wuu_in"], 16)
    c.recycle()


def program(nc, x):
    with ExitStack() as ctx:
        c = Core(nc, ctx)
        c.set_items(ring_items(x["w_in_even"][0], x["s5_glu_w"][0], x["w_out_even"][0], x["moe_w_gate"], x["moe_w_up"],
                               x["moe_w_down"], x["w_in_odd"][0], x["w_out_odd"][0]))
        x["bias_rows"] = nc.dram_tensor("bias_rows", (20, BROW), F32, kind="Internal").ap()
        x["x_rows"] = nc.dram_tensor("x_rows", (TOK, D), F32, kind="Internal").ap()
        x["y_rows"] = nc.dram_tensor("y_rows", (PAIR_ROWS, D), F32, kind="Internal").ap()
        copies = c.keep_sem("cache_copies")
        ev = even_arena(c)
        ev["wuu_in"] = c.keep_sem("ev_wuu_in")
        constants_block(c, x, ev)
        ev["pre"] = c.keep_sem("ev_prefetched")
        even_norm_bias(c, x, ev)
        even_in_s5_block(c, x, ev, copies)
        attn_a_block(c, x, ev)
        out_and_moe(c, x, 0, "oe", [ev["oaT"][:, i] for i in range(4)] + [ev["obT"][:, i] for i in range(4)],
                    [(IT_OUT_E, 0, 4), (IT_OUT_E + 1, 4, 4)])
        od = odd_arena(c)
        od["k_in"] = [c.keep_sem(f"od_k_in{b}") for b in range(2)]
        od["v_out"] = c.keep_sem("od_v_out")
        odd_norm_bias(c, x, od)
        odd_in_rglru_block(c, x, od)
        attn_d_prompt_block(c, x, od)
        attn_d_sample_block(c, x, od)
        out_and_moe(c, x, 1, "oo", [od["ocT"][:, i] for i in range(4)] + [od["odT"][:, i] for i in range(2)],
                    [(IT_OUT_O, 0, 6)])
        final_block(c, x, copies, 32 * 3 * NB)


_OUTS = [("y_p", (1, 256, 1024)), ("y_s", (8, 8, 1024)), ("o_a_p", (1, 1, 128, 2, 2, 64)), ("o_a_s", (1, 8, 128, 2, 2, 64)),
         ("o_b_p", (1, 1, 32, 64, 2)), ("o_b_s", (1, 8, 32, 64, 2)), ("o_h_p", (1, 1, 512)), ("o_h_s", (1, 8, 512)),
         ("o_c_p", (1, 1, 3, 512)), ("o_c_s", (1, 8, 3, 512)),
         ("o_d0_p", (1, 1, 128, 2, 4, 64)), ("o_d0_s", (1, 8, 128, 2, 4, 64)),
         ("o_d1_p", (1, 1, 256, 2, 4, 64)), ("o_d1_s", (1, 8, 512, 2, 4, 64)),
         ("o_d2_p", (1, 1, 256, 2, 4, 64)), ("o_d2_s", (1, 8, 1024, 2, 4, 64))]


def kernel(**inputs):
    import concourse.bacc as bacc
    from concourse.bass_utils import run_bass_kernel_spmd as run
    nc = bacc.Bacc("TRN2", target_bir_lowering=False, num_devices=1)
    arrays = {name: np.ascontiguousarray(a) for name, a in inputs.items()}
    arrays["onehot"] = bucket_onehots()
    arrays["flips"] = flip_matrices()
    arrays["route_consts"] = route_consts()
    x = {name: nc.dram_tensor("in_" + name, a.shape, F32, kind="ExternalInput").ap() for name, a in arrays.items()}
    for name, shape in _OUTS:
        x[name] = nc.dram_tensor("out_" + name, shape, F32, kind="ExternalOutput").ap()
    program(nc, x)
    r = run(nc, [{"in_" + name: a for name, a in arrays.items()}], core_ids=[0])
    return tuple(r.results[0]["out_" + name] for name, _ in _OUTS)
```
